# Optimizing a Trainium2 kernel written in Bass

```python
import jax
import jax.numpy as jnp
from jax import lax
import numpy as np

D_MODEL = 1024
BATCH = 1
SEQ = 1024
DEPTH = 2

CHUNK = 64
N_MIXERS = 4
L_RWKV = (DEPTH + N_MIXERS - 1) // N_MIXERS
L_HGRN = (DEPTH - 1 + N_MIXERS - 1) // N_MIXERS
L_SWA = (DEPTH - 2 + N_MIXERS - 1) // N_MIXERS
L_DSA = (DEPTH - 3 + N_MIXERS - 1) // N_MIXERS
RMS_EPS = 1e-6

RW_HEAD = 64
RW_HEADS = D_MODEL // RW_HEAD
RW_DECAY_LORA = 64
RW_A_LORA = 64
RW_GATE_LORA = 128
RW_GN_EPS = 64e-5

HG_HEADS = 8
HG_DK = 64
HG_DV = D_MODEL // HG_HEADS
HG_FD = HG_HEADS * HG_DK

ATT_HEAD = 64
ROT_DIM = ATT_HEAD // 4
ROPE_THETA = 500000.0

SW_HEADS = 16
SW_KV = 4
SW_GROUP = SW_HEADS // SW_KV
SW_WINDOW = 128
SW_CHUNKS = SW_WINDOW // CHUNK

DS_HEADS = 16
DS_Q_RANK = 256
DS_IDX_HEADS = 8
DS_IDX_DIM = 64
DS_TOPK = 256
DS_QBLK = 128

MOE_GROUPS = 4
MOE_PER_GROUP = 8
MOE_EXPERTS = MOE_GROUPS * MOE_PER_GROUP
MOE_TOPK = 2
MOE_FF = 512
MOE_BLK = 128

kernel_name = 'hybrid_chunk_causal_encoder'

def rms_norm(x, g, eps=RMS_EPS):
    xf = x.astype(jnp.float32)
    y = xf * lax.rsqrt(jnp.mean(xf * xf, axis=-1, keepdims=True) + eps)
    return (y * g.astype(jnp.float32)).astype(x.dtype)

def rope_tables(positions):
    inv = ROPE_THETA ** (-jnp.arange(0, ROT_DIM, 2, dtype=jnp.float32) / ROT_DIM)
    ang = positions.astype(jnp.float32)[..., None] * inv
    return jnp.cos(ang), jnp.sin(ang)

def apply_partial_rope(x, cos, sin):
    half = ROT_DIM // 2
    xr = x[..., :ROT_DIM].astype(jnp.float32)
    x1, x2 = xr[..., :half], xr[..., half:]
    c, s = cos[:, :, None, :], sin[:, :, None, :]
    rot = jnp.concatenate([x1 * c - x2 * s, x2 * c + x1 * s], axis=-1)
    return jnp.concatenate([rot.astype(x.dtype), x[..., ROT_DIM:]], axis=-1)

def rwkv7_mixer(h, mu, w_in, w0, w1, w2, a0, a1, a2, g1, g2, k_k, k_a, r_k, ln_w, ln_b, w_out):
    B, T, D = h.shape
    f32 = jnp.float32
    prev = jnp.pad(h, ((0, 0), (1, 0), (0, 0)))[:, :T]
    xs = h[:, :, None, :] + (prev - h)[:, :, None, :] * mu
    rkv = jnp.einsum('btjd,jde->btje', xs[:, :, :3], w_in)
    r, k, v = rkv[:, :, 0], rkv[:, :, 1], rkv[:, :, 2]
    x_w, x_a, x_g = xs[:, :, 3], xs[:, :, 4], xs[:, :, 5]
    w_log = -jax.nn.softplus(-(w0 + jnp.tanh(x_w @ w1) @ w2).astype(f32)) - 0.5
    decay = jnp.exp(-jnp.exp(w_log))
    a = jax.nn.sigmoid((a0 + (x_a @ a1) @ a2).astype(f32))
    gate = jax.nn.sigmoid(x_g @ g1) @ g2
    heads = lambda z: z.astype(f32).reshape(B, T, RW_HEADS, RW_HEAD)
    kk = heads(k * k_k)
    kk = kk / jnp.maximum(jnp.linalg.norm(kk, axis=-1, keepdims=True), 1e-12)
    k = k.astype(f32) * (1.0 + (a - 1.0) * k_a)
    r_h, k_h, v_h, w_h, a_h = heads(r), heads(k), heads(v), heads(decay), heads(a)

    def step(S, inp):
        r_t, w_t, k_t, v_t, kk_t, a_t = inp
        sa = jnp.einsum('bhvk,bhk->bhv', S, -kk_t)
        S = (S * w_t[:, :, None, :] + sa[..., None] * (kk_t * a_t)[:, :, None, :]
             + v_t[..., None] * k_t[:, :, None, :])
        return S, jnp.einsum('bhvk,bhk->bhv', S, r_t)

    tm = lambda z: z.swapaxes(0, 1)
    S0 = jnp.zeros((B, RW_HEADS, RW_HEAD, RW_HEAD), f32)
    _, y = lax.scan(step, S0, (tm(r_h), tm(w_h), tm(k_h), tm(v_h), tm(kk), tm(a_h)))
    y = tm(y)
    mean = jnp.mean(y, axis=-1, keepdims=True)
    var = jnp.mean(jnp.square(y - mean), axis=-1, keepdims=True)
    y = ((y - mean) * lax.rsqrt(var + RW_GN_EPS) * ln_w.reshape(RW_HEADS, RW_HEAD)
         + ln_b.reshape(RW_HEADS, RW_HEAD))
    y = y + jnp.sum(r_h * k_h * r_k, axis=-1, keepdims=True) * v_h
    y = y.reshape(B, T, D) * gate
    return y.astype(h.dtype) @ w_out

def hgrn2_lower_bound(lower, layer):
    cs = jnp.cumsum(jax.nn.softmax(lower.astype(jnp.float32), axis=0), axis=0)
    return cs[layer] - cs[0]

def hgrn2_mixer(h, lb, w_in, norm_g, w_out):
    B, T, D = h.shape
    f32 = jnp.float32
    nC = T // CHUNK
    proj = h @ w_in
    q, f_raw, i, g = jnp.split(proj, [HG_FD, 2 * HG_FD, 2 * HG_FD + D], axis=-1)
    q = jax.nn.silu(q.astype(f32)).reshape(B, T, HG_HEADS, HG_DK)
    f_raw = f_raw.astype(f32).reshape(B, T, HG_HEADS, HG_DK)
    lb = lb.reshape(HG_HEADS, HG_DK)
    log_f = jnp.logaddexp(jnp.log(lb), jnp.log1p(-lb) + jax.nn.log_sigmoid(f_raw))
    k = (1.0 - lb) * jax.nn.sigmoid(-f_raw)
    v = i.astype(f32).reshape(B, T, HG_HEADS, HG_DV)
    chunks = lambda z: z.reshape(B, nC, CHUNK, HG_HEADS, -1).transpose(1, 0, 3, 2, 4)
    causal = jnp.tril(jnp.ones((CHUNK, CHUNK), dtype=bool))

    def step(S, inp):
        qc, kc, vc, gc = inp
        b = jnp.cumsum(gc, axis=2)
        o = jnp.einsum('bhtd,bhde->bhte', qc * jnp.exp(b), S)
        rel = jnp.exp(jnp.where(causal[:, :, None], b[:, :, :, None, :] - b[:, :, None, :, :], -jnp.inf))
        att = jnp.einsum('bhtd,bhsd,bhtsd->bhts', qc, kc, rel)
        o = o + jnp.einsum('bhts,bhse->bhte', att, vc)
        b_end = b[:, :, -1:, :]
        S = (S * jnp.exp(b_end[:, :, 0, :, None])
             + jnp.einsum('bhsd,bhse->bhde', kc * jnp.exp(b_end - b), vc))
        return S, o

    S0 = jnp.zeros((B, HG_HEADS, HG_DK, HG_DV), f32)
    _, o = lax.scan(step, S0, (chunks(q), chunks(k), chunks(v), chunks(log_f)))
    o = o.transpose(1, 0, 3, 2, 4).reshape(B, T, HG_HEADS, HG_DV)
    o = rms_norm(o, norm_g).reshape(B, T, D) * jax.nn.silu(g.astype(f32))
    return o.astype(h.dtype) @ w_out

def swa_sink_mixer(h, cos, sin, w_in, q_gain, k_gain, sinks, w_out):
    B, T, _ = h.shape
    f32 = jnp.float32
    nC = T // CHUNK
    proj = h @ w_in
    q, k, v = jnp.split(proj, [SW_HEADS * ATT_HEAD, (SW_HEADS + SW_KV) * ATT_HEAD], axis=-1)
    q = apply_partial_rope(rms_norm(q.reshape(B, T, SW_HEADS, ATT_HEAD), q_gain), cos, sin)
    k = apply_partial_rope(rms_norm(k.reshape(B, T, SW_KV, ATT_HEAD), k_gain), cos, sin)
    v = v.reshape(B, T, SW_KV, ATT_HEAD)
    qc = q.reshape(B, nC, CHUNK, SW_KV, SW_GROUP, ATT_HEAD)
    shifts = list(range(SW_CHUNKS - 1, -1, -1))

    def band(z):
        zc = z.reshape(B, nC, CHUNK, SW_KV, ATT_HEAD)
        return jnp.concatenate(
            [jnp.pad(zc, ((0, 0), (sh, 0), (0, 0), (0, 0), (0, 0)))[:, :nC] for sh in shifts], axis=2)

    kb, vb = band(k), band(v)
    chunk_id = jnp.arange(nC)
    valid = jnp.concatenate(
        [jnp.broadcast_to((chunk_id >= sh)[:, None], (nC, CHUNK)) for sh in shifts], axis=1)
    scores = jnp.einsum('bnqkgd,bnskd->bnkgqs', qc, kb).astype(f32) * ATT_HEAD ** -0.5
    scores = jnp.where(valid[None, :, None, None, None, :], scores, -jnp.inf)
    sink = sinks.astype(f32).reshape(1, 1, SW_KV, SW_GROUP, 1, 1)
    m = jnp.maximum(jnp.max(scores, axis=-1, keepdims=True), sink)
    p = jnp.exp(scores - m)
    p = p / (jnp.sum(p, axis=-1, keepdims=True) + jnp.exp(sink - m))
    o = jnp.einsum('bnkgqs,bnskd->bnqkgd', p.astype(vb.dtype), vb)
    return o.reshape(B, T, SW_HEADS * ATT_HEAD) @ w_out

def dsa_mixer(h, cos, sin, w_in, cq_gain, w_uq, w_qi, q_gain, k_gain, ki_gain, w_out):
    B, T, _ = h.shape
    f32 = jnp.float32
    proj = h @ w_in
    c_q, k, v, k_idx, w_idx = jnp.split(
        proj, [DS_Q_RANK, DS_Q_RANK + ATT_HEAD, DS_Q_RANK + 2 * ATT_HEAD,
               DS_Q_RANK + 2 * ATT_HEAD + DS_IDX_DIM], axis=-1)
    c_q = rms_norm(c_q, cq_gain)
    q = apply_partial_rope(rms_norm((c_q @ w_uq).reshape(B, T, DS_HEADS, ATT_HEAD), q_gain), cos, sin)
    k = apply_partial_rope(rms_norm(k[:, :, None, :], k_gain), cos, sin)[:, :, 0]
    q_i = apply_partial_rope((c_q @ w_qi).reshape(B, T, DS_IDX_HEADS, DS_IDX_DIM), cos, sin)
    k_i = apply_partial_rope(rms_norm(k_idx[:, :, None, :], ki_gain), cos, sin)[:, :, 0]
    w_i = w_idx.astype(f32) * DS_IDX_HEADS ** -0.5
    n_sel = min(DS_TOPK, T // 4)
    nB = T // DS_QBLK
    key_pos = jnp.arange(T)

    def block(args):
        blk, q_b, qi_b, wi_b = args
        limit = ((blk * DS_QBLK + jnp.arange(DS_QBLK)) // CHUNK + 1) * CHUNK
        adm = key_pos[None, :] < limit[:, None]
        rel = jax.nn.relu(jnp.einsum('bthd,bsd->bths', qi_b, k_i).astype(f32) * DS_IDX_DIM ** -0.5)
        score = jnp.einsum('bths,bth->bts', rel, wi_b)
        score = jnp.where(adm[None], score, -jnp.inf)
        _, sel = lax.top_k(score, n_sel)
        ok = sel < limit[None, :, None]
        k_s = jax.vmap(lambda a, ix: a[ix])(k, sel)
        v_s = jax.vmap(lambda a, ix: a[ix])(v, sel)
        logits = jnp.einsum('bthd,btkd->bhtk', q_b, k_s).astype(f32) * ATT_HEAD ** -0.5
        p = jax.nn.softmax(jnp.where(ok[:, None], logits, -jnp.inf), axis=-1)
        return jnp.einsum('bhtk,btkd->bthd', p.astype(v_s.dtype), v_s)

    to_blocks = lambda z: z.reshape(B, nB, DS_QBLK, *z.shape[2:]).swapaxes(0, 1)
    o = lax.map(block, (jnp.arange(nB), to_blocks(q), to_blocks(q_i), to_blocks(w_i)))
    return o.swapaxes(0, 1).reshape(B, T, DS_HEADS * ATT_HEAD) @ w_out

def moe_ffn(u, w_rg, b_rg, w_re, b_re, w_in, w_out):
    n, D = u.shape
    f32 = jnp.float32
    g_prob = jax.nn.softmax((u @ w_rg).astype(f32) + b_rg, axis=-1)
    p_grp, grp = lax.top_k(g_prob, 1)
    e_logit = (u @ w_re).astype(f32).reshape(n, MOE_GROUPS, MOE_PER_GROUP) + b_re
    e_logit = jnp.take_along_axis(e_logit, grp[:, :, None], axis=1)[:, 0]
    top_logit, top_idx = lax.top_k(e_logit, MOE_TOPK)
    gate = p_grp * jax.nn.softmax(top_logit, axis=-1)
    expert = grp * MOE_PER_GROUP + top_idx
    A = n * MOE_TOPK
    e_flat = expert.reshape(-1)
    tok_flat = jnp.repeat(jnp.arange(n), MOE_TOPK)
    order = jnp.argsort(e_flat)
    e_s, tok_s, g_s = e_flat[order], tok_flat[order], gate.reshape(-1)[order]
    counts = jnp.bincount(e_flat, length=MOE_EXPERTS)
    starts = jnp.cumsum(counts) - counts
    padded = (counts + MOE_BLK - 1) // MOE_BLK * MOE_BLK
    p_end = jnp.cumsum(padded)
    dest = (p_end - padded)[e_s] + jnp.arange(A) - starts[e_s]
    P = -(-A // MOE_BLK) * MOE_BLK + MOE_EXPERTS * MOE_BLK
    nblk = P // MOE_BLK
    xp = jnp.zeros((P, D), u.dtype).at[dest].set(u[tok_s])
    block_e = jnp.clip(jnp.searchsorted(p_end, jnp.arange(nblk) * MOE_BLK, side='right'), 0, MOE_EXPERTS - 1)

    def expert_block(args):
        xb, e = args
        hgu = xb @ w_in[e]
        return (jax.nn.silu(hgu[:, :MOE_FF]) * hgu[:, MOE_FF:]) @ w_out[e]

    yp = lax.map(expert_block, (xp.reshape(nblk, MOE_BLK, D), block_e)).reshape(P, D)
    return jnp.zeros_like(u).at[tok_s].add(yp[dest] * g_s[:, None].astype(u.dtype))

def setup_inputs(seed: int = 0) -> dict:
    key = jax.random.key(seed)
    ks = iter(jax.random.split(key, 64))
    f32 = jnp.float32
    D = D_MODEL

    def nrm(shape, scale):
        return jax.random.normal(next(ks), shape, f32) * scale

    def gain(shape):
        return 1.0 + nrm(shape, 0.05)

    out_s = 0.5
    x = nrm((BATCH, SEQ, D), 1.0)
    offset = jax.random.randint(next(ks), (BATCH, 1), 0, 4096, dtype=jnp.int32)
    strides = jax.random.randint(next(ks), (BATCH, SEQ), 1, 3, dtype=jnp.int32)
    positions = (offset + jnp.cumsum(strides, axis=1)).astype(jnp.int32)
    LA, LB, LC, LD = L_RWKV, L_HGRN, L_SWA, L_DSA
    return {
        'x': x,
        'positions': positions,
        'norm1_g': gain((DEPTH, D)),
        'norm2_g': gain((DEPTH, D)),
        'rw_mu': jax.random.uniform(next(ks), (LA, 6, D), f32),
        'rw_in': nrm((LA, 3, D, D), D ** -0.5),
        'rw_w0': -1.0 + nrm((LA, D), 0.5),
        'rw_w1': nrm((LA, D, RW_DECAY_LORA), D ** -0.5),
        'rw_w2': nrm((LA, RW_DECAY_LORA, D), 0.1 * RW_DECAY_LORA ** -0.5),
        'rw_a0': nrm((LA, D), 0.1),
        'rw_a1': nrm((LA, D, RW_A_LORA), D ** -0.5),
        'rw_a2': nrm((LA, RW_A_LORA, D), 0.5 * RW_A_LORA ** -0.5),
        'rw_g1': nrm((LA, D, RW_GATE_LORA), D ** -0.5),
        'rw_g2': nrm((LA, RW_GATE_LORA, D), RW_GATE_LORA ** -0.5),
        'rw_kk': 0.85 + nrm((LA, D), 0.05),
        'rw_ka': gain((LA, D)),
        'rw_rk': nrm((LA, RW_HEADS, RW_HEAD), 0.1),
        'rw_ln_w': gain((LA, D)),
        'rw_ln_b': nrm((LA, D), 0.02),
        'rw_out': nrm((LA, D, D), out_s * D ** -0.5),
        'hg_lower': nrm((DEPTH, HG_FD), 0.1),
        'hg_in': nrm((LB, D, 2 * HG_FD + 2 * D), D ** -0.5),
        'hg_norm': gain((LB, HG_DV)),
        'hg_out': nrm((LB, D, D), out_s * D ** -0.5),
        'sw_in': nrm((LC, D, (SW_HEADS + 2 * SW_KV) * ATT_HEAD), D ** -0.5),
        'sw_qn': gain((LC, ATT_HEAD)),
        'sw_kn': gain((LC, ATT_HEAD)),
        'sw_sink': nrm((LC, SW_HEADS), 0.5),
        'sw_out': nrm((LC, SW_HEADS * ATT_HEAD, D), out_s * (SW_HEADS * ATT_HEAD) ** -0.5),
        'ds_in': nrm((LD, D, DS_Q_RANK + 2 * ATT_HEAD + DS_IDX_DIM + DS_IDX_HEADS), D ** -0.5),
        'ds_cqn': gain((LD, DS_Q_RANK)),
        'ds_uq': nrm((LD, DS_Q_RANK, DS_HEADS * ATT_HEAD), DS_Q_RANK ** -0.5),
        'ds_qi': nrm((LD, DS_Q_RANK, DS_IDX_HEADS * DS_IDX_DIM), DS_Q_RANK ** -0.5),
        'ds_qn': gain((LD, ATT_HEAD)),
        'ds_kn': gain((LD, ATT_HEAD)),
        'ds_kin': gain((LD, DS_IDX_DIM)),
        'ds_out': nrm((LD, DS_HEADS * ATT_HEAD, D), out_s * (DS_HEADS * ATT_HEAD) ** -0.5),
        'moe_rg': nrm((DEPTH, D, MOE_GROUPS), D ** -0.5),
        'moe_rg_b': nrm((DEPTH, MOE_GROUPS), 0.01),
        'moe_re': nrm((DEPTH, D, MOE_GROUPS * MOE_PER_GROUP), D ** -0.5),
        'moe_re_b': nrm((DEPTH, MOE_GROUPS, MOE_PER_GROUP), 0.01),
        'moe_w_in': nrm((DEPTH, MOE_EXPERTS, D, 2 * MOE_FF), D ** -0.5),
        'moe_w_out': nrm((DEPTH, MOE_EXPERTS, MOE_FF, D), out_s * MOE_FF ** -0.5),
    }

def reference(x, positions, norm1_g, norm2_g,
              rw_mu, rw_in, rw_w0, rw_w1, rw_w2, rw_a0, rw_a1, rw_a2, rw_g1, rw_g2,
              rw_kk, rw_ka, rw_rk, rw_ln_w, rw_ln_b, rw_out,
              hg_lower, hg_in, hg_norm, hg_out,
              sw_in, sw_qn, sw_kn, sw_sink, sw_out,
              ds_in, ds_cqn, ds_uq, ds_qi, ds_qn, ds_kn, ds_kin, ds_out,
              moe_rg, moe_rg_b, moe_re, moe_re_b, moe_w_in, moe_w_out):
    B, T, D = x.shape
    cos, sin = rope_tables(positions)
    h = x
    for i in range(DEPTH):
        m, j = i % N_MIXERS, i // N_MIXERS
        u = rms_norm(h, norm1_g[i])
        if m == 0:
            mix = rwkv7_mixer(u, rw_mu[j], rw_in[j], rw_w0[j], rw_w1[j], rw_w2[j], rw_a0[j], rw_a1[j],
                              rw_a2[j], rw_g1[j], rw_g2[j], rw_kk[j], rw_ka[j], rw_rk[j],
                              rw_ln_w[j], rw_ln_b[j], rw_out[j])
        elif m == 1:
            mix = hgrn2_mixer(u, hgrn2_lower_bound(hg_lower, i), hg_in[j], hg_norm[j], hg_out[j])
        elif m == 2:
            mix = swa_sink_mixer(u, cos, sin, sw_in[j], sw_qn[j], sw_kn[j], sw_sink[j], sw_out[j])
        else:
            mix = dsa_mixer(u, cos, sin, ds_in[j], ds_cqn[j], ds_uq[j], ds_qi[j], ds_qn[j], ds_kn[j],
                            ds_kin[j], ds_out[j])
        h = h + mix
        u = rms_norm(h, norm2_g[i]).reshape(B * T, D)
        h = h + moe_ffn(u, moe_rg[i], moe_rg_b[i], moe_re[i], moe_re_b[i],
                        moe_w_in[i], moe_w_out[i]).reshape(B, T, D)
    return h


_drawn_inputs = setup_inputs


def setup_inputs(seed=0):
    import zlib

    import numpy as np

    out = dict(_drawn_inputs(seed))
    spreads = {}
    factors = {'rw_w1': 5.572,
     'rw_w2': 5.216,
     'rw_a0': 2.682,
     'rw_kk': 20.654,
     'rw_ln_w': 2.723,
     'rw_ln_b': 4.797,
     'hg_lower': 6.023,
     'hg_norm': 3.005,
     'moe_rg_b': 27.372,
     'moe_re_b': 6.676}
    for name, (base, spread) in spreads.items():
        noise = np.random.default_rng([zlib.crc32(name.encode()), seed]).standard_normal(out[name].shape)
        drawn = base * np.exp(spread * noise) if base else spread * noise
        out[name] = jnp.asarray(drawn.astype(out[name].dtype))
    for name, factor in factors.items():
        out[name] = (out[name] * factor).astype(out[name].dtype)
    return out
```

```python
from contextlib import ExitStack

import concourse.bass as bass
from concourse import mybir

F32 = mybir.dt.float32
BF16 = mybir.dt.bfloat16
I32 = mybir.dt.int32
ALU = mybir.AluOpType
ACT = mybir.ActivationFunctionType
AX_X = mybir.AxisListType.X
ds = bass.ds

P = 128
T = 1024
D = 1024
KT = D // P
TT = T // P
HALF = 512
NH = T // HALF
HEAD = 64
PAIRS = D // P
CHUNK = 64
CHUNKS = T // CHUNK
LEVELS = 5
DECAY = 0.6065306597126334
RMS_EPS = 1e-6
GN_EPS = 64e-5
HG_PAIRS = 4
HG_HEADS = 8
HG_FD = 512
MAX_EXP = 80.0
GROUPS, PER_GROUP = 4, 8
EXPERTS = GROUPS * PER_GROUP
FF = 512
SLOTS = 128
EXTRA = 15
REGIONS = EXPERTS + EXTRA
NO_TOKEN = 4096


class Progress:

    def __init__(self, sem, steps, credit=1):
        self.sem, self.steps, self.credit, self.skipped = sem, steps, credit, 0

    def open(self, engine):
        engine.sem_inc(self.sem, self.credit * len(self.steps))

    def skip(self):
        self.skipped += 1

    def count(self):
        n, self.skipped = 1 + self.skipped, 0
        return n

    def after(self, step, trip):
        return trip * len(self.steps) + (self.credit * len(self.steps) + self.steps.index(step) + 1)


def spread(ap, axis, n):
    shape = list(ap.shape)
    shape.insert(axis, n)
    return ap.unsqueeze(axis).to_broadcast(shape)


class Stage:

    def __init__(self, nc, name):
        self.nc, self.name, self.ctx = nc, name, ExitStack()

    def __enter__(self):
        self.ctx.__enter__()
        return self

    def __exit__(self, *e):
        return self.ctx.__exit__(*e)

    def sb(self, name, shape, dt=F32):
        return self.ctx.enter_context(self.nc.sbuf_tensor(f"{self.name}_{name}", shape, dt))

    def psum(self, name="psum"):
        return self.ctx.enter_context(self.nc.psum_tensor(f"{self.name}_{name}", [P, 8, HALF], F32))

    def sem(self, name):
        return self.ctx.enter_context(self.nc.semaphore(f"{self.name}_{name}"))

    def progress(self, name, steps, credit=1):
        return Progress(self.sem(name), steps, credit)

    def block(self):
        return self.ctx.enter_context(self.nc.Block())


def clear_semaphores(nc, first, last):
    E = mybir.EngineType
    nc.multi_engine_barrier([E.Pool, E.SP, E.Activation, E.DVE, E.PE], sems_to_clear=range(first, last + 1))


PARAM_ROWS = ["mu", "w0", "a0", "kk", "ka", "rk", "ln_w", "ln_b"]


def setup(nc, io, c):
    with Stage(nc, "setup") as s:
        raw_a = s.sb("raw_a", [P, P])
        raw_b = s.sb("raw_b", [P, P])
        psum = s.psum()
        zeroed, shaped, loaded, turned = (s.sem(x) for x in ("zeroed", "shaped", "loaded", "turned"))
        rows = [(io["rw_mu"].rearrange("l j (k p) -> (l j k) p", p=P), 48),
                (io["rw_w0"].rearrange("l (k p) -> (l k) p", p=P), 8),
                (io["rw_a0"].rearrange("l (k p) -> (l k) p", p=P), 8),
                (io["rw_kk"].rearrange("l (k p) -> (l k) p", p=P), 8),
                (io["rw_ka"].rearrange("l (k p) -> (l k) p", p=P), 8),
                (io["rw_rk"].rearrange("l (k a) d -> (l k) (a d)", a=2), 8),
                (io["rw_ln_w"].rearrange("l (k p) -> (l k) p", p=P), 8),
                (io["rw_ln_b"].rearrange("l (k p) -> (l k) p", p=P), 8)]
        rows_b = [(io["norm1_g"].rearrange("l (k p) -> (l k) p", p=P), 16),
                  (io["norm2_g"].rearrange("l (k p) -> (l k) p", p=P), 16),
                  (io["hg_lower"].rearrange("l (k p) -> (l k) p", p=P), 8),
                  (io["hg_norm"], 1)]
        n_b = 41
        block = s.block()

        @block.sync
        def _(sp):
            at = 0
            for src, n in rows:
                sp.dma_start(raw_a[at:at + n, :], src).then_inc(loaded, 16)
                at += n
            at = 0
            for src, n in rows_b:
                sp.dma_start(raw_b[at:at + n, :], src).then_inc(loaded, 16)
                at += n

        @block.gpsimd
        def _(g):
            g.memset(c.ident[:], 0.0).then_inc(zeroed, 1)
            g.memset(c.head_ones[:], 0.0).then_inc(zeroed, 1)
            g.memset(c.low_neg[:], -1.0).then_inc(zeroed, 1)
            g.memset(c.up_neg[:], -1.0).then_inc(zeroed, 1)
            g.memset(c.up_pos[:], 1.0).then_inc(zeroed, 1)
            g.memset(c.up_incl_bd[:], 1.0).then_inc(zeroed, 1)
            g.memset(c.before[:], 1.0).then_inc(zeroed, 1)
            g.memset(c.ones[:], 1.0).then_inc(zeroed, 1)
            g.memset(c.ones_bf[:], 1.0).then_inc(zeroed, 1)
            g.memset(c.chunk_start[:], 1.0).then_inc(zeroed, 1)
            g.wait_ge(zeroed, 10)
            g.affine_select(out=c.ident[:], in_=c.ident[:], compare_op=ALU.not_equal, fill=1.0, base=0,
                            pattern=[[-1, P]], channel_multiplier=1).then_inc(shaped, 1)
            g.affine_select(out=c.low_neg[:], in_=c.low_neg[:], compare_op=ALU.is_gt, fill=0.0, base=0,
                            pattern=[[-1, P]], channel_multiplier=1).then_inc(shaped, 1)
            for m in (c.up_neg, c.up_pos, c.before):
                g.affine_select(out=m[:], in_=m[:], compare_op=ALU.is_gt, fill=0.0, base=0,
                                pattern=[[1, P]], channel_multiplier=-1).then_inc(shaped, 1)
            g.affine_select(out=c.up_incl_bd[:], in_=c.up_incl_bd[:], compare_op=ALU.is_ge, fill=0.0, base=0,
                            pattern=[[1, P]], channel_multiplier=-1).then_inc(shaped, 1)

        @block.tensor
        def _(pe):
            pe.wait_ge(shaped, 6)
            pe.wait_ge(loaded, 16 * (len(rows) + len(rows_b)))
            pe.transpose(psum[:, 0, 0:104], raw_a[0:104, :], c.ident[0:104, 0:104]).then_inc(turned, 1)
            pe.transpose(psum[:, 1, 0:n_b], raw_b[0:n_b, :], c.ident[0:n_b, 0:n_b]).then_inc(turned, 1)

        @block.vector
        def _(v):
            v.wait_ge(shaped, 6)
            v.memset(c.low_neg[HEAD:P, 0:HEAD], 0.0)
            for m in (c.up_neg, c.up_pos, c.up_incl_bd):
                v.memset(m[0:HEAD, HEAD:P], 0.0)
            for lo in (0, HEAD):
                v.memset(c.head_ones[lo:lo + HEAD, lo:lo + HEAD], 1.0)
                v.tensor_copy(c.up_incl[lo:lo + HEAD, :], c.up_incl_bd[lo:lo + HEAD, lo:lo + HEAD])
            v.memset(c.chunk_start[:].rearrange("p (n t) -> p n t", t=CHUNK)[:, :, 0:1], 0.0)
            v.wait_ge(turned, 2)
            v.tensor_copy(c.rw_cols[:, 0:104], psum[:, 0, 0:104]).then_inc(shaped, 1)
            v.tensor_copy(c.norm_cols[:, 0:n_b], psum[:, 1, 0:n_b]).then_inc(shaped, 1)
            v.wait_ge(shaped, 8)
            v.tensor_scalar(c.one_less_ka[:], c.col("ka"), -1.0, 1.0, ALU.mult, ALU.add).then_inc(shaped, 1)
            v.tensor_sub(c.lower_diff[:], c.norm_cols[:, 36:40], c.norm_cols[:, 32:36]).then_inc(shaped, 1)

        @block.scalar
        def _(a):
            a.wait_ge(shaped, 10)
            a.activation(c.lb[:], c.lower_diff[:], ACT.Sigmoid).then_inc(zeroed, 1)
            a.activation(c.one_less_lb[:], c.lower_diff[:], ACT.Sigmoid, scale=-1.0).then_inc(zeroed, 1)


class Constants:
    def __init__(self, nc):
        def sb(name, shape, dt=F32):
            return nc.alloc_sbuf_tensor(name, shape, dt)
        self.ident = sb("ident", [P, P])
        self.head_ones = sb("head_ones", [P, P])
        self.ones = sb("ones", [P, P])
        self.ones_bf = sb("ones_bf", [P, P], BF16)
        self.before = sb("before", [P, P], BF16)
        self.low_neg = sb("low_neg", [P, P])
        self.up_neg = sb("up_neg", [P, P])
        self.up_pos = sb("up_pos", [P, P])
        self.up_incl_bd = sb("up_incl_bd", [P, P])
        self.up_incl = sb("up_incl", [P, HEAD])
        self.chunk_start = sb("chunk_start", [P, PAIRS * 2 * CHUNK])
        self.rw_cols = sb("rw_cols", [P, 104])
        self.norm_cols = sb("norm_cols", [P, 41])
        self.one_less_ka = sb("one_less_ka", [P, KT])
        self.lower_diff = sb("lower_diff", [P, HG_PAIRS])
        self.lb = sb("lb", [P, HG_PAIRS])
        self.one_less_lb = sb("one_less_lb", [P, HG_PAIRS])

    def mu(self, j):
        return self.rw_cols[:, 8 * j:8 * j + 8]

    def col(self, name):
        at = 48 + 8 * (PARAM_ROWS.index(name) - 1)
        return self.rw_cols[:, at:at + 8]

    def gain(self, which, layer):
        at = 16 * which + 8 * layer
        return self.norm_cols[:, at:at + 8]

    def hg_norm(self):
        return self.norm_cols[:, 40:41]


def norm(nc, c, name, hidden, gain, turned_out, col0, rows_out=None):
    with Stage(nc, name) as s:
        h = s.sb("h", [P, TT, D])
        scaled = s.sb("scaled", [P, 2, D])
        squares = s.sb("squares", [P, D])
        mean = s.sb("mean", [P, TT])
        rms = s.sb("rms", [P, TT])
        inv = s.sb("inv", [P, TT])
        psum = s.psum()
        loaded = [s.sem(f"loaded{i}") for i in range(2)]
        stored = [s.sem(f"stored{b}") for b in range(2)]
        stats = s.sem("stats")
        act = s.progress("act", ["scale"], credit=2)
        pe = s.progress("pe", ["turn"], credit=2)
        dve = s.progress("dve", ["gain"], credit=2)
        halves = hidden.rearrange("(a i p) d -> a p i d", a=2, p=P)
        block = s.block()

        @block.sync
        def _(sp):
            for a in range(2):
                sp.dma_start(h[:, 4 * a:4 * a + 4, :], halves[a]).then_inc(loaded[a], 16)
            if rows_out is not None:
                for b in range(2):
                    sp.sem_inc(stored[b], 16)
                with sp.Fori(0, TT // 2) as trip:
                    for b in range(2):
                        tile = trip * 2 + b
                        sp.wait_ge(act.sem, act.after("scale", tile))
                        sp.dma_start(rows_out[ds(tile * P, P), :], scaled[:, b, :]).then_inc(stored[b], 16)
                for b in range(2):
                    sp.wait_ge(stored[b], 16 + 16 * (TT // 2))

        @block.scalar
        def _(a):
            for i in range(TT):
                if i % 4 == 0:
                    a.wait_ge(loaded[i // 4], 16)
                if i:
                    a.wait_ge(stats, i)
                a.activation(squares[:], h[:, i, :], ACT.Square, accum_out=mean[:, i:i + 1]).then_inc(stats, 1)
            a.wait_ge(stats, TT + 1)
            a.activation(rms[:], rms[:], ACT.Sqrt).then_inc(stats, 1)
            a.wait_ge(stats, TT + 3)
            act.open(a)
            with a.Fori(0, TT // 2) as trip:
                for b in range(2):
                    tile = trip * 2 + b
                    a.wait_ge(pe.sem, pe.after("turn", tile - 2))
                    if rows_out is not None:
                        a.wait_ge(stored[b], 16 * trip + 16)
                    a.activation(scaled[:, b, :], h[:, tile, :], ACT.Copy,
                                 scale=inv[:, ds(tile, 1)]).then_inc(act.sem, 1)

        @block.tensor
        def _(t):
            pe.open(t)
            with t.Fori(0, TT // 2) as trip:
                for b in range(2):
                    tile = trip * 2 + b
                    t.wait_ge(act.sem, act.after("scale", tile))
                    t.wait_ge(dve.sem, dve.after("gain", tile - 2))
                    for k in range(KT):
                        mm = t.transpose(psum[:, 2 * b + k // 4, (k % 4) * P:(k % 4 + 1) * P],
                                         scaled[:, b, k * P:(k + 1) * P], c.ident[:])
                    mm.then_inc(pe.sem, 1)

        @block.vector
        def _(v):
            v.wait_ge(stats, TT)
            v.tensor_scalar(rms[:], mean[:], 1.0 / D, RMS_EPS, ALU.mult, ALU.add).then_inc(stats, 1)
            v.wait_ge(stats, TT + 2)
            v.reciprocal(inv[:], rms[:]).then_inc(stats, 1)
            dve.open(v)
            with v.Fori(0, TT // 2) as trip:
                for b in range(2):
                    tile = trip * 2 + b
                    v.wait_ge(pe.sem, pe.after("turn", tile))
                    v.tensor_tensor(turned_out[:, :, ds(tile * P + col0, P)],
                                    psum[:, 2 * b:2 * b + 2, :].rearrange("p a (k t) -> p (a k) t", t=P),
                                    spread(gain, 2, P), ALU.mult).then_inc(dve.sem, 1)


def rwkv_project(nc, io, c, u, d):
    with Stage(nc, "proj") as s:
        delta = s.sb("delta", [P, KT, T])
        mix = [s.sb(f"mix{b}", [P, KT, T]) for b in range(2)]
        rate = s.sb("rate", [P, KT, T])
        ring = [s.sb(f"ring{b}", [P, KT, 2 * P]) for b in range(2)]
        hid = s.sb("hid", [P, T])
        out = [s.sb(f"out{b}", [P, T]) for b in range(2)]
        rinv = s.sb("rinv", [P, T])
        keys = s.sb("keys", [P, T])
        down = ring[0]
        ring1 = ring[1][:].rearrange("p k e -> p (k e)")
        up = [ring1[:, 0:D], ring1[:, D:2 * D], rinv[:]]
        psum = s.psum()

        lora_in = s.sem("lora_in")
        ring_in = [s.sem(f"ring_in{b}") for b in range(2)]
        stored = [s.sem(f"stored{b}") for b in range(2)]
        kept = [s.sem(f"kept{b}") for b in range(3)]
        mixed, lora_h, lora_t = s.sem("mixed"), s.sem("lora_h"), s.sem("lora_t")
        lora_e, lora_tiles = s.sem("lora_e"), s.sem("lora_tiles")
        k_pe = s.progress("k_pe", ["k", "sum"])
        k_act = s.progress("k_act", ["unscaled", "square", "root"])
        k_dve = s.progress("k_dve", ["floor", "inverse", "kk", "kka", "factor", "k"])
        rv_pe = s.progress("rv_pe", ["tile"], credit=2)
        rv_act = s.progress("rv_act", ["copy"], credit=2)
        v_pe = s.progress("v_pe", ["turn"], credit=2)
        v_dve = s.progress("v_dve", ["copy"], credit=2)
        block = s.block()
        order = [5, 3, 4, 1, 0, 2]
        weights = [io["rw_in"][0, j].rearrange("(k p) e -> p k e", p=P) for j in (1, 0, 2)]
        n_chunks = D // (2 * P)

        @block.sync
        def _(sp):
            sp.dma_start(down[:, :, 128:256], io["rw_g1"][0].rearrange("(k p) e -> p k e", p=P)).then_inc(lora_in, 16)
            sp.dma_start(down[:, :, 0:64], io["rw_w1"][0].rearrange("(k p) e -> p k e", p=P)).then_inc(lora_in, 16)
            sp.dma_start(down[:, :, 64:128], io["rw_a1"][0].rearrange("(k p) e -> p k e", p=P)).then_inc(lora_in, 16)
            sp.dma_start(up[0][0:64, :], io["rw_w2"][0]).then_inc(lora_in, 16)
            sp.dma_start(up[1][0:64, :], io["rw_a2"][0]).then_inc(lora_in, 16)
            sp.dma_start(up[2], io["rw_g2"][0]).then_inc(lora_in, 16)
            sp.wait_ge(lora_tiles, 3 * KT)
            for m, w in enumerate(weights):
                for q in range(n_chunks):
                    n = m * n_chunks + q
                    if n >= 2:
                        if n - 2 < n_chunks:
                            sp.wait_ge(k_pe.sem, k_pe.after("k", 2 * (n - 2) + 1))
                        else:
                            sp.wait_ge(rv_pe.sem, rv_pe.after("tile", 2 * (n - 2 - n_chunks) + 1))
                    sp.dma_start(ring[n % 2][:], w[:, :, q * 2 * P:(q + 1) * 2 * P]).then_inc(ring_in[n % 2], 16)
            with sp.Fori(0, KT // 2) as trip:
                for b in range(2):
                    tile = trip * 2 + b
                    sp.wait_ge(v_dve.sem, v_dve.after("copy", tile))
                    sp.dma_start(d.v_rows.rearrange("(i p) e -> p i e", p=P)[:, :, ds(tile * P, P)],
                                 mix[0][:, b, :].rearrange("p (i e) -> p i e", e=P)).then_inc(kept[b], 16)
            for b in range(2):
                sp.wait_ge(kept[b], 16 + 16 * KT + 16 * (KT // 2))

        @block.vector
        def _(v):
            v.memset(u[:, :, 0:1], 0.0).then_inc(mixed, 1)
            v.wait_ge(mixed, 1)
            v.tensor_sub(delta[:], u[:, :, 0:T], u[:, :, 1:T + 1]).then_inc(mixed, 1)
            v.wait_ge(mixed, 2)

            def blend(n):
                j = order[n]
                if n in (2, 3, 4):
                    v.wait_ge(lora_h, n - 1)
                if n == 5:
                    v.wait_ge(k_pe.sem, k_pe.after("k", KT - 1))
                for k in range(KT):
                    v.scalar_tensor_tensor(out=mix[n % 2][:, k, :], in0=delta[:, k, :], scalar=c.mu(j)[:, k:k + 1],
                                           in1=u[:, k, 1:T + 1], op0=ALU.mult, op1=ALU.add).then_inc(mixed, 1)

            for n in range(4):
                blend(n)
            blend(4)
            k_dve.open(v)
            v_dve.open(v)
            with v.Fori(0, KT) as tile:
                kps = psum[:, 0:2, :].rearrange("p a t -> p (a t)")
                sps = psum[:, 2:4, :].rearrange("p a t -> p (a t)")
                v.wait_ge(k_pe.sem, k_pe.after("sum", tile))
                v.wait_ge(kept[1], 16 * tile + 16)
                v.tensor_scalar(keys[:], sps, 1e-24, None, ALU.max).then_inc(k_dve.sem, 1)
                v.wait_ge(k_act.sem, k_act.after("root", tile))
                v.reciprocal(rinv[:], keys[:]).then_inc(k_dve.sem, 1)
                v.wait_ge(k_dve.sem, k_dve.after("inverse", tile))
                v.wait_ge(kept[0], 16 * tile + 16)
                v.tensor_mul(out[0][:], out[0][:], rinv[:]).then_inc(k_dve.sem, 1)
                v.wait_ge(k_dve.sem, k_dve.after("kk", tile))
                v.tensor_mul(keys[:], out[0][:], rate[:, tile, :]).then_inc(k_dve.sem, 1)
                v.wait_ge(kept[2], 16 * tile + 16)
                v.tensor_scalar(out[1][:], rate[:, tile, :], c.col("ka")[:, ds(tile, 1)],
                                c.one_less_ka[:, ds(tile, 1)], ALU.mult, ALU.add).then_inc(k_dve.sem, 1)
                v.wait_ge(k_dve.sem, k_dve.after("factor", tile))
                v.tensor_mul(out[1][:], out[1][:], kps).then_inc(k_dve.sem, 1)
            blend(5)
            with v.Fori(0, KT // 2) as trip:
                for b in range(2):
                    tile = trip * 2 + b
                    v.wait_ge(v_pe.sem, v_pe.after("turn", tile))
                    v.wait_ge(kept[b], 16 * trip + 16 * KT + 16)
                    v.tensor_copy(mix[0][:, b, :], psum[:, 4 + 2 * b:6 + 2 * b, :].rearrange("p a t -> p (a t)")
                                  ).then_inc(v_dve.sem, 1)

        @block.tensor
        def _(pe):
            pe.wait_ge(lora_in, 16 * 6)

            for n, (cols, row, m) in enumerate(((slice(128, 256), 2, 128), (slice(0, 64), 0, 64), (slice(64, 128), 1, 64))):
                pe.wait_ge(mixed, 2 + KT * (n + 1))
                for half in range(NH):
                    for k in range(KT):
                        mm = pe.matmul(psum[0:m, half, :], down[:, k, cols], mix[n % 2][:, k, half * HALF:(half + 1) * HALF],
                                       start=(k == 0), stop=(k == KT - 1))
                mm.then_inc(lora_h, 1)
                pe.wait_ge(lora_t, n + 1)
                for tile in range(KT):
                    i = n * KT + tile
                    if i >= 3:
                        pe.wait_ge(lora_e, i - 2)
                    for half in range(NH):
                        mm = pe.matmul(psum[:, 2 + 2 * (i % 3) + half, :], up[row][0:m, tile * P:(tile + 1) * P],
                                       hid[0:m, half * HALF:(half + 1) * HALF], start=True, stop=True)
                    mm.then_inc(lora_tiles, 1)
            pe.wait_ge(lora_e, 3 * KT)

            def product(slot, part, src, bank):
                for half in range(NH):
                    for k in range(KT):
                        mm = pe.matmul(psum[:, bank + half, :], ring[slot][:, k, part * P:(part + 1) * P],
                                       src[:, k, half * HALF:(half + 1) * HALF], start=(k == 0), stop=(k == KT - 1))
                return mm

            k_pe.open(pe)
            pe.wait_ge(mixed, 2 + KT * 4)
            with pe.Fori(0, KT // 4) as trip:
                for n in range(4):
                    tile = trip * 4 + n
                    if n % 2 == 0:
                        pe.wait_ge(ring_in[n // 2], 16 * trip + 16)
                    pe.wait_ge(k_dve.sem, k_dve.after("k", tile - 1))
                    product(n // 2, n % 2, mix[1], 0).then_inc(k_pe.sem, 1)
                    pe.wait_ge(k_act.sem, k_act.after("square", tile))
                    for half in range(NH):
                        mm = pe.matmul(psum[:, 2 + half, :], c.head_ones[:], rinv[:, half * HALF:(half + 1) * HALF],
                                       start=True, stop=True)
                    mm.then_inc(k_pe.sem, 1)
            rv_pe.open(pe)
            v_pe.open(pe)
            pe.wait_ge(k_dve.sem, k_dve.after("k", KT - 1))
            for m in range(2):
                pe.wait_ge(mixed, 2 + KT * (5 + m))
                with pe.Fori(0, KT // 4) as trip:
                    for n in range(4):
                        tile = trip * 4 + n
                        if n % 2 == 0:
                            pe.wait_ge(ring_in[n // 2], 16 * trip + 16 * (2 * (m + 1) + 1))
                        pe.wait_ge(rv_act.sem, rv_act.after("copy", tile + m * KT - 2))
                        product(n // 2, n % 2, mix[m], 2 * (n % 2)).then_inc(rv_pe.sem, 1)
                        if m == 1:
                            pe.wait_ge(rv_act.sem, rv_act.after("copy", tile + KT))
                            pe.wait_ge(v_dve.sem, v_dve.after("copy", tile - 2))
                            for k in range(TT):
                                mm = pe.transpose(psum[:, 4 + 2 * (n % 2) + k // 4, (k % 4) * P:(k % 4 + 1) * P],
                                                  out[n % 2][:, k * P:(k + 1) * P], c.ident[:])
                            mm.then_inc(v_pe.sem, 1)

        @block.scalar
        def _(a):
            for n, (func, m) in enumerate(((ACT.Sigmoid, 128), (ACT.Tanh, 64), (ACT.Copy, 64))):
                a.wait_ge(lora_h, n + 1)
                if n:
                    a.wait_ge(lora_tiles, n * KT)
                a.activation(hid[0:m, :], psum[0:m, 0:2, :].rearrange("p a t -> p (a t)"), func).then_inc(lora_t, 1)
                for tile in range(KT):
                    i = n * KT + tile
                    pair = psum[:, 2 + 2 * (i % 3):4 + 2 * (i % 3), :].rearrange("p a t -> p (a t)")
                    a.wait_ge(lora_tiles, i + 1)
                    if n < 2 and i >= 2:
                        a.wait_ge(stored[i % 2], 16 * (i // 2))
                    if n == 0:
                        a.activation(out[i % 2][:], pair, ACT.Copy).then_inc(lora_e, 1)
                    elif n == 1:
                        a.activation(out[i % 2][:], pair, ACT.Sigmoid, bias=c.col("w0")[:, tile:tile + 1]).then_inc(lora_e, 1)
                    else:
                        a.activation(rate[:, tile, :], pair, ACT.Sigmoid, bias=c.col("a0")[:, tile:tile + 1]).then_inc(lora_e, 1)
                    if n < 2:
                        a.wait_ge(lora_e, i + 1)
                        dst = (d.cm["gate"], d.cm["decay"])[n]
                        a.dma_start(dst[tile * P:(tile + 1) * P, :], out[i % 2][:]).then_inc(stored[i % 2], 16)
            for b in range(2):
                a.wait_ge(stored[b], 16 * KT)
            k_act.open(a)
            for b in range(3):
                a.sem_inc(kept[b], 16)
            with a.Fori(0, KT) as tile:
                kps = psum[:, 0:2, :].rearrange("p a t -> p (a t)")
                a.wait_ge(k_pe.sem, k_pe.after("k", tile))
                a.wait_ge(kept[0], 16 * tile + 16)
                a.activation(out[0][:], kps, ACT.Copy, scale=c.col("kk")[:, ds(tile, 1)]).then_inc(k_act.sem, 1)
                a.wait_ge(k_act.sem, k_act.after("unscaled", tile))
                a.activation(rinv[:], out[0][:], ACT.Square).then_inc(k_act.sem, 1)
                a.wait_ge(k_dve.sem, k_dve.after("floor", tile))
                a.activation(keys[:], keys[:], ACT.Sqrt).then_inc(k_act.sem, 1)
                a.wait_ge(k_dve.sem, k_dve.after("kk", tile))
                a.dma_start(d.cm["kk"][ds(tile * P, P), :], out[0][:]).then_inc(kept[0], 16)
                a.wait_ge(k_dve.sem, k_dve.after("kka", tile))
                a.dma_start(d.cm["kka"][ds(tile * P, P), :], keys[:]).then_inc(kept[1], 16)
                a.wait_ge(k_dve.sem, k_dve.after("k", tile))
                a.dma_start(d.cm["k"][ds(tile * P, P), :], out[1][:]).then_inc(kept[2], 16)
            for b in range(3):
                a.wait_ge(kept[b], 16 + 16 * KT)
            rv_act.open(a)
            for m, dst in enumerate((d.cm["r"], d.cm["v"])):
                with a.Fori(0, KT // 2) as trip:
                    for b in range(2):
                        tile = trip * 2 + b
                        a.wait_ge(rv_pe.sem, rv_pe.after("tile", tile + m * KT))
                        a.wait_ge(stored[b], 16 * trip + 16 * KT + 16 * m * (KT // 2))
                        if m == 1:
                            a.wait_ge(v_pe.sem, v_pe.after("turn", tile - 2))
                        a.activation(out[b][:], psum[:, 2 * b:2 * b + 2, :].rearrange("p a t -> p (a t)"),
                                     ACT.Copy).then_inc(rv_act.sem, 1)
                        a.wait_ge(rv_act.sem, rv_act.after("copy", tile + m * KT))
                        a.dma_start(dst[ds(tile * P, P), :], out[b][:]).then_inc(stored[b], 16)
            for b in range(2):
                a.wait_ge(stored[b], 16 * KT + 16 * KT)


class Scratch:

    def __init__(self, nc):
        def dram(name, shape, dt=F32):
            return nc.dram_tensor(name, shape, dt, kind="Internal").ap()
        self.cm = {}
        for name in ("decay", "gate", "r", "k", "kk", "kka", "v"):
            self.cm[name] = dram(f"{name}_cm", (D, T))
        self.v_rows = dram("v_rows", (T, D))
        self.hidden = dram("hidden", (T, D))
        self.rows = dram("normed_rows", (T, D))
        self.slot_table = dram("slot_table", (REGIONS * SLOTS, 1), I32)
        self.expert_rows = dram("expert_rows", (2 * T, D))


def rwkv_scan(nc, c, d, y):
    with Stage(nc, "scan") as s:
        names = ("decay", "r", "kk", "kka", "k")
        fresh = {n: s.sb(n, [P, PAIRS, 2 * CHUNK]) for n in names}
        total = s.sb("total", [P, PAIRS, 2 * CHUNK])
        shifted = s.sb("shifted", [P, PAIRS, 2 * CHUNK])
        fall = s.sb("fall", [P, PAIRS, 2 * CHUNK])
        fall1 = s.sb("fall1", [P, PAIRS, 2 * CHUNK])
        rise = s.sb("rise", [P, PAIRS, 2 * CHUNK])
        ar = [s.sb(f"ar{b}", [P, PAIRS, 2, CHUNK]) for b in range(2)]
        a_bd = [s.sb(f"a_bd{b}", [P, PAIRS, P]) for b in range(2)]
        b_bd = [s.sb(f"b_bd{b}", [P, PAIRS, P]) for b in range(2)]
        k_bd = [s.sb(f"k_bd{b}", [P, PAIRS, P]) for b in range(2)]
        v_bd = [s.sb(f"v_bd{b}", [P, PAIRS, P]) for b in range(2)]
        x = [s.sb(f"x{b}", [P, PAIRS, P]) for b in range(2)]
        xt = [s.sb(f"xt{b}", [P, PAIRS, P]) for b in range(2)]
        pt = [s.sb(f"pt{b}", [P, PAIRS, P]) for b in range(2)]
        ak_t = s.sb("ak_t", [P, PAIRS, P])
        rb_t = s.sb("rb_t", [P, PAIRS, CHUNK])
        rk_t = s.sb("rk_t", [P, PAIRS, CHUNK])
        b_rows = s.sb("b_rows", [P, PAIRS, P])
        k_rows = s.sb("k_rows", [P, PAIRS, P])
        w_bd = s.sb("w_bd", [P, PAIRS, P])
        u_bd = s.sb("u_bd", [P, PAIRS, P])
        state = s.sb("state", [P, PAIRS, P])
        grown = s.sb("grown", [P, PAIRS, P])
        psum = s.psum()

        def banks(slot):
            return psum[:, 2 * slot:2 * slot + 2, :].rearrange("p a (m e) -> p (a m) e", e=P)

        arrived = s.sem("arrived")
        v_in = [s.sem(f"v_in{b}") for b in range(2)]
        ready, ready_parts = s.sem("ready"), s.sem("ready_parts")
        g_trip = s.progress("g_trip", ["shift"])
        a_trip = s.progress("a_trip", ["fall", "fall1", "rise"])
        v_trip = s.progress("v_trip", ["total"])
        pool = s.progress("pool", ["A", "R"], credit=2)
        prep = s.progress("prep", ["A", "B", "K"], credit=2)
        pe_steps = ["N", "B.AR", "K.AR", "B_rows", "K_rows"]
        for j in range(1, LEVELS + 1):
            pe_steps += [f"X{j}"] + ([f"XT{j}"] if j < LEVELS else []) + [f"P{j}"]
        pe_steps += ["W", "U", "Y", "S"]
        pe = s.progress("pe", pe_steps, credit=2)
        dve = s.progress("dve", ["XT0", "P0", "rb", "X0"] +
                         sum([([f"XT{j}"] if j < LEVELS else []) + [f"P{j}"] for j in range(1, LEVELS + 1)], []) +
                         ["U", "grown", "S"], credit=2)
        act = s.progress("act", ["B_rows", "K_rows"] + [f"X{j}" for j in range(1, LEVELS + 1)] + ["W", "Y"], credit=2)
        mask = s.progress("mask", ["ak", "rk"], credit=2)
        block = s.block()

        @block.sync
        def _(sp):
            sp.wait_ge(ready, 1)
            with sp.Fori(0, CHUNKS // 2) as trip:
                sp.wait_ge(g_trip.sem, g_trip.after("shift", trip - 1))
                sp.wait_ge(prep.sem, prep.after("K", trip * 2 - 1))
                sp.wait_ge(pool.sem, pool.after("R", trip * 2 - 1))
                sp.wait_ge(ready, 1)
                for n in names:
                    sp.dma_start(fresh[n][:], d.cm[n].rearrange("(m p) t -> p m t", p=P)
                                 [:, :, ds(trip * 2 * CHUNK, 2 * CHUNK)]).then_inc(arrived, 16)
                for b in range(2):
                    chunk = trip * 2 + b
                    sp.wait_ge(pe.sem, pe.after("S", chunk - 2))
                    sp.wait_ge(ready, 1)
                    for h in range(2):
                        sp.dma_start(v_bd[b][h * CHUNK:(h + 1) * CHUNK, :, h * HEAD:(h + 1) * HEAD],
                                     d.v_rows.rearrange("t (m e) -> t m e", e=P)
                                     [ds(chunk * CHUNK, CHUNK), :, h * HEAD:(h + 1) * HEAD]).then_inc(v_in[b], 16)

        @block.gpsimd
        def _(g):
            for z in (*a_bd, *b_bd, *k_bd, *v_bd, state):
                g.memset(z[:], 0.0).then_inc(ready_parts, 1)
            g.wait_ge(ready_parts, 9)
            g.sem_inc(ready, 1)
            g_trip.open(g)
            pool.open(g)
            with g.Fori(0, CHUNKS // 2) as trip:
                g.wait_ge(v_trip.sem, v_trip.after("total", trip))
                g.wait_ge(a_trip.sem, a_trip.after("fall1", trip - 1))
                g.tensor_sub(shifted[:], total[:], fresh["decay"][:]).then_inc(g_trip.sem, 1)
                for b in range(2):
                    chunk = trip * 2 + b
                    at = slice(b * CHUNK, (b + 1) * CHUNK)
                    if b == 0:
                        g.wait_ge(a_trip.sem, a_trip.after("fall1", trip))
                    g.wait_ge(pe.sem, pe.after("Y", chunk - 2))
                    g.tensor_mul(ar[b][:, :, 0, :], fresh["kk"][:, :, at], fall1[:, :, at]).then_inc(pool.sem, 1)
                    g.tensor_mul(ar[b][:, :, 1, :], fresh["r"][:, :, at], fall[:, :, at]).then_inc(pool.sem, 1)

        @block.vector
        def _(v):
            v.wait_ge(ready, 1)
            v_trip.open(v)
            prep.open(v)
            dve.open(v)
            mask.open(v)
            with v.Fori(0, CHUNKS // 2) as trip:
                v.wait_ge(arrived, 80 * trip + 80)
                v.wait_ge(g_trip.sem, g_trip.after("shift", trip - 1))
                v.wait_ge(a_trip.sem, a_trip.after("rise", trip - 1))
                v.tensor_tensor_scan(total[:].rearrange("p m t -> p (m t)"), c.chunk_start[:],
                                     fresh["decay"][:].rearrange("p m t -> p (m t)"), 0.0,
                                     ALU.mult, ALU.add).then_inc(v_trip.sem, 1)
                for b in range(2):
                    chunk = trip * 2 + b
                    at = slice(b * CHUNK, (b + 1) * CHUNK)
                    if b == 0:
                        v.wait_ge(a_trip.sem, a_trip.after("rise", trip))
                    v.wait_ge(pe.sem, pe.after("W", chunk - 2))
                    for dst, src, scale in ((a_bd, "kk", fall1), (b_bd, "kka", rise), (k_bd, "k", rise)):
                        for h in range(2):
                            rows = slice(h * HEAD, (h + 1) * HEAD)
                            mul = v.tensor_mul(dst[b][rows, :, rows], fresh[src][rows, :, at], scale[rows, :, at])
                        mul.then_inc(prep.sem, 1)

                    v.wait_ge(pe.sem, pe.after("B.AR", chunk))
                    v.tensor_tensor(xt[0][:].rearrange("p m (h t) -> p m h t", h=2),
                                    spread(banks(1)[:, :, 0:CHUNK], 2, 2),
                                    spread(c.up_neg[:].rearrange("p (h t) -> p h t", h=2), 1, PAIRS),
                                    ALU.mult).then_inc(dve.sem, 1)
                    v.wait_ge(dve.sem, dve.after("XT0", chunk))
                    v.tensor_tensor(pt[0][:], xt[0][:], spread(c.ident[:], 1, PAIRS), ALU.add).then_inc(dve.sem, 1)
                    v.tensor_tensor(rb_t[:], banks(1)[:, :, CHUNK:P], spread(c.up_incl[:], 1, PAIRS),
                                    ALU.mult).then_inc(dve.sem, 1)
                    v.tensor_tensor(x[0][:], banks(0), spread(c.low_neg[:], 1, PAIRS), ALU.mult).then_inc(dve.sem, 1)
                    v.wait_ge(pe.sem, pe.after("K.AR", chunk))
                    v.tensor_tensor(ak_t[:].rearrange("p m (h t) -> p m h t", h=2),
                                    spread(banks(3)[:, :, 0:CHUNK], 2, 2),
                                    spread(c.up_pos[:].rearrange("p (h t) -> p h t", h=2), 1, PAIRS),
                                    ALU.mult).then_inc(mask.sem, 1)
                    v.tensor_tensor(rk_t[:], banks(3)[:, :, CHUNK:P], spread(c.up_incl[:], 1, PAIRS),
                                    ALU.mult).then_inc(mask.sem, 1)

                    for j in range(1, LEVELS + 1):
                        if j < LEVELS:
                            v.wait_ge(pe.sem, pe.after(f"XT{j}", chunk))
                            v.tensor_copy(xt[j % 2][:], banks(1)).then_inc(dve.sem, 1)
                        v.wait_ge(pe.sem, pe.after(f"P{j}", chunk))
                        v.tensor_add(pt[j % 2][:], pt[(j - 1) % 2][:], banks(2)).then_inc(dve.sem, 1)

                    v.wait_ge(pe.sem, pe.after("U", chunk))
                    v.tensor_copy(u_bd[:], banks(2)).then_inc(dve.sem, 1)
                    v.wait_ge(pe.sem, pe.after("S", chunk))
                    v.tensor_add(grown[:], state[:], banks(1)).then_inc(dve.sem, 1)
                    v.wait_ge(dve.sem, dve.after("grown", chunk))
                    v.tensor_tensor(state[:], grown[:], spread(fall[:, :, (b + 1) * CHUNK - 1], 2, P),
                                    ALU.mult).then_inc(dve.sem, 1)

        @block.scalar
        def _(a):
            a_trip.open(a)
            act.open(a)
            with a.Fori(0, CHUNKS // 2) as trip:
                a.wait_ge(v_trip.sem, v_trip.after("total", trip))
                a.wait_ge(dve.sem, dve.after("S", trip * 2 - 1))
                a.wait_ge(pool.sem, pool.after("R", trip * 2 - 1))
                a.activation(fall[:], total[:], ACT.Exp, scale=-DECAY).then_inc(a_trip.sem, 1)
                a.wait_ge(g_trip.sem, g_trip.after("shift", trip))
                a.activation(fall1[:], shifted[:], ACT.Exp, scale=-DECAY).then_inc(a_trip.sem, 1)
                a.activation(rise[:], total[:], ACT.Exp, scale=DECAY).then_inc(a_trip.sem, 1)
                for b in range(2):
                    chunk = trip * 2 + b
                    a.wait_ge(pe.sem, pe.after("B_rows", chunk))
                    a.activation(b_rows[:], banks(2), ACT.Copy).then_inc(act.sem, 1)
                    a.wait_ge(pe.sem, pe.after("K_rows", chunk))
                    a.activation(k_rows[:], banks(0), ACT.Copy).then_inc(act.sem, 1)
                    for j in range(1, LEVELS + 1):
                        a.wait_ge(pe.sem, pe.after(f"X{j}", chunk))
                        a.activation(x[j % 2][:], banks(0), ACT.Copy).then_inc(act.sem, 1)
                    a.wait_ge(pe.sem, pe.after("W", chunk))
                    a.activation(w_bd[:], banks(3), ACT.Copy, scale=-1.0).then_inc(act.sem, 1)
                    a.wait_ge(pe.sem, pe.after("Y", chunk))
                    a.activation(y[:, :, ds(chunk * CHUNK, CHUNK)], psum[:, 0, :].rearrange("p (m t) -> p m t", t=CHUNK),
                                 ACT.Copy).then_inc(act.sem, 1)

        @block.tensor
        def _(t):
            def each_pair(slot, step, *products):
                for m in range(PAIRS):
                    for n, (lhs, rhs) in enumerate(products):
                        mm = t.matmul(banks(slot)[:, m, :], lhs[:, m, :], rhs(m),
                                      start=(n == 0), stop=(n == len(products) - 1))
                mm.then_inc(pe.sem, 1)

            def whole(buf):
                return lambda m: buf[:, m, :]

            pe.open(t)
            with t.Fori(0, CHUNKS // 2) as trip:
                for b in range(2):
                    chunk = trip * 2 + b
                    ar_b = ar[b][:].rearrange("p m a t -> p m (a t)")
                    t.wait_ge(prep.sem, prep.after("B", chunk))
                    t.wait_ge(act.sem, act.after("Y", chunk - 1))
                    each_pair(0, "N", (a_bd[b], whole(b_bd[b])))
                    t.wait_ge(pool.sem, pool.after("R", chunk))
                    t.wait_ge(dve.sem, dve.after("grown", chunk - 1))
                    each_pair(1, "B.AR", (b_bd[b], lambda m: ar_b[:, m, :]))
                    t.wait_ge(prep.sem, prep.after("K", chunk))
                    each_pair(3, "K.AR", (k_bd[b], lambda m: ar_b[:, m, :]))
                    for m in range(PAIRS):
                        mm = t.transpose(banks(2)[:, m, :], b_bd[b][:, m, :], c.ident[:])
                    mm.then_inc(pe.sem, 1)
                    t.wait_ge(dve.sem, dve.after("X0", chunk))
                    for m in range(PAIRS):
                        mm = t.transpose(banks(0)[:, m, :], k_bd[b][:, m, :], c.ident[:])
                    mm.then_inc(pe.sem, 1)
                    t.wait_ge(act.sem, act.after("K_rows", chunk))
                    for j in range(1, LEVELS + 1):
                        old, new = (j - 1) % 2, j % 2
                        if j > 1:
                            t.wait_ge(dve.sem, dve.after(f"XT{j - 1}", chunk))
                        each_pair(0, f"X{j}", (xt[old], whole(x[old])))
                        if j < LEVELS:
                            each_pair(1, f"XT{j}", (x[old], whole(xt[old])))
                        t.wait_ge(act.sem, act.after(f"X{j}", chunk))
                        t.wait_ge(dve.sem, dve.after(f"P{j - 1}", chunk))
                        each_pair(2, f"P{j}", (x[new], whole(pt[old])))
                    t.wait_ge(dve.sem, dve.after("S", chunk - 1))
                    t.wait_ge(mask.sem, mask.after("rk", chunk))
                    t.wait_ge(v_in[b], 32 * trip + 32)
                    each_pair(3, "W", (a_bd[b], whole(state)), (ak_t, whole(v_bd[b])))
                    t.wait_ge(act.sem, act.after("W", chunk))
                    t.wait_ge(dve.sem, dve.after(f"P{LEVELS}", chunk))
                    each_pair(2, "U", (pt[LEVELS % 2], whole(w_bd)))
                    t.wait_ge(dve.sem, dve.after("U", chunk))
                    for m in range(PAIRS):
                        for n, (lhs, rhs) in enumerate(((state, ar_b[:, m, CHUNK:P]), (v_bd[b], rk_t[:, m, :]),
                                                        (u_bd, rb_t[:, m, :]))):
                            mm = t.matmul(psum[:, 0, m * CHUNK:(m + 1) * CHUNK], lhs[:, m, :], rhs,
                                          start=(n == 0), stop=(n == 2))
                    mm.then_inc(pe.sem, 1)
                    each_pair(1, "S", (k_rows, whole(v_bd[b])), (b_rows, whole(u_bd)))


def rwkv_output(nc, io, c, d, y):
    with Stage(nc, "gn") as s:
        r, k, v_, gate = ([s.sb(f"{n}{b}", [P, T]) for b in range(2)] for n in ("r", "k", "v", "gate"))
        squares = [s.sb(f"squares{b}", [P, T]) for b in range(2)]
        inv = [s.sb(f"inv{b}", [P, T]) for b in range(2)]
        psum = s.psum()
        loaded = [s.sem(f"loaded{b}") for b in range(2)]
        opened, between = s.sem("opened"), s.sem("between")
        pe = s.progress("pe", ["sum", "bonus", "squares"], credit=2)
        dve = s.progress("dve", ["rk", "centered", "variance", "bonus", "unit"], credit=2)
        act = s.progress("act", ["square", "ln", "inverse", "affine"], credit=2)
        pool = s.progress("pool", ["add", "gate"], credit=2)
        block = s.block()

        def flat(bank):
            return psum[:, bank:bank + 2, :].rearrange("p a t -> p (a t)")

        @block.sync
        def _(sp):
            with sp.Fori(0, PAIRS // 2) as trip:
                for b in range(2):
                    tile = trip * 2 + b
                    sp.wait_ge(pool.sem, pool.after("gate", tile - 2))
                    sp.wait_ge(dve.sem, dve.after("unit", tile - 2))
                    sp.wait_ge(opened, 1)
                    for buf, src in ((r, d.cm["r"]), (k, d.cm["k"]), (v_, d.cm["v"]), (gate, d.cm["gate"])):
                        sp.dma_start(buf[b][:], src[ds(tile * P, P), :]).then_inc(loaded[b], 16)

        @block.tensor
        def _(t):
            pe.open(t)
            with t.Fori(0, PAIRS // 2) as trip:
                for b in range(2):
                    tile = trip * 2 + b

                    def head_sum(bank, src, step):
                        for half in range(NH):
                            mm = t.matmul(psum[:, bank + half, :], c.head_ones[:], src(half * HALF), start=True, stop=True)
                        mm.then_inc(pe.sem, 1)

                    t.wait_ge(dve.sem, dve.after("centered", tile - 1))
                    head_sum(0, lambda at: y[:, tile, at:at + HALF], "sum")
                    t.wait_ge(dve.sem, dve.after("rk", tile))
                    t.wait_ge(dve.sem, dve.after("bonus", tile - 1))
                    head_sum(4, lambda at: r[b][:, at:at + HALF], "bonus")
                    t.wait_ge(act.sem, act.after("square", tile))
                    t.wait_ge(dve.sem, dve.after("variance", tile - 1))
                    head_sum(2, lambda at: squares[b][:, at:at + HALF], "squares")

        @block.vector
        def _(v):
            v.sem_inc(opened, 1)
            dve.open(v)
            with v.Fori(0, PAIRS // 2) as trip:
                for b in range(2):
                    tile = trip * 2 + b
                    v.wait_ge(loaded[b], 64 * trip + 64)
                    v.scalar_tensor_tensor(out=r[b][:], in0=r[b][:], scalar=c.col("rk")[:, ds(tile, 1)], in1=k[b][:],
                                           op0=ALU.mult, op1=ALU.mult).then_inc(dve.sem, 1)
                    v.wait_ge(pe.sem, pe.after("sum", tile))
                    v.scalar_tensor_tensor(out=y[:, tile, :], in0=flat(0), scalar=-1.0 / HEAD, in1=y[:, tile, :],
                                           op0=ALU.mult, op1=ALU.add).then_inc(dve.sem, 1)
                    v.wait_ge(pe.sem, pe.after("squares", tile))
                    v.wait_ge(act.sem, act.after("inverse", tile - 2))
                    v.tensor_scalar(inv[b][:], flat(2), 1.0 / HEAD, GN_EPS, ALU.mult, ALU.add).then_inc(dve.sem, 1)
                    v.wait_ge(pe.sem, pe.after("bonus", tile))
                    v.tensor_mul(v_[b][:], v_[b][:], flat(4)).then_inc(dve.sem, 1)
                    v.wait_ge(act.sem, act.after("inverse", tile))
                    v.tensor_mul(inv[b][:], inv[b][:], y[:, tile, :]).then_inc(dve.sem, 1)

        @block.scalar
        def _(a):
            act.open(a)
            with a.Fori(0, PAIRS // 2) as trip:
                for b in range(2):
                    tile = trip * 2 + b
                    a.wait_ge(dve.sem, dve.after("centered", tile))
                    a.wait_ge(act.sem, act.after("affine", tile - 1))
                    a.wait_ge(pe.sem, pe.after("squares", tile - 2))
                    a.activation(squares[b][:], y[:, tile, :], ACT.Square).then_inc(act.sem, 1)
                    a.wait_ge(dve.sem, dve.after("variance", tile))
                    a.activation(inv[b][:], inv[b][:], ACT.Ln).then_inc(act.sem, 1)
                    a.wait_ge(act.sem, act.after("ln", tile))
                    a.activation(inv[b][:], inv[b][:], ACT.Exp, scale=-0.5).then_inc(act.sem, 1)
                    a.wait_ge(dve.sem, dve.after("unit", tile))
                    a.activation(y[:, tile, :], inv[b][:], ACT.Identity, bias=c.col("ln_b")[:, ds(tile, 1)],
                                 scale=c.col("ln_w")[:, ds(tile, 1)]).then_inc(act.sem, 1)

        @block.gpsimd
        def _(g):
            pool.open(g)
            with g.Fori(0, PAIRS // 2) as trip:
                for b in range(2):
                    tile = trip * 2 + b
                    g.wait_ge(act.sem, act.after("affine", tile))
                    g.wait_ge(opened, 1)
                    g.tensor_add(y[:, tile, :], y[:, tile, :], v_[b][:]).then_inc(pool.sem, 1)
                    g.wait_ge(pool.sem, pool.after("add", tile))
                    g.sem_inc(between, 1)
                    g.tensor_mul(y[:, tile, :], y[:, tile, :], gate[b][:]).then_inc(pool.sem, 1)


def project_out(nc, name, w_out, mixed, hidden, hidden_out):
    with Stage(nc, name) as s:
        w = s.sb("w", [P, KT, D])
        h = s.sb("h", [P, TT, D])
        psum = s.psum()
        w_in = [s.sem(f"w_in{a}") for a in range(2)]
        h_in, product, added, stored = s.sem("h_in"), s.sem("product"), s.sem("added"), s.sem("stored")
        block = s.block()

        @block.sync
        def _(sp):
            for a in range(NH):
                sp.dma_start(w[:, :, a * HALF:(a + 1) * HALF],
                             w_out.rearrange("(k p) e -> p k e", p=P)[:, :, a * HALF:(a + 1) * HALF]).then_inc(w_in[a], 16)
            sp.dma_start(h[:], hidden.rearrange("(i p) e -> p i e", p=P)).then_inc(h_in, 16)
            for i in range(TT):
                sp.wait_ge(added, i + 1)
                sp.dma_start(hidden_out[i * P:(i + 1) * P, :], h[:, i, :]).then_inc(stored, 16)
            sp.wait_ge(stored, 16 * TT)

        @block.tensor
        def _(t):
            for i in range(TT):
                if i >= 4:
                    t.wait_ge(added, i - 3)
                for a in range(NH):
                    if i == 0:
                        t.wait_ge(w_in[a], 16)
                    for k in range(KT):
                        mm = t.matmul(psum[:, 2 * (i % 4) + a, :], mixed[:, k, i * P:(i + 1) * P],
                                      w[:, k, a * HALF:(a + 1) * HALF], start=(k == 0), stop=(k == KT - 1))
                mm.then_inc(product, 1)

        @block.vector
        def _(v):
            v.wait_ge(h_in, 16)
            for i in range(TT):
                v.wait_ge(product, i + 1)
                v.tensor_add(h[:, i, :], h[:, i, :], psum[:, 2 * (i % 4):2 * (i % 4) + 2, :].rearrange("p a t -> p (a t)")
                             ).then_inc(added, 1)


def route(nc, io, c, d, r, layer, name, u):
    with Stage(nc, name) as s:
        n_out = GROUPS + EXPERTS
        w = s.sb("w", [P, KT, n_out])
        bias = s.sb("bias", [P, n_out])
        logits = s.sb("logits", [P, TT, n_out])
        lg = logits[:, :, 0:GROUPS]
        le = logits[:, :, GROUPS:n_out]
        iota = s.sb("iota", [P, EXPERTS])
        expert_base = s.sb("expert_base", [P, EXPERTS])
        limits = s.sb("limits", [P, TT - 1])
        blocks = s.sb("blocks", [1, EXTRA])
        assignment = s.sb("assignment", [P, TT, 2], I32)
        top = s.sb("top", [P, TT])
        masked = s.sb("masked", [P, TT, EXPERTS])
        group_hot = s.sb("group_hot", [P, TT, GROUPS])
        group_exp = s.sb("group_exp", [P, TT, GROUPS])
        first = s.sb("first", [P, TT, EXPERTS])
        second = s.sb("second", [P, TT, EXPERTS])
        cand = s.sb("cand", [P, TT, EXPERTS])
        least = s.sb("least", [P, TT])
        top1 = s.sb("top1", [P, TT])
        top2 = s.sb("top2", [P, TT])
        p_group = s.sb("p_group", [P, TT])
        ratio = s.sb("ratio", [P, TT])
        share = s.sb("share", [P, TT])
        chosen = s.sb("chosen", [P, TT, EXPERTS], BF16)
        count = s.sb("count", [P, EXPERTS])
        over = s.sb("over", [P, EXPERTS, TT - 1])
        extra = s.sb("extra", [P, EXPERTS])
        extra_end = s.sb("extra_end", [P, EXPERTS])
        extra_base = s.sb("extra_base", [P, EXPERTS])
        slot = s.sb("slot", [P, TT, EXPERTS])
        picked = s.sb("picked", [P, TT, 2])
        slot_of = s.sb("slot_of", [P, TT, 2], I32)
        passed = s.sb("passed", [1, EXTRA, EXPERTS])
        block_expert = s.sb("block_expert", [1, EXTRA + 1])
        empty = s.sb("empty", [REGIONS, P], I32)
        table = s.sb("table", [REGIONS, P], I32)
        table_f = s.sb("table_f", [REGIONS, P])
        psum = s.psum()
        loaded, made, product, step, soft, written, table_in = (
            s.sem(x) for x in ("loaded", "made", "product", "step", "soft", "written", "table_in"))
        emptied, step_act, chosen_ready, slots_ready, table_ready = (
            s.sem(x) for x in ("emptied", "step_act", "chosen_ready", "slots_ready", "table_ready"))
        block = s.block()

        @block.sync
        def _(sp):
            sp.dma_start(w[:, :, 0:GROUPS], io["moe_rg"][layer].rearrange("(k p) e -> p k e", p=P)).then_inc(loaded, 16)
            sp.dma_start(w[:, :, GROUPS:n_out], io["moe_re"][layer].rearrange("(k p) e -> p k e", p=P)).then_inc(loaded, 16)
            sp.dma_start(bias[:, 0:GROUPS], io["moe_rg_b"][layer:layer + 1, :].partition_broadcast(P)
                         .rearrange("p a e -> p (a e)")).then_inc(loaded, 16)
            sp.dma_start(bias[:, GROUPS:n_out], io["moe_re_b"][layer].rearrange("(a g) e -> a (g e)", a=1)
                         .partition_broadcast(P).rearrange("p a e -> p (a e)")).then_inc(loaded, 16)

        @block.gpsimd
        def _(g):
            g.memset(empty[:], NO_TOKEN).then_inc(made, 1)
            g.iota(iota[:], [[1, EXPERTS]], base=0, channel_multiplier=0,
                   allow_small_or_imprecise_dtypes=True).then_inc(made, 1)
            g.iota(expert_base[:], [[SLOTS, EXPERTS]], base=0, channel_multiplier=0,
                   allow_small_or_imprecise_dtypes=True).then_inc(made, 1)
            g.iota(limits[:], [[SLOTS, TT - 1]], base=SLOTS, channel_multiplier=0,
                   allow_small_or_imprecise_dtypes=True).then_inc(made, 1)
            g.iota(blocks[:], [[1, EXTRA]], base=0, channel_multiplier=0,
                   allow_small_or_imprecise_dtypes=True).then_inc(made, 1)
            g.iota(assignment[:], [[2 * P, TT], [1, 2]], base=0, channel_multiplier=2).then_inc(made, 1)
            g.wait_ge(made, 6)
            g.dma_start(d.slot_table.rearrange("(r p) o -> r (p o)", p=P), empty[:]).then_inc(emptied, 16)
            g.wait_ge(emptied, 16)
            g.wait_ge(slots_ready, 1)
            for i in range(TT):
                for choice in range(2):
                    g.indirect_dma_start(
                        out=d.slot_table, out_offset=bass.IndirectOffsetOnAxis(ap=slot_of[:, i, choice:choice + 1], axis=0),
                        in_=assignment[:, i, choice:choice + 1], in_offset=None).then_inc(written, 16)
            g.wait_ge(written, 16 * 2 * TT)
            g.dma_start(table[:], d.slot_table.rearrange("(r p) o -> r (p o)", p=P)).then_inc(table_in, 16)

        @block.tensor
        def _(t):
            t.wait_ge(loaded, 64)
            for i in range(TT):
                for k in range(KT):
                    mm = t.matmul(psum[:, 0, i * 64:i * 64 + n_out], u[:, k, i * P:(i + 1) * P], w[:, k, :],
                                  start=(k == 0), stop=(k == KT - 1))
            mm.then_inc(product, 1)
            t.wait_ge(chosen_ready, 1)
            for i in range(TT):
                for j in range(i):
                    t.matmul(psum[:, 1, i * EXPERTS:(i + 1) * EXPERTS], c.ones_bf[:], chosen[:, j, :],
                             start=(j == 0), stop=False)
                t.matmul(psum[:, 1, i * EXPERTS:(i + 1) * EXPERTS], c.before[:], chosen[:, i, :],
                         start=(i == 0), stop=True)
            for j in range(TT):
                mm = t.matmul(psum[:, 2, 0:EXPERTS], c.ones_bf[:], chosen[:, j, :], start=(j == 0), stop=(j == TT - 1))
            mm.then_inc(product, 1)
            t.wait_ge(table_ready, 1)
            t.transpose(psum[:, 3, 0:REGIONS], table_f[:], c.ident[0:REGIONS, 0:REGIONS]).then_inc(product, 1)

        @block.scalar
        def _(a):
            a.wait_ge(soft, 1)
            a.activation(group_exp[:], group_exp[:], ACT.Exp).then_inc(step_act, 1)
            a.wait_ge(soft, 2)
            a.activation(ratio[:], ratio[:], ACT.Exp).then_inc(step_act, 1)

        @block.vector
        def _(v):
            done = [0]

            def after(ins):
                done[0] += 1
                ins.then_inc(step, 1)
                v.wait_ge(step, done[0])

            def one_hot(out, values, best, n):
                after(v.tensor_reduce(best[:], values, AX_X, ALU.max))
                after(v.tensor_tensor(cand[:, :, 0:n], values, spread(best[:], 2, n), ALU.is_ge))
                after(v.scalar_tensor_tensor(out=cand[:, :, 0:n], in0=cand[:, :, 0:n], scalar=-64.0,
                                             in1=spread(iota[:, 0:n], 1, TT), op0=ALU.mult, op1=ALU.add))
                after(v.tensor_reduce(least[:], cand[:, :, 0:n], AX_X, ALU.min))
                after(v.tensor_tensor(out, cand[:, :, 0:n], spread(least[:], 2, n), ALU.is_equal))

            v.wait_ge(product, 1)
            v.wait_ge(made, 6)
            after(v.tensor_tensor(logits[:], psum[:, 0, :].rearrange("p (i e) -> p i e", e=64)[:, :, 0:n_out],
                                  spread(bias[:], 1, TT), ALU.add))
            one_hot(group_hot[:], lg, top, GROUPS)
            v.tensor_tensor(group_exp[:], lg, spread(top[:], 2, GROUPS), ALU.subtract).then_inc(soft, 1)
            after(v.tensor_scalar(masked[:].rearrange("p i (g e) -> p i g e", e=PER_GROUP),
                                  spread(group_hot[:], 3, PER_GROUP), 3e38, -3e38, ALU.mult, ALU.add))
            after(v.tensor_tensor(second[:].rearrange("p i (g e) -> p i g e", e=PER_GROUP),
                                  le.rearrange("p i (g e) -> p i g e", e=PER_GROUP),
                                  spread(group_hot[:], 3, PER_GROUP), ALU.mult))
            after(v.tensor_tensor(masked[:], masked[:], second[:], ALU.add))
            one_hot(first[:], masked[:], top1, EXPERTS)
            after(v.scalar_tensor_tensor(out=masked[:], in0=first[:], scalar=-3e38, in1=masked[:],
                                         op0=ALU.mult, op1=ALU.add))
            one_hot(second[:], masked[:], top2, EXPERTS)
            v.tensor_sub(ratio[:], top2[:], top1[:]).then_inc(soft, 1)
            after(v.tensor_add(cand[:], first[:], second[:]))
            after(v.tensor_copy(chosen[:], cand[:]))
            v.sem_inc(chosen_ready, 1)
            v.wait_ge(step_act, 2)
            after(v.tensor_reduce(p_group[:], group_exp[:], AX_X, ALU.add))
            after(v.tensor_scalar(share[:], ratio[:], 1.0, None, ALU.add))
            after(v.tensor_mul(share[:], share[:], p_group[:]))
            after(v.reciprocal(r.gates[:, :, 0], share[:]))
            after(v.tensor_mul(r.gates[:, :, 1], r.gates[:, :, 0], ratio[:]))
            v.wait_ge(product, 2)
            after(v.tensor_copy(count[:], psum[:, 2, 0:EXPERTS]))
            after(v.tensor_tensor(over[:], spread(count[:], 2, TT - 1), spread(limits[:], 1, EXPERTS), ALU.is_gt))
            after(v.tensor_reduce(extra[:], over[:], AX_X, ALU.add))
            after(v.tensor_tensor_scan(extra_end[:], c.ones[:, 0:EXPERTS], extra[:], 0.0, ALU.mult, ALU.add))
            after(v.tensor_sub(extra_base[:], extra_end[:], extra[:]))
            after(v.tensor_scalar(extra_base[:], extra_base[:], float(SLOTS), float(SLOTS * (EXPERTS - 1)), ALU.mult, ALU.add))
            after(v.tensor_sub(extra_base[:], extra_base[:], expert_base[:]))
            rank = psum[:, 1, 0:TT * EXPERTS].rearrange("p (i e) -> p i e", e=EXPERTS)
            after(v.tensor_scalar(slot[:], rank, float(SLOTS), None, ALU.is_ge))
            after(v.tensor_tensor(slot[:], slot[:], spread(extra_base[:], 1, TT), ALU.mult))
            after(v.tensor_tensor(slot[:], slot[:], rank, ALU.add))
            after(v.tensor_tensor(slot[:], slot[:], spread(expert_base[:], 1, TT), ALU.add))
            for choice, hot in enumerate((first, second)):
                after(v.tensor_mul(cand[:], slot[:], hot[:]))
                after(v.tensor_reduce(picked[:, :, choice], cand[:], AX_X, ALU.add))
            after(v.tensor_copy(slot_of[:], picked[:]))
            v.sem_inc(slots_ready, 1)
            after(v.tensor_tensor(passed[:], spread(extra_end[0:1, :], 1, EXTRA), spread(blocks[:], 2, EXPERTS), ALU.is_le))
            after(v.tensor_reduce(block_expert[:, 0:EXTRA], passed[:], AX_X, ALU.add))
            after(v.tensor_scalar(block_expert[:, 0:EXTRA], block_expert[:, 0:EXTRA], float(EXPERTS - 1), None, ALU.min))
            after(v.tensor_copy(block_expert[:, EXTRA:EXTRA + 1], extra_end[0:1, EXPERTS - 1:EXPERTS]))
            after(v.tensor_copy(r.extra_blocks[:], block_expert[:]))
            v.wait_ge(table_in, 16)
            after(v.tensor_copy(table_f[:], table[:]))
            v.sem_inc(table_ready, 1)
            v.wait_ge(product, 3)
            after(v.tensor_copy(r.scatter_row[:], psum[:, 3, 0:REGIONS]))
            after(v.tensor_scalar(r.gather_row[:], r.scatter_row[:], 1, None, ALU.arith_shift_right))


class Routing:

    def __init__(self, s):
        self.gates = s.sb("gates", [P, TT, 2])
        self.scatter_row = s.sb("scatter_row", [P, REGIONS], I32)
        self.gather_row = s.sb("gather_row", [P, REGIONS], I32)
        self.extra_blocks = s.sb("extra_blocks", [1, EXTRA + 1], I32)


class ExpertBuffers:
    def __init__(self, s):
        self.w_in = [s.sb(f"w_in{b}", [P, KT, 2 * FF]) for b in range(2)]
        self.w_out = [s.sb(f"w_out{b}", [P, FF // P, D]) for b in range(2)]
        self.x = [s.sb(f"x{b}", [P, D]) for b in range(2)]
        self.x_t = s.sb("x_t", [P, KT, P])
        self.silu = s.sb("silu", [P, FF])
        self.act = s.sb("act", [P, FF])
        self.act_t = s.sb("act_t", [P, FF // P, P])
        self.out = [s.sb(f"out{b}", [P, D]) for b in range(2)]
        self.gather_row = [s.sb(f"gather_row{b}", [P, 1], I32) for b in range(2)]
        self.scatter_row = [s.sb(f"scatter_row{b}", [P, 1], I32) for b in range(2)]
        self.psum = s.psum()
        self.gate_p = self.psum[:, 0, :]
        self.value_p = self.psum[:, 1, :]
        self.x_p = self.psum[:, 2:4, :].rearrange("p a (k t) -> p (a k) t", t=P)
        self.act_p = self.psum[:, 4, :].rearrange("p (k t) -> p k t", t=P)
        self.out_p = self.psum[:, 6:8, :].rearrange("p a e -> p (a e)")

    def turn_x(self, t, c, b):
        for k in range(KT):
            mm = t.transpose(self.x_p[:, k, :], self.x[b][:, k * P:(k + 1) * P], c.ident[:])
        return mm

    def up(self, t, b):
        for a in range(2):
            for k in range(KT):
                mm = t.matmul(self.psum[:, a, :], self.x_t[:, k, :], self.w_in[b][:, k, a * FF:(a + 1) * FF],
                              start=(k == 0), stop=(k == KT - 1))
        return mm

    def turn_act(self, t, c):
        for k in range(FF // P):
            mm = t.transpose(self.act_p[:, k, :], self.act[:, k * P:(k + 1) * P], c.ident[:])
        return mm

    def down(self, t, b):
        for a in range(2):
            for k in range(FF // P):
                mm = t.matmul(self.psum[:, 6 + a, :], self.act_t[:, k, :], self.w_out[b][:, k, a * HALF:(a + 1) * HALF],
                              start=(k == 0), stop=(k == FF // P - 1))
        return mm


def gather(g, d, e, b, bound):
    return g.indirect_dma_start(out=e.x[b][:], out_offset=None, in_=d.rows,
                                in_offset=bass.IndirectOffsetOnAxis(ap=e.gather_row[b][:], axis=0),
                                bounds_check=bound, oob_is_err=False)


def scatter(g, d, e, b, bound):
    return g.indirect_dma_start(out=d.expert_rows, in_=e.out[b][:], in_offset=None,
                                out_offset=bass.IndirectOffsetOnAxis(ap=e.scatter_row[b][:], axis=0),
                                bounds_check=bound, oob_is_err=False)


class Turn:

    def __init__(self, at, trip=None):
        self.trip, self.at, self.b = trip, at, at % 2
        self.n = at if trip is None else trip * 2 + at

    def has(self, first, last):
        return self.trip is not None or first <= self.at <= last

    def uses(self, ahead):
        k = (self.at + ahead) // 2 + 1
        return 16 * k if self.trip is None else self.trip * 16 + 16 * k


HEAD_TURNS = 3
TAIL_TURNS = 4


def all_turns(engine, turn):
    for n in range(HEAD_TURNS):
        turn(Turn(n))
    steady = EXPERTS + 1 - HEAD_TURNS - TAIL_TURNS
    with engine.Fori(0, steady // 2) as trip:
        for j in range(2):
            turn(Turn(HEAD_TURNS + j, trip))
    for n in range(HEAD_TURNS + steady, EXPERTS + 1):
        turn(Turn(n))


def experts(nc, io, c, d, r, layer, name):
    with Stage(nc, name) as s:
        e = ExpertBuffers(s)
        w_in_in = [s.sem(f"w_in_in{b}") for b in range(2)]
        w_out_in = [s.sem(f"w_out_in{b}") for b in range(2)]
        gathered = [s.sem(f"gathered{b}") for b in range(2)]
        scattered = [s.sem(f"scattered{b}") for b in range(2)]
        cleared, first_x, first_x_t, rows_set = (s.sem(x) for x in ("cleared", "first_x", "first_x_t", "rows_set"))
        pe = s.progress("pe", ["up", "turn_x", "down", "turn_act"], credit=2)
        dve = s.progress("dve", ["act", "x_t", "out"], credit=2)
        act = s.progress("act", ["silu", "out", "act_t"], credit=2)
        pool = s.progress("pool", ["gather_row", "scatter_row"], credit=2)
        block = s.block()
        last = EXPERTS - 1
        w_in = io["moe_w_in"][layer].rearrange("e (k p) f -> p e k f", p=P)
        w_out = io["moe_w_out"][layer].rearrange("e (k p) f -> p e k f", p=P)

        def of_expert(w, n):
            return w[:, ds(n, 1), :, :].rearrange("p e k f -> p (e k) f")

        @block.sync
        def _(sp):
            sp.dma_start(e.w_in[0][:], of_expert(w_in, 0)).then_inc(w_in_in[0], 16)
            sp.dma_start(e.w_out[0][:], of_expert(w_out, 0)).then_inc(w_out_in[0], 16)
            sp.dma_start(e.w_in[1][:], of_expert(w_in, 1)).then_inc(w_in_in[1], 16)

            def turn(t):
                if t.has(0, last - 2):
                    sp.wait_ge(pe.sem, pe.after("up", t.n))
                    sp.wait_ge(cleared, 2)
                    sp.dma_start(e.w_in[t.b][:], of_expert(w_in, t.n + 2)).then_inc(w_in_in[t.b], 16)
                if t.has(0, last - 1):
                    sp.wait_ge(pe.sem, pe.after("down", t.n))
                    sp.wait_ge(cleared, 2)
                    sp.dma_start(e.w_out[1 - t.b][:], of_expert(w_out, t.n + 1)).then_inc(w_out_in[1 - t.b], 16)

            all_turns(sp, turn)

        @block.gpsimd
        def _(g):
            last_token, last_assignment = g.to_reg(T - 1), g.to_reg(2 * T - 1)
            for b in range(2):
                g.memset(e.x[b][:], 0.0).then_inc(cleared, 1)
            g.wait_ge(cleared, 2)
            pool.open(g)
            for b in range(2):
                g.tensor_copy(e.gather_row[b][:], r.gather_row[:, b:b + 1]).then_inc(cleared, 1)
                g.wait_ge(cleared, 3 + b)
                gather(g, d, e, b, last_token).then_inc(gathered[b], 16)

            def turn(t):
                b = t.b
                if t.has(0, last - 2):
                    if t.trip is None and t.n == 0:
                        g.wait_ge(first_x, 1)
                    else:
                        g.wait_ge(pe.sem, pe.after("turn_x", t.n - 1))
                    g.wait_ge(gathered[b], t.uses(0))
                    g.wait_ge(cleared, 2)
                    g.tensor_copy(e.gather_row[b][:], r.gather_row[:, ds(t.n + 2, 1)]).then_inc(pool.sem, pool.count())
                    g.wait_ge(pool.sem, pool.after("gather_row", t.n))
                    g.sem_inc(rows_set, 1)
                    gather(g, d, e, b, last_token).then_inc(gathered[b], 16)
                else:
                    pool.skip()
                if t.has(1, last + 1):
                    g.wait_ge(dve.sem, dve.after("out", t.n))
                    g.wait_ge(act.sem, act.after("out", t.n))
                    if t.has(3, last + 1):
                        g.wait_ge(scattered[1 - b], t.uses(-3))
                    g.wait_ge(cleared, 2)
                    g.tensor_copy(e.scatter_row[1 - b][:], r.scatter_row[:, ds(t.n - 1, 1)]).then_inc(pool.sem, pool.count())
                    g.wait_ge(pool.sem, pool.after("scatter_row", t.n))
                    g.sem_inc(rows_set, 1)
                    scatter(g, d, e, 1 - b, last_assignment).then_inc(scattered[1 - b], 16)
                else:
                    pool.skip()

            all_turns(g, turn)
            for b in range(2):
                g.wait_ge(scattered[b], 16 * (EXPERTS // 2))

        @block.tensor
        def _(t_):
            pe.open(t_)
            t_.wait_ge(gathered[0], 16)
            e.turn_x(t_, c, 0).then_inc(first_x, 1)
            t_.wait_ge(first_x_t, 1)

            def turn(t):
                b = t.b
                if t.has(0, last):
                    t_.wait_ge(w_in_in[b], t.uses(0))
                    t_.wait_ge(dve.sem, dve.after("x_t", t.n - 1))
                    e.up(t_, b).then_inc(pe.sem, pe.count())
                else:
                    pe.skip()
                if t.has(0, last - 1):
                    t_.wait_ge(gathered[1 - b], t.uses(1))
                    e.turn_x(t_, c, 1 - b).then_inc(pe.sem, pe.count())
                else:
                    pe.skip()
                if t.has(1, last + 1):
                    t_.wait_ge(w_out_in[1 - b], t.uses(-1))
                    t_.wait_ge(act.sem, act.after("act_t", t.n - 1))
                    if t.has(2, last + 1):
                        t_.wait_ge(dve.sem, dve.after("out", t.n - 1))
                        t_.wait_ge(act.sem, act.after("out", t.n - 1))
                    e.down(t_, 1 - b).then_inc(pe.sem, pe.count())
                else:
                    pe.skip()
                if t.has(0, last):
                    t_.wait_ge(dve.sem, dve.after("act", t.n))
                    e.turn_act(t_, c).then_inc(pe.sem, pe.count())
                else:
                    pe.skip()

            all_turns(t_, turn)

        @block.vector
        def _(v):
            dve.open(v)
            gain = spread(c.gain(1, layer), 2, P)
            v.wait_ge(first_x, 1)
            v.tensor_tensor(e.x_t[:], e.x_p, gain, ALU.mult).then_inc(first_x_t, 1)

            def turn(t):
                if t.has(0, last):
                    v.wait_ge(act.sem, act.after("silu", t.n))
                    v.wait_ge(pe.sem, pe.after("turn_act", t.n - 1))
                    v.tensor_mul(e.act[:], e.silu[:], e.value_p).then_inc(dve.sem, dve.count())
                else:
                    dve.skip()
                if t.has(0, last - 1):
                    v.wait_ge(pe.sem, pe.after("turn_x", t.n))
                    v.tensor_tensor(e.x_t[:], e.x_p, gain, ALU.mult).then_inc(dve.sem, dve.count())
                else:
                    dve.skip()
                if t.has(1, last + 1):
                    v.wait_ge(pe.sem, pe.after("down", t.n))
                    if t.has(3, last + 1):
                        v.wait_ge(scattered[1 - t.b], t.uses(-3))
                    v.tensor_copy(e.out[1 - t.b][:, HALF:D], e.out_p[:, HALF:D]).then_inc(dve.sem, dve.count())
                else:
                    dve.skip()

            all_turns(v, turn)

        @block.scalar
        def _(a):
            act.open(a)

            def turn(t):
                if t.has(0, last):
                    a.wait_ge(pe.sem, pe.after("up", t.n))
                    a.wait_ge(dve.sem, dve.after("act", t.n - 1))
                    a.activation(e.silu[:], e.gate_p, ACT.Silu).then_inc(act.sem, act.count())
                else:
                    act.skip()
                if t.has(1, last + 1):
                    a.wait_ge(pe.sem, pe.after("down", t.n))
                    if t.has(3, last + 1):
                        a.wait_ge(scattered[1 - t.b], t.uses(-3))
                    a.activation(e.out[1 - t.b][:, 0:HALF], e.out_p[:, 0:HALF], ACT.Copy).then_inc(act.sem, act.count())
                else:
                    act.skip()
                if t.has(0, last):
                    a.wait_ge(pe.sem, pe.after("turn_act", t.n))
                    a.activation(e.act_t[:], e.act_p, ACT.Copy).then_inc(act.sem, act.count())
                else:
                    act.skip()

            all_turns(a, turn)


def extra_experts(nc, io, c, d, r, layer, name):
    with Stage(nc, name) as s:
        e = ExpertBuffers(s)
        x_in, w_in_in, w_out_in, scattered = (s.sem(x) for x in ("x_in", "w_in_in", "w_out_in", "scattered"))
        cleared, rows_set = s.sem("cleared"), s.sem("rows_set")
        pe = s.progress("pe", ["turn_x", "up", "turn_act", "down"])
        dve = s.progress("dve", ["x_t", "act"])
        act = s.progress("act", ["silu", "act_t", "out"])
        pool = s.progress("pool", ["gather_row", "scatter_row"])
        block = s.block()

        def for_each(engine, body):
            n_blocks = engine.value_load(r.extra_blocks[0:1, EXTRA:EXTRA + 1], min_val=0, max_val=EXTRA)
            with engine.Fori(0, EXTRA) as i:
                with engine.If(i < n_blocks):
                    body(i)
                with engine.Else():
                    engine.nop()

        @block.scalar
        def _(a):
            act.open(a)

            def body(i):
                expert = a.value_load(r.extra_blocks[0:1, ds(i, 1)], min_val=0, max_val=EXPERTS - 1)
                a.wait_ge(pe.sem, pe.after("down", i - 1))
                a.wait_ge(cleared, 1)
                a.dma_start(e.w_in[0][:], io["moe_w_in"][layer].rearrange("e (k p) f -> p e k f", p=P)
                            [:, ds(expert, 1), :, :].rearrange("p e k f -> p (e k) f")).then_inc(w_in_in, 16)
                a.dma_start(e.w_out[0][:], io["moe_w_out"][layer].rearrange("e (k p) f -> p e k f", p=P)
                            [:, ds(expert, 1), :, :].rearrange("p e k f -> p (e k) f")).then_inc(w_out_in, 16)
                a.wait_ge(pe.sem, pe.after("up", i))
                a.activation(e.silu[:], e.gate_p, ACT.Silu).then_inc(act.sem, 1)
                a.wait_ge(pe.sem, pe.after("turn_act", i))
                a.activation(e.act_t[:], e.act_p, ACT.Copy).then_inc(act.sem, 1)
                a.wait_ge(pe.sem, pe.after("down", i))
                a.wait_ge(pool.sem, pool.after("scatter_row", i - 1))
                a.activation(e.out[0][:], e.out_p, ACT.Copy).then_inc(act.sem, 1)

            for_each(a, body)

        @block.gpsimd
        def _(g):
            last_token, last_assignment = g.to_reg(T - 1), g.to_reg(2 * T - 1)
            g.memset(e.x[0][:], 0.0).then_inc(cleared, 1)
            g.wait_ge(cleared, 1)
            pool.open(g)

            def body(i):
                g.wait_ge(pe.sem, pe.after("turn_x", i - 1))
                g.wait_ge(cleared, 1)
                g.tensor_copy(e.gather_row[0][:], r.gather_row[:, ds(i + EXPERTS, 1)]).then_inc(pool.sem, 1)
                g.wait_ge(pool.sem, pool.after("gather_row", i))
                g.sem_inc(rows_set, 1)
                gather(g, d, e, 0, last_token).then_inc(x_in, 16)
                g.wait_ge(act.sem, act.after("out", i))
                g.wait_ge(cleared, 1)
                g.tensor_copy(e.scatter_row[0][:], r.scatter_row[:, ds(i + EXPERTS, 1)]).then_inc(cleared, 1)
                g.wait_ge(cleared, i + 2)
                g.sem_inc(rows_set, 1)
                scatter(g, d, e, 0, last_assignment).then_inc(scattered, 16)
                g.wait_ge(scattered, i * 16 + 16)
                g.sem_inc(pool.sem, 1)

            for_each(g, body)

        @block.tensor
        def _(t):
            pe.open(t)

            def body(i):
                t.wait_ge(x_in, i * 16 + 16)
                e.turn_x(t, c, 0).then_inc(pe.sem, 1)
                t.wait_ge(dve.sem, dve.after("x_t", i))
                t.wait_ge(w_in_in, i * 16 + 16)
                e.up(t, 0).then_inc(pe.sem, 1)
                t.wait_ge(dve.sem, dve.after("act", i))
                e.turn_act(t, c).then_inc(pe.sem, 1)
                t.wait_ge(act.sem, act.after("act_t", i))
                t.wait_ge(w_out_in, i * 16 + 16)
                t.wait_ge(act.sem, act.after("out", i - 1))
                e.down(t, 0).then_inc(pe.sem, 1)

            for_each(t, body)

        @block.vector
        def _(v):
            dve.open(v)

            def body(i):
                v.wait_ge(pe.sem, pe.after("turn_x", i))
                v.tensor_tensor(e.x_t[:], e.x_p, spread(c.gain(1, layer), 2, P), ALU.mult).then_inc(dve.sem, 1)
                v.wait_ge(act.sem, act.after("silu", i))
                v.tensor_mul(e.act[:], e.silu[:], e.value_p).then_inc(dve.sem, 1)

            for_each(v, body)


def combine(nc, c, d, r, name, hidden, hidden_out):
    with Stage(nc, name) as s:
        h = [s.sb(f"h{b}", [P, D]) for b in range(2)]
        rows = [s.sb(f"rows{b}", [P, 2, D]) for b in range(2)]
        h_in = [s.sem(f"h_in{b}") for b in range(2)]
        rows_in = [s.sem(f"rows_in{b}") for b in range(2)]
        stored = [s.sem(f"stored{b}") for b in range(2)]
        opened = s.sem("opened")
        dve = s.progress("dve", ["first", "second"], credit=2)
        block = s.block()

        @block.sync
        def _(sp):
            with sp.Fori(0, TT // 2) as trip:
                for b in range(2):
                    tile = trip * 2 + b
                    sp.wait_ge(dve.sem, dve.after("second", tile - 2))
                    sp.wait_ge(stored[b], trip * 16 + 16)
                    sp.wait_ge(opened, 1)
                    sp.dma_start(h[b][:], hidden[ds(tile * P, P), :]).then_inc(h_in[b], 16)
                    sp.dma_start(rows[b][:], d.expert_rows.rearrange("(t a) e -> t a e", a=2)
                                 [ds(tile * P, P), :, :]).then_inc(rows_in[b], 16)

        @block.vector
        def _(v):
            v.sem_inc(opened, 1)
            dve.open(v)
            with v.Fori(0, TT // 2) as trip:
                for b in range(2):
                    tile = trip * 2 + b
                    v.wait_ge(h_in[b], trip * 16 + 16)
                    v.wait_ge(rows_in[b], trip * 16 + 16)
                    for choice, step in enumerate(("first", "second")):
                        v.scalar_tensor_tensor(out=h[b][:], in0=rows[b][:, choice, :], in1=h[b][:],
                                               scalar=r.gates[:, ds(tile, 1), choice:choice + 1]
                                               .rearrange("p a c -> p (a c)"),
                                               op0=ALU.mult, op1=ALU.add).then_inc(dve.sem, 1)
                        if choice == 0:
                            v.wait_ge(dve.sem, dve.after("first", tile))

        @block.scalar
        def _(a):
            for b in range(2):
                a.sem_inc(stored[b], 16)
            with a.Fori(0, TT // 2) as trip:
                for b in range(2):
                    tile = trip * 2 + b
                    a.wait_ge(dve.sem, dve.after("second", tile))
                    a.wait_ge(opened, 1)
                    a.dma_start(hidden_out[ds(tile * P, P), :], h[b][:]).then_inc(stored[b], 16)
            for b in range(2):
                a.wait_ge(stored[b], 16 * (TT // 2) + 16)


def mixture(nc, io, c, d, layer, hidden, hidden_out):
    name = f"moe{layer}"
    with Stage(nc, name) as s:
        r = Routing(s)
        with Stage(nc, f"{name}_in") as s2:
            u = s2.sb("u", [P, KT, T])
            norm(nc, c, f"{name}_norm", hidden, c.gain(1, layer), u, 0, d.rows)
            route(nc, io, c, d, r, layer, f"{name}_route", u)
        experts(nc, io, c, d, r, layer, f"{name}_first")
        extra_experts(nc, io, c, d, r, layer, f"{name}_extra")
        combine(nc, c, d, r, f"{name}_sum", hidden, hidden_out)


def hgrn_project(nc, io, c, d, u):
    with Stage(nc, "hproj") as s:
        ring = [s.sb(f"ring{b}", [P, KT, 2 * P]) for b in range(2)]
        wide = [s.sb(f"wide{b}", [P, KT, HALF]) for b in range(NH)]
        out = [s.sb(f"out{b}", [P, T]) for b in range(2)]
        key = [s.sb(f"key{b}", [P, T]) for b in range(2)]
        psum = s.psum()
        ring_in = [s.sem(f"ring_in{b}") for b in range(2)]
        wide_in = [s.sem(f"wide_in{b}") for b in range(NH)]
        stored = [s.sem(f"stored{b}") for b in range(2)]
        keys_out = [s.sem(f"keys_out{b}") for b in range(2)]
        rows_out = [s.sem(f"rows_out{b}") for b in range(2)]
        n_tiles = (2 * HG_FD + D) // P
        first_gate = 2 * HG_FD // P
        tiles_pe = s.progress("tiles_pe", ["tile"], credit=2)
        tiles_act = s.progress("tiles_act", ["out"], credit=2)
        sig_act, key_act, key_dve = s.sem("sig_act"), s.sem("key_act"), s.sem("key_dve")
        rows_pe, rows_dve = s.sem("rows_pe"), s.sem("rows_dve")
        block = s.block()
        w = io["hg_in"][0].rearrange("(k p) e -> p k e", p=P)
        columns = [HG_FD, HG_FD + 2 * P, 0, 2 * P] + [2 * HG_FD + D + i * 2 * P for i in range(D // (2 * P))]

        @block.sync
        def _(sp):
            for n, at in enumerate(columns):
                if n >= 2:
                    sp.wait_ge(tiles_pe.sem, tiles_pe.after("tile", 2 * (n - 2) + 1))
                sp.dma_start(ring[n % 2][:], w[:, :, at:at + 2 * P]).then_inc(ring_in[n % 2], 16)
                if n == 1:
                    for a in range(NH):
                        at = 2 * HG_FD + a * HALF
                        sp.dma_start(wide[a][:], w[:, :, at:at + HALF]).then_inc(wide_in[a], 16)

        def rows_buf(i):
            return key[i % 2][:]

        def pair(b):
            return psum[:, 2 * b:2 * b + 2, :].rearrange("p a t -> p (a t)")

        @block.tensor
        def _(t):
            tiles_pe.open(t)

            def four(first, trip):
                for n in range(4):
                    tile = first + n if trip is None else trip * 4 + first + n
                    if n % 2 == 0:
                        uses = first // 4 if trip is None else trip + first // 4
                        t.wait_ge(ring_in[n // 2], uses * 16 + 16)
                    t.wait_ge(tiles_act.sem, tiles_act.after("out", tile - 2))
                    for half in range(NH):
                        for k in range(KT):
                            mm = t.matmul(psum[:, 2 * (n % 2) + half, :], ring[n // 2][:, k, (n % 2) * P:(n % 2 + 1) * P],
                                          u[:, k, half * HALF:(half + 1) * HALF], start=(k == 0), stop=(k == KT - 1))
                    mm.then_inc(tiles_pe.sem, 1)

            four(0, None)
            four(4, None)
            with t.Fori(0, (n_tiles - first_gate) // 4) as trip:
                four(first_gate, trip)
            for i in range(TT):
                if i >= 2:
                    t.wait_ge(rows_dve, i - 1)
                for a in range(NH):
                    if i == 0:
                        t.wait_ge(wide_in[a], 16)
                    for k in range(KT):
                        mm = t.matmul(psum[:, 4 + 2 * (i % 2) + a, :], u[:, k, i * P:(i + 1) * P], wide[a][:, k, :],
                                      start=(k == 0), stop=(k == KT - 1))
                mm.then_inc(rows_pe, 1)

        @block.scalar
        def _(a):
            tiles_act.open(a)
            for tile in range(HG_PAIRS):
                b = tile % 2
                a.wait_ge(tiles_pe.sem, tiles_pe.after("tile", tile))
                if tile >= 2:
                    a.wait_ge(keys_out[b], 16 * (tile // 2))
                    a.wait_ge(stored[b], 16 * (tile // 2))
                a.activation(key[b][:], pair(b), ACT.Sigmoid, scale=-1.0).then_inc(key_act, 1)
                a.activation(out[b][:], pair(b), ACT.Sigmoid).then_inc(sig_act, 1)
                a.wait_ge(sig_act, tile + 1)
                a.activation(out[b][:], out[b][:], ACT.Ln, scale=c.one_less_lb[:, tile:tile + 1],
                             bias=c.lb[:, tile:tile + 1]).then_inc(tiles_act.sem, 1)
                a.wait_ge(tiles_act.sem, tiles_act.after("out", tile))
                a.dma_start(d.cm["decay"][tile * P:(tile + 1) * P, :], out[b][:]).then_inc(stored[b], 16)
                a.wait_ge(key_dve, tile + 1)
                a.dma_start(d.cm["k"][tile * P:(tile + 1) * P, :], key[b][:]).then_inc(keys_out[b], 16)
            for tile in range(HG_PAIRS):
                b = tile % 2
                a.wait_ge(tiles_pe.sem, tiles_pe.after("tile", tile + HG_PAIRS))
                a.wait_ge(stored[b], 16 * (tile // 2 + 2))
                a.activation(out[b][:], pair(b), ACT.Silu).then_inc(tiles_act.sem, 1)
                a.wait_ge(tiles_act.sem, tiles_act.after("out", tile + HG_PAIRS))
                a.dma_start(d.cm["r"][tile * P:(tile + 1) * P, :], out[b][:]).then_inc(stored[b], 16)
            with a.Fori(0, KT // 2) as trip:
                for b in range(2):
                    tile = trip * 2 + b
                    a.wait_ge(tiles_pe.sem, tiles_pe.after("tile", tile + first_gate))
                    a.wait_ge(stored[b], trip * 16 + 16 * HG_PAIRS)
                    a.activation(out[b][:], pair(b), ACT.Silu).then_inc(tiles_act.sem, 1)
                    a.wait_ge(tiles_act.sem, tiles_act.after("out", tile + first_gate))
                    a.dma_start(d.cm["gate"][ds(tile * P, P), :], out[b][:]).then_inc(stored[b], 16)
            for i in range(TT):
                a.wait_ge(rows_dve, i + 1)
                a.dma_start(d.v_rows[i * P:(i + 1) * P, :], rows_buf(i)).then_inc(rows_out[i % 2], 16)
            for b in range(2):
                a.wait_ge(stored[b], 16 * (HG_PAIRS + KT // 2))
                a.wait_ge(keys_out[b], 16 * (HG_PAIRS // 2))
                a.wait_ge(rows_out[b], 16 * (TT // 2))

        @block.vector
        def _(v):
            for tile in range(HG_PAIRS):
                v.wait_ge(key_act, tile + 1)
                v.tensor_scalar(key[tile % 2][:], key[tile % 2][:], c.one_less_lb[:, tile:tile + 1], None,
                                ALU.mult).then_inc(key_dve, 1)
            for b in range(2):
                v.wait_ge(keys_out[b], 16 * (HG_PAIRS // 2))
            for i in range(TT):
                v.wait_ge(rows_pe, i + 1)
                if i >= 2:
                    v.wait_ge(rows_out[i % 2], 16 * (i // 2))
                v.tensor_copy(rows_buf(i), pair(2 + i % 2)).then_inc(rows_dve, 1)


def hgrn_scan(nc, c, d, o):
    with Stage(nc, "hscan") as s:
        names = ("decay", "r", "k")
        fresh = {n: s.sb(n, [P, HG_PAIRS, 2 * CHUNK]) for n in names}
        total = s.sb("total", [P, HG_PAIRS, 2, CHUNK])
        offset = s.sb("offset", [P, HG_PAIRS, 2, CHUNK])
        down = s.sb("down", [P, HG_PAIRS, 2, CHUNK])
        up = s.sb("up", [P, HG_PAIRS, 2, CHUNK])
        late = s.sb("late", [P, HG_PAIRS, 2])
        e_mid = s.sb("e_mid", [P, HG_PAIRS, 2])
        e_end = s.sb("e_end", [P, HG_PAIRS, 2])
        e_late = s.sb("e_late", [P, HG_PAIRS, 2])
        q = s.sb("q", [P, HG_PAIRS, 2 * CHUNK])
        q_bd = [s.sb(f"q_bd{b}", [P, HG_PAIRS, P]) for b in range(2)]
        k_bd = [s.sb(f"k_bd{b}", [P, HG_PAIRS, P]) for b in range(2)]
        k_rows = s.sb("k_rows", [P, HG_PAIRS, P])
        values = [s.sb(f"values{b}", [P, HG_PAIRS, P]) for b in range(2)]
        att_t = s.sb("att_t", [P, HG_PAIRS, P])
        state = s.sb("state", [P, HG_PAIRS, P])
        state_mid = s.sb("state_mid", [P, HG_PAIRS, P])
        grown = s.sb("grown", [P, HG_PAIRS, P])
        psum = s.psum()

        def bank(n):
            return psum[:, n, :].rearrange("p (m e) -> p m e", e=P)

        arrived, ready, zeroed = s.sem("arrived"), s.sem("ready"), s.sem("zeroed")
        v_in = [s.sem(f"v_in{b}") for b in range(2)]
        v_trip = s.progress("v_trip", ["total", "offset", "clamp", "late", "q"])
        a_trip = s.progress("a_trip", ["down", "up", "mid", "end", "late"])
        prep = s.progress("prep", ["q_bd", "k_bd"], credit=2)
        dve = s.progress("dve", ["state_mid", "att", "grown", "kept", "S"], credit=2)
        act = s.progress("act", ["k_rows", "o"], credit=2)
        pe = s.progress("pe", ["att", "k_rows", "o", "S"], credit=2)
        block = s.block()

        @block.sync
        def _(sp):
            with sp.Fori(0, CHUNKS // 2) as trip:
                sp.wait_ge(prep.sem, prep.after("k_bd", trip * 2 - 1))
                sp.wait_ge(v_trip.sem, v_trip.after("q", trip - 1))
                sp.wait_ge(ready, 1)
                for n in names:
                    sp.dma_start(fresh[n][:], d.cm[n].rearrange("(m p) t -> p m t", p=P)
                                 [:, 0:HG_PAIRS, ds(trip * 2 * CHUNK, 2 * CHUNK)]).then_inc(arrived, 16)
                for b in range(2):
                    chunk = trip * 2 + b
                    sp.wait_ge(pe.sem, pe.after("S", chunk - 2))
                    sp.wait_ge(ready, 1)
                    for h in range(2):
                        sp.dma_start(values[b][h * CHUNK:(h + 1) * CHUNK, :, :],
                                     d.v_rows.rearrange("t (m h e) -> t m h e", h=2, e=P)
                                     [ds(chunk * CHUNK, CHUNK), :, h, :]).then_inc(v_in[b], 16)

        @block.gpsimd
        def _(g):
            for z in (*q_bd, *k_bd, state):
                g.memset(z[:], 0.0).then_inc(zeroed, 1)
            g.wait_ge(zeroed, 5)
            g.sem_inc(ready, 1)

        @block.vector
        def _(v):
            v.wait_ge(ready, 1)
            v_trip.open(v)
            prep.open(v)
            dve.open(v)
            with v.Fori(0, CHUNKS // 2) as trip:
                def after_own(step):
                    v.wait_ge(v_trip.sem, v_trip.after(step, trip))
                v.wait_ge(arrived, 48 * trip + 48)
                v.tensor_tensor_scan(total[:].rearrange("p m c t -> p (m c t)"), c.chunk_start[:, 0:HG_PAIRS * 2 * CHUNK],
                                     fresh["decay"][:].rearrange("p m t -> p (m t)"), 0.0,
                                     ALU.mult, ALU.add).then_inc(v_trip.sem, 1)
                after_own("total")
                v.wait_ge(a_trip.sem, a_trip.after("up", trip - 1))
                flat = total[:].rearrange("p m c t -> p (m c) t")
                v.tensor_tensor(offset[:].rearrange("p m c t -> p (m c) t"), flat, spread(flat[:, :, CHUNK // 2 - 1], 2, CHUNK),
                                ALU.subtract).then_inc(v_trip.sem, 1)
                after_own("offset")
                v.tensor_scalar(offset[:], offset[:], -MAX_EXP, MAX_EXP, ALU.max, ALU.min).then_inc(v_trip.sem, 1)
                v.tensor_sub(late[:], total[:, :, :, CHUNK - 1], total[:, :, :, CHUNK // 2 - 1]).then_inc(v_trip.sem, 1)
                v.wait_ge(a_trip.sem, a_trip.after("up", trip))
                v.wait_ge(pe.sem, pe.after("att", trip * 2 - 1))
                v.tensor_mul(q[:], fresh["r"][:], down[:].rearrange("p m c t -> p m (c t)")).then_inc(v_trip.sem, 1)
                for b in range(2):
                    chunk = trip * 2 + b
                    at = slice(b * CHUNK, (b + 1) * CHUNK)
                    v.wait_ge(v_trip.sem, v_trip.after("q", trip))
                    v.wait_ge(pe.sem, pe.after("o", chunk - 2))
                    for h in range(2):
                        rows = slice(h * HEAD, (h + 1) * HEAD)
                        copy = v.tensor_copy(q_bd[b][rows, :, rows], q[rows, :, at])
                    copy.then_inc(prep.sem, 1)
                    for h in range(2):
                        rows = slice(h * HEAD, (h + 1) * HEAD)
                        mul = v.tensor_mul(k_bd[b][rows, :, rows], fresh["k"][rows, :, at], up[rows, :, b, :])
                    mul.then_inc(prep.sem, 1)
                    v.wait_ge(a_trip.sem, a_trip.after("late", trip))
                    v.wait_ge(dve.sem, dve.after("S", chunk - 1))
                    v.wait_ge(pe.sem, pe.after("o", chunk - 1))
                    v.tensor_tensor(state_mid[:], state[:], spread(e_mid[:, :, b], 2, P), ALU.mult).then_inc(dve.sem, 1)
                    v.wait_ge(pe.sem, pe.after("att", chunk))
                    v.tensor_tensor(att_t[:].rearrange("p m (h t) -> p m h t", h=2),
                                    spread(psum[:, 0, 0:HG_PAIRS * CHUNK].rearrange("p (m t) -> p m t", t=CHUNK), 2, 2),
                                    spread(c.up_incl_bd[:].rearrange("p (h t) -> p h t", h=2), 1, HG_PAIRS),
                                    ALU.mult).then_inc(dve.sem, 1)
                    v.wait_ge(pe.sem, pe.after("S", chunk))
                    v.tensor_tensor(grown[:], bank(3), spread(e_late[:, :, b], 2, P), ALU.mult).then_inc(dve.sem, 1)
                    v.wait_ge(dve.sem, dve.after("state_mid", chunk))
                    v.tensor_tensor(state[:], state[:], spread(e_end[:, :, b], 2, P), ALU.mult).then_inc(dve.sem, 1)
                    v.wait_ge(dve.sem, dve.after("kept", chunk))
                    v.tensor_add(state[:], state[:], grown[:]).then_inc(dve.sem, 1)

        @block.scalar
        def _(a):
            a_trip.open(a)
            act.open(a)
            with a.Fori(0, CHUNKS // 2) as trip:
                a.wait_ge(v_trip.sem, v_trip.after("late", trip))
                a.wait_ge(dve.sem, dve.after("S", trip * 2 - 1))
                a.activation(down[:], offset[:], ACT.Exp).then_inc(a_trip.sem, 1)
                a.activation(up[:], offset[:], ACT.Exp, scale=-1.0).then_inc(a_trip.sem, 1)
                a.activation(e_mid[:], total[:, :, :, CHUNK // 2 - 1], ACT.Exp).then_inc(a_trip.sem, 1)
                a.activation(e_end[:], total[:, :, :, CHUNK - 1], ACT.Exp).then_inc(a_trip.sem, 1)
                a.activation(e_late[:], late[:], ACT.Exp).then_inc(a_trip.sem, 1)
                for b in range(2):
                    chunk = trip * 2 + b
                    a.wait_ge(pe.sem, pe.after("k_rows", chunk))
                    a.wait_ge(pe.sem, pe.after("S", chunk - 1))
                    a.activation(k_rows[:], bank(1), ACT.Copy).then_inc(act.sem, 1)
                    a.wait_ge(pe.sem, pe.after("o", chunk))
                    a.activation(o[:, :, ds(chunk * CHUNK, CHUNK)], psum[:, 2, :].rearrange("p (h t) -> p h t", t=CHUNK),
                                 ACT.Copy).then_inc(act.sem, 1)

        @block.tensor
        def _(t):
            pe.open(t)
            with t.Fori(0, CHUNKS // 2) as trip:
                for b in range(2):
                    chunk = trip * 2 + b
                    t.wait_ge(prep.sem, prep.after("k_bd", chunk))
                    t.wait_ge(dve.sem, dve.after("att", chunk - 1))
                    for m in range(HG_PAIRS):
                        mm = t.matmul(psum[:, 0, m * CHUNK:(m + 1) * CHUNK], k_bd[b][:, m, :],
                                      q[:, m, b * CHUNK:(b + 1) * CHUNK], start=True, stop=True)
                    mm.then_inc(pe.sem, 1)
                    t.wait_ge(act.sem, act.after("k_rows", chunk - 1))
                    for m in range(HG_PAIRS):
                        mm = t.transpose(bank(1)[:, m, :], k_bd[b][:, m, :], c.ident[:])
                    mm.then_inc(pe.sem, 1)
                    t.wait_ge(v_in[b], 32 * trip + 32)
                    t.wait_ge(dve.sem, dve.after("att", chunk))
                    t.wait_ge(act.sem, act.after("o", chunk - 1))
                    for m in range(HG_PAIRS):
                        t.matmul(bank(2)[:, m, :], state_mid[:, m, :], q_bd[b][:, m, :], start=True, stop=False)
                        mm = t.matmul(bank(2)[:, m, :], values[b][:, m, :], att_t[:, m, :], start=False, stop=True)
                    mm.then_inc(pe.sem, 1)
                    t.wait_ge(act.sem, act.after("k_rows", chunk))
                    t.wait_ge(dve.sem, dve.after("grown", chunk - 1))
                    for m in range(HG_PAIRS):
                        mm = t.matmul(bank(3)[:, m, :], k_rows[:, m, :], values[b][:, m, :], start=True, stop=True)
                    mm.then_inc(pe.sem, 1)


def hgrn_output(nc, io, c, d, o):
    with Stage(nc, "hnorm") as s:
        gate = [s.sb(f"gate{b}", [P, T]) for b in range(2)]
        squares = [s.sb(f"squares{b}", [P, T]) for b in range(2)]
        inv = [s.sb(f"inv{b}", [P, T]) for b in range(2)]
        psum = s.psum()
        loaded = [s.sem(f"loaded{b}") for b in range(2)]
        opened = s.sem("opened")
        pe = s.progress("pe", ["squares"], credit=2)
        dve = s.progress("dve", ["mean", "unit"], credit=2)
        act = s.progress("act", ["square", "ln", "inverse"], credit=2)
        pool = s.progress("pool", ["gate"], credit=2)
        block = s.block()

        @block.sync
        def _(sp):
            with sp.Fori(0, HG_HEADS // 2) as trip:
                for b in range(2):
                    tile = trip * 2 + b
                    sp.wait_ge(pool.sem, pool.after("gate", tile - 2))
                    sp.wait_ge(opened, 1)
                    sp.dma_start(gate[b][:], d.cm["gate"][ds(tile * P, P), :]).then_inc(loaded[b], 16)

        @block.tensor
        def _(t):
            pe.open(t)
            with t.Fori(0, HG_HEADS // 2) as trip:
                for b in range(2):
                    tile = trip * 2 + b
                    t.wait_ge(act.sem, act.after("square", tile))
                    t.wait_ge(dve.sem, dve.after("mean", tile - 2))
                    for half in range(NH):
                        mm = t.matmul(psum[:, 2 * b + half, :], c.ones[:], squares[b][:, half * HALF:(half + 1) * HALF],
                                      start=True, stop=True)
                    mm.then_inc(pe.sem, 1)

        @block.scalar
        def _(a):
            act.open(a)
            with a.Fori(0, HG_HEADS // 2) as trip:
                for b in range(2):
                    tile = trip * 2 + b
                    a.wait_ge(pe.sem, pe.after("squares", tile - 2))
                    a.activation(squares[b][:], o[:, tile, :], ACT.Square).then_inc(act.sem, 1)
                    a.wait_ge(dve.sem, dve.after("mean", tile))
                    a.activation(inv[b][:], inv[b][:], ACT.Ln).then_inc(act.sem, 1)
                    a.wait_ge(act.sem, act.after("ln", tile))
                    a.activation(inv[b][:], inv[b][:], ACT.Exp, scale=-0.5).then_inc(act.sem, 1)

        @block.vector
        def _(v):
            v.sem_inc(opened, 1)
            dve.open(v)
            with v.Fori(0, HG_HEADS // 2) as trip:
                for b in range(2):
                    tile = trip * 2 + b
                    v.wait_ge(pe.sem, pe.after("squares", tile))
                    v.wait_ge(dve.sem, dve.after("unit", tile - 2))
                    v.tensor_scalar(inv[b][:], psum[:, 2 * b:2 * b + 2, :].rearrange("p a t -> p (a t)"),
                                    1.0 / P, RMS_EPS, ALU.mult, ALU.add).then_inc(dve.sem, 1)
                    v.wait_ge(act.sem, act.after("inverse", tile))
                    v.scalar_tensor_tensor(out=o[:, tile, :], in0=o[:, tile, :], scalar=c.hg_norm(), in1=inv[b][:],
                                           op0=ALU.mult, op1=ALU.mult).then_inc(dve.sem, 1)

        @block.gpsimd
        def _(g):
            pool.open(g)
            with g.Fori(0, HG_HEADS // 2) as trip:
                for b in range(2):
                    tile = trip * 2 + b
                    g.wait_ge(loaded[b], trip * 16 + 16)
                    g.wait_ge(dve.sem, dve.after("unit", tile))
                    g.wait_ge(opened, 1)
                    g.tensor_mul(o[:, tile, :], o[:, tile, :], gate[b][:]).then_inc(pool.sem, 1)


def build(nc, io, out):
    c = Constants(nc)
    d = Scratch(nc)
    x = io["x"].rearrange("b t d -> (b t) d")
    with Stage(nc, "start") as s:
        first = s.sem("first")
    setup(nc, io, c)
    with Stage(nc, "rwkv_in") as s:
        u = s.sb("u", [P, KT, 1 + T])
        norm(nc, c, "rwkv_norm", x, c.gain(0, 0), u, 1)
        rwkv_project(nc, io, c, u, d)
    with Stage(nc, "rwkv") as s:
        y = s.sb("y", [P, PAIRS, T])
        rwkv_scan(nc, c, d, y)
        rwkv_output(nc, io, c, d, y)
        project_out(nc, "rwkv_out", io["rw_out"][0], y, x, d.hidden)
    mixture(nc, io, c, d, 0, d.hidden, d.hidden)
    with Stage(nc, "mark") as s:
        unused = s.sem("unused")
    clear_semaphores(nc, first.num, unused.num - 1)
    with Stage(nc, "hgrn") as s:
        with Stage(nc, "hgrn_in") as s2:
            u = s2.sb("u", [P, KT, T])
            norm(nc, c, "hgrn_norm", d.hidden, c.gain(0, 1), u, 0)
            hgrn_project(nc, io, c, d, u)
        o = s.sb("o", [P, HG_HEADS, T])
        hgrn_scan(nc, c, d, o)
        hgrn_output(nc, io, c, d, o)
        project_out(nc, "hgrn_out", io["hg_out"][0], o, d.hidden, d.hidden)
    mixture(nc, io, c, d, 1, d.hidden, out.rearrange("b t d -> (b t) d"))


_NAMES = ["x", "norm1_g", "norm2_g", "rw_mu", "rw_in", "rw_w0", "rw_w1", "rw_w2", "rw_a0", "rw_a1", "rw_a2",
          "rw_g1", "rw_g2", "rw_kk", "rw_ka", "rw_rk", "rw_ln_w", "rw_ln_b", "rw_out", "hg_lower", "hg_in",
          "hg_norm", "hg_out", "moe_rg", "moe_rg_b", "moe_re", "moe_re_b", "moe_w_in", "moe_w_out"]


def kernel(**inputs):
    import numpy as np
    import concourse.bacc as bacc
    from concourse.bass_utils import run_bass_kernel_spmd

    nc = bacc.Bacc("TRN2", target_bir_lowering=False, num_devices=1)
    arrays, io = {}, {}
    for name in _NAMES:
        a = np.ascontiguousarray(inputs[name])
        arrays[f"in_{name}"] = a
        io[name] = nc.dram_tensor(f"in_{name}", a.shape, mybir.dt.from_np(a.dtype), kind="ExternalInput").ap()
    out = nc.dram_tensor("out", (1, T, D), F32, kind="ExternalOutput").ap()
    build(nc, io, out)
    r = run_bass_kernel_spmd(nc, [arrays], core_ids=[0])
    return r.results[0]["out"]
```

```python
from contextlib import ExitStack

import concourse.bass as bass
from concourse import mybir

F32 = mybir.dt.float32
BF16 = mybir.dt.bfloat16
I32 = mybir.dt.int32
ALU = mybir.AluOpType
ACT = mybir.ActivationFunctionType
AX_X = mybir.AxisListType.X
ds = bass.ds

P = 128
T = 1024
D = 1024
KT = D // P
TT = T // P
HALF = 512
NH = T // HALF
HEAD = 64
PAIRS = D // P
CHUNK = 64
CHUNKS = T // CHUNK
LEVELS = 5
DECAY = 0.6065306597126334
RMS_EPS = 1e-6
GN_EPS = 64e-5
HG_PAIRS = 4
HG_HEADS = 8
HG_FD = 512
MAX_EXP = 80.0
GROUPS, PER_GROUP = 4, 8
EXPERTS = GROUPS * PER_GROUP
FF = 512
SLOTS = 128
EXTRA = 15
REGIONS = EXPERTS + EXTRA
NO_TOKEN = 4096


class Progress:

    def __init__(self, sem, steps, credit=1):
        self.sem, self.steps, self.credit, self.skipped = sem, steps, credit, 0

    def open(self, engine):
        engine.sem_inc(self.sem, self.credit * len(self.steps))

    def skip(self):
        self.skipped += 1

    def count(self):
        n, self.skipped = 1 + self.skipped, 0
        return n

    def after(self, step, trip):
        return trip * len(self.steps) + (self.credit * len(self.steps) + self.steps.index(step) + 1)


def spread(ap, axis, n):
    shape = list(ap.shape)
    shape.insert(axis, n)
    return ap.unsqueeze(axis).to_broadcast(shape)


class Stage:

    used = set()

    def __init__(self, nc, name):
        self.nc, self.name, self.ctx = nc, name, ExitStack()

    def __enter__(self):
        self.ctx.__enter__()
        return self

    def __exit__(self, *e):
        return self.ctx.__exit__(*e)

    def sb(self, name, shape, dt=F32):
        return self.ctx.enter_context(self.nc.sbuf_tensor(f"{self.name}_{name}", shape, dt))

    def psum(self, name="psum"):
        return self.ctx.enter_context(self.nc.psum_tensor(f"{self.name}_{name}", [P, 8, HALF], F32))

    def sem(self, name):
        sem = self.ctx.enter_context(self.nc.semaphore(f"{self.name}_{name}"))
        self.used.add(sem.num)
        return sem

    def progress(self, name, steps, credit=1):
        return Progress(self.sem(name), steps, credit)

    def block(self):
        return self.ctx.enter_context(self.nc.Block())


def clear_semaphores(nc):
    E = mybir.EngineType
    nc.multi_engine_barrier([E.Pool, E.SP, E.Activation, E.DVE, E.PE],
                            sems_to_clear=range(min(Stage.used), max(Stage.used) + 1))


PARAM_ROWS = ["mu", "w0", "a0", "kk", "ka", "rk", "ln_w", "ln_b"]


def setup(nc, io, c):
    with Stage(nc, "setup") as s:
        raw_a = s.sb("raw_a", [P, P])
        raw_b = s.sb("raw_b", [P, P])
        psum = s.psum()
        zeroed, shaped, loaded, turned = (s.sem(x) for x in ("zeroed", "shaped", "loaded", "turned"))
        rows = [(io["rw_mu"].rearrange("l j (k p) -> (l j k) p", p=P), 48),
                (io["rw_w0"].rearrange("l (k p) -> (l k) p", p=P), 8),
                (io["rw_a0"].rearrange("l (k p) -> (l k) p", p=P), 8),
                (io["rw_kk"].rearrange("l (k p) -> (l k) p", p=P), 8),
                (io["rw_ka"].rearrange("l (k p) -> (l k) p", p=P), 8),
                (io["rw_rk"].rearrange("l (k a) d -> (l k) (a d)", a=2), 8),
                (io["rw_ln_w"].rearrange("l (k p) -> (l k) p", p=P), 8),
                (io["rw_ln_b"].rearrange("l (k p) -> (l k) p", p=P), 8)]
        rows_b = [(io["norm1_g"].rearrange("l (k p) -> (l k) p", p=P), 16),
                  (io["norm2_g"].rearrange("l (k p) -> (l k) p", p=P), 16),
                  (io["hg_lower"].rearrange("l (k p) -> (l k) p", p=P), 8),
                  (io["hg_norm"], 1)]
        n_b = 41
        block = s.block()

        @block.sync
        def _(sp):
            at = 0
            for src, n in rows:
                sp.dma_start(raw_a[at:at + n, :], src).then_inc(loaded, 16)
                at += n
            at = 0
            for src, n in rows_b:
                sp.dma_start(raw_b[at:at + n, :], src).then_inc(loaded, 16)
                at += n

        @block.gpsimd
        def _(g):
            g.memset(c.ident[:], 0.0).then_inc(zeroed, 1)
            g.memset(c.head_ones[:], 0.0).then_inc(zeroed, 1)
            g.memset(c.up_neg[:], -1.0).then_inc(zeroed, 1)
            g.memset(c.up_pos[:], 1.0).then_inc(zeroed, 1)
            g.memset(c.up_incl_bd[:], 1.0).then_inc(zeroed, 1)
            g.memset(c.before[:], 1.0).then_inc(zeroed, 1)
            g.memset(c.ones[:], 1.0).then_inc(zeroed, 1)
            g.memset(c.ones_bf[:], 1.0).then_inc(zeroed, 1)
            g.memset(c.chunk_start[:], 1.0).then_inc(zeroed, 1)
            g.wait_ge(zeroed, 9)
            g.affine_select(out=c.ident[:], in_=c.ident[:], compare_op=ALU.not_equal, fill=1.0, base=0,
                            pattern=[[-1, P]], channel_multiplier=1).then_inc(shaped, 1)
            for m in (c.up_neg, c.up_pos, c.before):
                g.affine_select(out=m[:], in_=m[:], compare_op=ALU.is_gt, fill=0.0, base=0,
                                pattern=[[1, P]], channel_multiplier=-1).then_inc(shaped, 1)
            g.affine_select(out=c.up_incl_bd[:], in_=c.up_incl_bd[:], compare_op=ALU.is_ge, fill=0.0, base=0,
                            pattern=[[1, P]], channel_multiplier=-1).then_inc(shaped, 1)

        @block.tensor
        def _(pe):
            pe.wait_ge(shaped, 5)
            pe.wait_ge(loaded, 16 * (len(rows) + len(rows_b)))
            pe.transpose(psum[:, 0, 0:104], raw_a[0:104, :], c.ident[0:104, 0:104]).then_inc(turned, 1)
            pe.transpose(psum[:, 1, 0:n_b], raw_b[0:n_b, :], c.ident[0:n_b, 0:n_b]).then_inc(turned, 1)

        @block.vector
        def _(v):
            v.wait_ge(shaped, 5)
            for m in (c.up_neg, c.up_pos, c.up_incl_bd):
                v.memset(m[0:HEAD, HEAD:P], 0.0)
            for lo in (0, HEAD):
                v.memset(c.head_ones[lo:lo + HEAD, lo:lo + HEAD], 1.0)
                v.tensor_copy(c.up_incl[lo:lo + HEAD, :], c.up_incl_bd[lo:lo + HEAD, lo:lo + HEAD])
            v.memset(c.chunk_start[:].rearrange("p (n t) -> p n t", t=CHUNK)[:, :, 0:1], 0.0)
            v.wait_ge(turned, 2)
            v.tensor_copy(c.rw_cols[:, 0:104], psum[:, 0, 0:104]).then_inc(shaped, 1)
            v.tensor_copy(c.norm_cols[:, 0:n_b], psum[:, 1, 0:n_b]).then_inc(shaped, 1)
            v.wait_ge(shaped, 7)
            v.tensor_scalar(c.one_less_ka[:], c.col("ka"), -1.0, 1.0, ALU.mult, ALU.add).then_inc(shaped, 1)
            v.tensor_sub(c.lower_diff[:], c.norm_cols[:, 36:40], c.norm_cols[:, 32:36]).then_inc(shaped, 1)

        @block.scalar
        def _(a):
            a.wait_ge(shaped, 9)
            a.activation(c.lb[:], c.lower_diff[:], ACT.Sigmoid).then_inc(zeroed, 1)
            a.activation(c.one_less_lb[:], c.lower_diff[:], ACT.Sigmoid, scale=-1.0).then_inc(zeroed, 1)


class Constants:
    def __init__(self, nc):
        def sb(name, shape, dt=F32):
            return nc.alloc_sbuf_tensor(name, shape, dt)
        self.ident = sb("ident", [P, P])
        self.head_ones = sb("head_ones", [P, P])
        self.ones = sb("ones", [P, P])
        self.ones_bf = sb("ones_bf", [P, P], BF16)
        self.before = sb("before", [P, P], BF16)
        self.up_neg = sb("up_neg", [P, P])
        self.up_pos = sb("up_pos", [P, P])
        self.up_incl_bd = sb("up_incl_bd", [P, P])
        self.up_incl = sb("up_incl", [P, HEAD])
        self.chunk_start = sb("chunk_start", [P, PAIRS * 2 * CHUNK])
        self.rw_cols = sb("rw_cols", [P, 104])
        self.norm_cols = sb("norm_cols", [P, 41])
        self.one_less_ka = sb("one_less_ka", [P, KT])
        self.lower_diff = sb("lower_diff", [P, HG_PAIRS])
        self.lb = sb("lb", [P, HG_PAIRS])
        self.one_less_lb = sb("one_less_lb", [P, HG_PAIRS])

    def mu(self, j):
        return self.rw_cols[:, 8 * j:8 * j + 8]

    def col(self, name):
        at = 48 + 8 * (PARAM_ROWS.index(name) - 1)
        return self.rw_cols[:, at:at + 8]

    def gain(self, which, layer):
        at = 16 * which + 8 * layer
        return self.norm_cols[:, at:at + 8]

    def hg_norm(self):
        return self.norm_cols[:, 40:41]


def norm(nc, c, name, h, gain, turned_out, col0, rows_out=None, source=None):
    with Stage(nc, name) as s:
        scaled = s.sb("scaled", [P, 2, D])
        squares = s.sb("squares", [P, 2, D])
        mean = s.sb("mean", [P, TT])
        rms = s.sb("rms", [P, TT])
        inv = s.sb("inv", [P, TT])
        psum = s.psum()
        n_groups = TT // 2
        loaded = [s.sem(f"loaded{q}") for q in range(n_groups)]
        stored = [s.sem(f"stored{b}") for b in range(2)]
        squared, rooted, mean_ready, inv_ready = (s.sem(x) for x in ("squared", "rooted", "mean_ready", "inv_ready"))
        act = s.progress("act", ["scale"], credit=2)
        pe = s.progress("pe", ["turn"], credit=2)
        dve = s.progress("dve", ["gain"], credit=2)
        block = s.block()

        @block.sync
        def _(sp):
            if source is not None:
                groups = source.rearrange("(q i p) d -> q p i d", q=n_groups, p=P)
                for q in range(n_groups):
                    sp.dma_start(h[:, 2 * q:2 * q + 2, :], groups[q]).then_inc(loaded[q], 16)
            if rows_out is not None:
                for b in range(2):
                    sp.sem_inc(stored[b], 16)
                with sp.Fori(0, TT // 2) as trip:
                    for b in range(2):
                        tile = trip * 2 + b
                        sp.wait_ge(act.sem, act.after("scale", tile))
                        sp.dma_start(rows_out[ds(tile * P, P), :], scaled[:, b, :]).then_inc(stored[b], 16)
                for b in range(2):
                    sp.wait_ge(stored[b], 16 + 16 * (TT // 2))

        @block.scalar
        def _(a):
            act.open(a)

            def square_sums(q):
                if source is not None:
                    a.wait_ge(loaded[q], 16)
                for b in range(2):
                    tile = 2 * q + b
                    if q:
                        a.wait_ge(squared, tile - 1)
                    a.activation(squares[:, b, :], h[:, tile, :], ACT.Square,
                                 accum_out=mean[:, tile:tile + 1]).then_inc(squared, 1)

            def scale(q):
                pair = slice(2 * q, 2 * q + 2)
                a.wait_ge(mean_ready, q + 1)
                a.activation(rms[:, pair], rms[:, pair], ACT.Sqrt).then_inc(rooted, 1)
                a.wait_ge(inv_ready, q + 1)
                for b in range(2):
                    tile = 2 * q + b
                    a.wait_ge(pe.sem, pe.after("turn", tile - 2))
                    if rows_out is not None:
                        a.wait_ge(stored[b], 16 * q + 16)
                    a.activation(scaled[:, b, :], h[:, tile, :], ACT.Copy,
                                 scale=inv[:, tile:tile + 1]).then_inc(act.sem, 1)

            square_sums(0)
            for q in range(1, n_groups):
                square_sums(q)
                scale(q - 1)
            scale(n_groups - 1)

        @block.tensor
        def _(t):
            pe.open(t)
            with t.Fori(0, TT // 2) as trip:
                for b in range(2):
                    tile = trip * 2 + b
                    t.wait_ge(act.sem, act.after("scale", tile))
                    t.wait_ge(dve.sem, dve.after("gain", tile - 2))
                    for k in range(KT):
                        mm = t.transpose(psum[:, 2 * b + k // 4, (k % 4) * P:(k % 4 + 1) * P],
                                         scaled[:, b, k * P:(k + 1) * P], c.ident[:])
                    mm.then_inc(pe.sem, 1)

        @block.vector
        def _(v):
            dve.open(v)

            def inverse(q):
                pair = slice(2 * q, 2 * q + 2)
                v.wait_ge(squared, 2 * q + 2)
                v.tensor_scalar(rms[:, pair], mean[:, pair], 1.0 / D, RMS_EPS, ALU.mult, ALU.add).then_inc(mean_ready, 1)
                v.wait_ge(rooted, q + 1)
                v.reciprocal(inv[:, pair], rms[:, pair]).then_inc(inv_ready, 1)

            inverse(0)
            for q in range(n_groups):
                if q + 1 < n_groups:
                    inverse(q + 1)
                for b in range(2):
                    tile = 2 * q + b
                    v.wait_ge(pe.sem, pe.after("turn", tile))
                    v.tensor_tensor(turned_out[:, :, tile * P + col0:(tile + 1) * P + col0],
                                    psum[:, 2 * b:2 * b + 2, :].rearrange("p a (k t) -> p (a k) t", t=P),
                                    spread(gain, 2, P), ALU.mult).then_inc(dve.sem, 1)


def rwkv_project(nc, io, c, u, d):
    with Stage(nc, "proj") as s:
        delta = s.sb("delta", [P, KT, T])
        mix = [s.sb(f"mix{b}", [P, KT, T]) for b in range(2)]
        rate = s.sb("rate", [P, KT, T])
        ring = [s.sb(f"ring{b}", [P, KT, 2 * P]) for b in range(2)]
        hid = s.sb("hid", [P, T])
        out = [s.sb(f"out{b}", [P, T]) for b in range(2)]
        rinv = s.sb("rinv", [P, T])
        keys = s.sb("keys", [P, T])
        down = ring[0]
        ring1 = ring[1][:].rearrange("p k e -> p (k e)")
        up = [ring1[:, 0:D], ring1[:, D:2 * D], rinv[:]]
        psum = s.psum()

        lora_in = s.sem("lora_in")
        ring_in = [s.sem(f"ring_in{b}") for b in range(2)]
        stored = [s.sem(f"stored{b}") for b in range(2)]
        kept = [s.sem(f"kept{b}") for b in range(3)]
        mixed, lora_h, lora_t = s.sem("mixed"), s.sem("lora_h"), s.sem("lora_t")
        lora_e, lora_tiles = s.sem("lora_e"), s.sem("lora_tiles")
        store_order = s.sem("store_order")
        k_pe, sum_pe = s.progress("k_pe", ["k"], credit=2), s.progress("sum_pe", ["sum"])
        k_act = s.progress("k_act", ["unscaled", "square"], credit=2)
        root_act = s.progress("root_act", ["log", "inverse"])
        k_dve = s.progress("k_dve", ["factor", "k"], credit=2)
        unit_dve = s.progress("unit_dve", ["floor", "kk", "kka"], credit=2)
        rv_pe = s.progress("rv_pe", ["tile"], credit=2)
        rv_act = s.progress("rv_act", ["copy"], credit=2)
        v_pe = s.progress("v_pe", ["turn"], credit=2)
        v_dve = s.progress("v_dve", ["copy"], credit=2)
        block = s.block()
        order = [5, 3, 4, 1, 0, 2]
        weights = [io["rw_in"][0, j].rearrange("(k p) e -> p k e", p=P) for j in (1, 0, 2)]
        n_chunks = D // (2 * P)

        squares, inverse, scaled = rinv, hid, keys
        sums = psum[:, 2:4, :].rearrange("p a t -> p (a t)")

        def kps(b):
            return psum[:, 4 * b:4 * b + 2, :].rearrange("p a t -> p (a t)")

        def unit_keys(engine, unit, scaled_part):
            scaled_part(0, 0)
            with engine.Fori(0, (KT - 2) // 2) as trip:
                for n in (1, 2):
                    tile = trip * 2 + n
                    unit(tile - 1, (n - 1) % 2)
                    scaled_part(tile, n % 2)
            unit(KT - 2, 0)
            scaled_part(KT - 1, 1)
            unit(KT - 1, 1)

        @block.sync
        def _(sp):
            sp.dma_start(down[:, :, 128:256], io["rw_g1"][0].rearrange("(k p) e -> p k e", p=P)).then_inc(lora_in, 16)
            sp.dma_start(down[:, :, 0:64], io["rw_w1"][0].rearrange("(k p) e -> p k e", p=P)).then_inc(lora_in, 16)
            sp.dma_start(down[:, :, 64:128], io["rw_a1"][0].rearrange("(k p) e -> p k e", p=P)).then_inc(lora_in, 16)
            sp.dma_start(up[0][0:64, :], io["rw_w2"][0]).then_inc(lora_in, 16)
            sp.dma_start(up[1][0:64, :], io["rw_a2"][0]).then_inc(lora_in, 16)
            sp.dma_start(up[2], io["rw_g2"][0]).then_inc(lora_in, 16)
            sp.wait_ge(lora_tiles, 3 * KT)
            for m, w in enumerate(weights):
                for q in range(n_chunks):
                    n = m * n_chunks + q
                    if n >= 2:
                        if n - 2 < n_chunks:
                            sp.wait_ge(k_pe.sem, k_pe.after("k", 2 * (n - 2) + 1))
                        else:
                            sp.wait_ge(rv_pe.sem, rv_pe.after("tile", 2 * (n - 2 - n_chunks) + 1))
                    sp.dma_start(ring[n % 2][:], w[:, :, q * 2 * P:(q + 1) * 2 * P]).then_inc(ring_in[n % 2], 16)
            with sp.Fori(0, KT // 2) as trip:
                for b in range(2):
                    tile = trip * 2 + b
                    sp.wait_ge(v_dve.sem, v_dve.after("copy", tile))
                    sp.dma_start(d.v_rows.rearrange("(i p) e -> p i e", p=P)[:, :, ds(tile * P, P)],
                                 mix[0][:, b, :].rearrange("p (i e) -> p i e", e=P)).then_inc(kept[b], 16)
            for b in range(2):
                sp.wait_ge(kept[b], 16 + 16 * KT + 16 * (KT // 2))

        @block.vector
        def _(v):
            def v_unit(tile, b):
                v.wait_ge(sum_pe.sem, sum_pe.after("sum", tile))
                v.wait_ge(unit_dve.sem, unit_dve.after("kk", tile - 1))
                v.tensor_scalar(inverse[:], sums, 1e-24, None, ALU.max).then_inc(unit_dve.sem, 1)
                v.wait_ge(root_act.sem, root_act.after("inverse", tile))
                v.tensor_mul(out[b][:], out[b][:], inverse[:]).then_inc(unit_dve.sem, 1)
                v.wait_ge(unit_dve.sem, unit_dve.after("kk", tile))
                rate_tile = rate[:, ds(tile, 1), :].rearrange("p a t -> p (a t)")
                v.tensor_mul(rate_tile, out[b][:], rate_tile).then_inc(unit_dve.sem, 1)

            def v_scaled(tile, b):
                v.wait_ge(kept[2], 16 * tile + 16)
                v.tensor_scalar(scaled[:], rate[:, ds(tile, 1), :].rearrange("p a t -> p (a t)"),
                                c.col("ka")[:, ds(tile, 1)], c.one_less_ka[:, ds(tile, 1)],
                                ALU.mult, ALU.add).then_inc(k_dve.sem, 1)
                v.wait_ge(k_act.sem, k_act.after("square", tile))
                v.wait_ge(k_dve.sem, k_dve.after("factor", tile))
                v.tensor_mul(scaled[:], scaled[:], kps(b)).then_inc(k_dve.sem, 1)

            v.memset(u[:, :, 0:1], 0.0).then_inc(mixed, 1)
            v.wait_ge(mixed, 1)
            v.tensor_sub(delta[:], u[:, :, 0:T], u[:, :, 1:T + 1]).then_inc(mixed, 1)
            v.wait_ge(mixed, 2)

            def blend(n):
                j = order[n]
                if n in (2, 3, 4):
                    v.wait_ge(lora_h, n - 1)
                if n == 5:
                    v.wait_ge(k_pe.sem, k_pe.after("k", KT - 1))
                for k in range(KT):
                    v.scalar_tensor_tensor(out=mix[n % 2][:, k, :], in0=delta[:, k, :], scalar=c.mu(j)[:, k:k + 1],
                                           in1=u[:, k, 1:T + 1], op0=ALU.mult, op1=ALU.add).then_inc(mixed, 1)

            for n in range(4):
                blend(n)
            blend(4)
            k_dve.open(v)
            unit_dve.open(v)
            v_dve.open(v)
            unit_keys(v, v_unit, v_scaled)
            blend(5)
            with v.Fori(0, KT // 2) as trip:
                for b in range(2):
                    tile = trip * 2 + b
                    v.wait_ge(v_pe.sem, v_pe.after("turn", tile))
                    v.wait_ge(kept[b], 16 * trip + 16 * KT + 16)
                    v.tensor_copy(mix[0][:, b, :], psum[:, 4 + 2 * b:6 + 2 * b, :].rearrange("p a t -> p (a t)")
                                  ).then_inc(v_dve.sem, 1)

        @block.tensor
        def _(pe):
            pe.wait_ge(lora_in, 16 * 6)

            for n, (cols, row, m) in enumerate(((slice(128, 256), 2, 128), (slice(0, 64), 0, 64), (slice(64, 128), 1, 64))):
                for k in range(KT):
                    pe.wait_ge(mixed, 2 + KT * n + k + 1)
                    for half in range(NH):
                        mm = pe.matmul(psum[0:m, half, :], down[:, k, cols], mix[n % 2][:, k, half * HALF:(half + 1) * HALF],
                                       start=(k == 0), stop=(k == KT - 1))
                mm.then_inc(lora_h, 1)
                pe.wait_ge(lora_t, n + 1)
                for tile in range(KT):
                    i = n * KT + tile
                    if i >= 3:
                        pe.wait_ge(lora_e, i - 2)
                    for half in range(NH):
                        mm = pe.matmul(psum[:, 2 + 2 * (i % 3) + half, :], up[row][0:m, tile * P:(tile + 1) * P],
                                       hid[0:m, half * HALF:(half + 1) * HALF], start=True, stop=True)
                    mm.then_inc(lora_tiles, 1)
            pe.wait_ge(lora_e, 3 * KT)

            def half_product(slot, part, src, bank, half):
                for k in range(KT):
                    mm = pe.matmul(psum[:, bank + half, :], ring[slot][:, k, part * P:(part + 1) * P],
                                   src[:, k, half * HALF:(half + 1) * HALF], start=(k == 0), stop=(k == KT - 1))
                return mm

            def product(slot, part, src, bank):
                half_product(slot, part, src, bank, 0)
                return half_product(slot, part, src, bank, 1)

            k_pe.open(pe)
            sum_pe.open(pe)
            pe.wait_ge(mixed, 2 + KT * 4)

            def head_sums(tile):
                pe.wait_ge(k_act.sem, k_act.after("square", tile))
                pe.wait_ge(unit_dve.sem, unit_dve.after("floor", tile - 1))
                for half in range(NH):
                    mm = pe.matmul(psum[:, 2 + half, :], c.head_ones[:], squares[:, half * HALF:(half + 1) * HALF],
                                   start=True, stop=True)
                mm.then_inc(sum_pe.sem, 1)

            for tile in range(KT):
                if tile % 2 == 0:
                    pe.wait_ge(ring_in[tile // 2 % 2], 16 * (tile // 4) + 16)
                if tile >= 2:
                    pe.wait_ge(k_dve.sem, k_dve.after("k", tile - 2))
                    pe.wait_ge(k_act.sem, k_act.after("square", tile - 2))
                half_product(tile // 2 % 2, tile % 2, mix[1], 4 * (tile % 2), 0)
                if tile:
                    head_sums(tile - 1)
                half_product(tile // 2 % 2, tile % 2, mix[1], 4 * (tile % 2), 1).then_inc(k_pe.sem, 1)
            head_sums(KT - 1)
            rv_pe.open(pe)
            v_pe.open(pe)
            pe.wait_ge(k_dve.sem, k_dve.after("k", KT - 1))
            pe.wait_ge(unit_dve.sem, unit_dve.after("floor", KT - 1))
            for m in range(2):
                pe.wait_ge(mixed, 2 + KT * (5 + m))
                with pe.Fori(0, KT // 4) as trip:
                    for n in range(4):
                        tile = trip * 4 + n
                        if n % 2 == 0:
                            pe.wait_ge(ring_in[n // 2], 16 * trip + 16 * (2 * (m + 1) + 1))
                        pe.wait_ge(rv_act.sem, rv_act.after("copy", tile + m * KT - 2))
                        product(n // 2, n % 2, mix[m], 2 * (n % 2)).then_inc(rv_pe.sem, 1)
                        if m == 1:
                            pe.wait_ge(rv_act.sem, rv_act.after("copy", tile + KT))
                            pe.wait_ge(v_dve.sem, v_dve.after("copy", tile - 2))
                            for k in range(TT):
                                mm = pe.transpose(psum[:, 4 + 2 * (n % 2) + k // 4, (k % 4) * P:(k % 4 + 1) * P],
                                                  out[n % 2][:, k * P:(k + 1) * P], c.ident[:])
                            mm.then_inc(v_pe.sem, 1)

        @block.scalar
        def _(a):
            def a_unit(tile, b):
                a.wait_ge(unit_dve.sem, unit_dve.after("floor", tile))
                a.activation(inverse[:], inverse[:], ACT.Ln).then_inc(root_act.sem, 1)
                a.wait_ge(root_act.sem, root_act.after("log", tile))
                a.activation(inverse[:], inverse[:], ACT.Exp, scale=-0.5).then_inc(root_act.sem, 1)
                a.wait_ge(unit_dve.sem, unit_dve.after("kk", tile))
                a.dma_start(d.cm["kk"][ds(tile * P, P), :], out[b][:]).then_inc(kept[0], 16)
                a.wait_ge(unit_dve.sem, unit_dve.after("kka", tile))
                a.wait_ge(kept[1], 16 * tile + 16)
                a.sem_inc(store_order, 1)
                a.dma_start(d.cm["kka"][ds(tile * P, P), :],
                            rate[:, ds(tile, 1), :].rearrange("p a t -> p (a t)")).then_inc(kept[1], 16)

            def a_scaled(tile, b):
                a.wait_ge(k_pe.sem, k_pe.after("k", tile))
                a.wait_ge(kept[0], 16 * tile + (16 if isinstance(tile, int) and tile == 0 else 0))
                a.activation(out[b][:], kps(b), ACT.Copy, scale=c.col("kk")[:, ds(tile, 1)]).then_inc(k_act.sem, 1)
                a.activation(squares[:], kps(b), ACT.Square, scale=c.col("kk")[:, ds(tile, 1)]).then_inc(k_act.sem, 1)
                a.wait_ge(k_dve.sem, k_dve.after("k", tile))
                a.dma_start(d.cm["k"][ds(tile * P, P), :], scaled[:]).then_inc(kept[2], 16)

            for n, (func, m) in enumerate(((ACT.Sigmoid, 128), (ACT.Tanh, 64), (ACT.Copy, 64))):
                a.wait_ge(lora_h, n + 1)
                if n:
                    a.wait_ge(lora_tiles, n * KT)
                a.activation(hid[0:m, :], psum[0:m, 0:2, :].rearrange("p a t -> p (a t)"), func).then_inc(lora_t, 1)
                for tile in range(KT):
                    i = n * KT + tile
                    pair = psum[:, 2 + 2 * (i % 3):4 + 2 * (i % 3), :].rearrange("p a t -> p (a t)")
                    a.wait_ge(lora_tiles, i + 1)
                    if n < 2 and i >= 2:
                        a.wait_ge(stored[i % 2], 16 * (i // 2))
                    if n == 0:
                        a.activation(out[i % 2][:], pair, ACT.Copy).then_inc(lora_e, 1)
                    elif n == 1:
                        a.activation(out[i % 2][:], pair, ACT.Sigmoid, bias=c.col("w0")[:, tile:tile + 1]).then_inc(lora_e, 1)
                    else:
                        a.activation(rate[:, tile, :], pair, ACT.Sigmoid, bias=c.col("a0")[:, tile:tile + 1]).then_inc(lora_e, 1)
                    if n < 2:
                        a.wait_ge(lora_e, i + 1)
                        dst = (d.cm["gate"], d.cm["decay"])[n]
                        a.dma_start(dst[tile * P:(tile + 1) * P, :], out[i % 2][:]).then_inc(stored[i % 2], 16)
            for b in range(2):
                a.wait_ge(stored[b], 16 * KT)
            k_act.open(a)
            root_act.open(a)
            for b in range(3):
                a.sem_inc(kept[b], 16)
            unit_keys(a, a_unit, a_scaled)
            for b in range(3):
                a.wait_ge(kept[b], 16 + 16 * KT)
            rv_act.open(a)
            for m, dst in enumerate((d.cm["r"], d.cm["v"])):
                with a.Fori(0, KT // 2) as trip:
                    for b in range(2):
                        tile = trip * 2 + b
                        a.wait_ge(rv_pe.sem, rv_pe.after("tile", tile + m * KT))
                        a.wait_ge(stored[b], 16 * trip + 16 * KT + 16 * m * (KT // 2))
                        if m == 1:
                            a.wait_ge(v_pe.sem, v_pe.after("turn", tile - 2))
                        a.activation(out[b][:], psum[:, 2 * b:2 * b + 2, :].rearrange("p a t -> p (a t)"),
                                     ACT.Copy).then_inc(rv_act.sem, 1)
                        a.wait_ge(rv_act.sem, rv_act.after("copy", tile + m * KT))
                        a.dma_start(dst[ds(tile * P, P), :], out[b][:]).then_inc(stored[b], 16)
            for b in range(2):
                a.wait_ge(stored[b], 16 * KT + 16 * KT)


class Scratch:

    def __init__(self, nc):
        self.pool_dma = [{name: nc.alloc_semaphore(name=f"{name}_of_layer{layer}") for name in (
            "emptied", "written", "table_in", "gathered0", "gathered1", "scattered0", "scattered1",
            "extra_gathered", "extra_scattered")} for layer in range(2)]

        def dram(name, shape, dt=F32):
            return nc.dram_tensor(name, shape, dt, kind="Internal").ap()
        self.cm = {}
        for name in ("decay", "gate", "r", "k", "kk", "kka", "v"):
            self.cm[name] = dram(f"{name}_cm", (D, T))
        self.v_rows = dram("v_rows", (T, D))
        self.rows = dram("normed_rows", (T, D))
        self.slot_table = dram("slot_table", (REGIONS * SLOTS, 1), I32)
        self.expert_rows = dram("expert_rows", (2 * T, D))


def rwkv_scan(nc, c, d, y):
    with Stage(nc, "scan") as s:
        names = ("decay", "r", "kk", "kka", "k")
        fresh = {n: s.sb(n, [P, PAIRS, 2 * CHUNK]) for n in names}
        total = s.sb("total", [P, PAIRS, 2 * CHUNK])
        shifted = s.sb("shifted", [P, PAIRS, 2 * CHUNK])
        fall = s.sb("fall", [P, PAIRS, 2 * CHUNK])
        fall1 = s.sb("fall1", [P, PAIRS, 2 * CHUNK])
        rise = s.sb("rise", [P, PAIRS, 2 * CHUNK])
        ends = s.sb("ends", [P, PAIRS, 2])
        ar = [s.sb(f"ar{b}", [P, PAIRS, 2, CHUNK]) for b in range(2)]
        a_bd = [s.sb(f"a_bd{b}", [P, PAIRS, P]) for b in range(2)]
        b_bd = [s.sb(f"b_bd{b}", [P, PAIRS, P]) for b in range(2)]
        k_bd = [s.sb(f"k_bd{b}", [P, PAIRS, P]) for b in range(2)]
        v_bd = [s.sb(f"v_bd{b}", [P, PAIRS, P]) for b in range(2)]
        x = [s.sb(f"x{b}", [P, PAIRS, P]) for b in range(2)]
        xt = [s.sb(f"xt{b}", [P, PAIRS, P]) for b in range(2)]
        pt = [s.sb(f"pt{b}", [P, PAIRS, P]) for b in range(2)]
        ak_t = s.sb("ak_t", [P, PAIRS, P])
        rb_t = s.sb("rb_t", [P, PAIRS, CHUNK])
        rk_t = s.sb("rk_t", [P, PAIRS, CHUNK])
        b_rows = s.sb("b_rows", [P, PAIRS, P])
        k_rows = s.sb("k_rows", [P, PAIRS, P])
        w_bd = s.sb("w_bd", [P, PAIRS, P])
        u_bd = s.sb("u_bd", [P, PAIRS, P])
        state = s.sb("state", [P, PAIRS, P])
        grown = s.sb("grown", [P, PAIRS, P])
        psum = s.psum()

        def banks(slot):
            return psum[:, 2 * slot:2 * slot + 2, :].rearrange("p a (m e) -> p (a m) e", e=P)

        def bank(slot, h):
            return psum[:, 2 * slot + h, :].rearrange("p (m e) -> p m e", e=P)

        arrived = s.sem("arrived")
        v_in = [s.sem(f"v_in{b}") for b in range(2)]
        ready, ready_parts = s.sem("ready"), s.sem("ready_parts")
        g_trip = s.progress("g_trip", ["shift"])
        a_trip = s.progress("a_trip", ["fall1", "rise", "fall"])
        v_trip = s.progress("v_trip", ["total"])
        v_ends = s.progress("v_ends", ["ends"])
        pool = s.progress("pool", ["A", "R"], credit=2)
        prep = s.progress("prep", ["A", "B", "K"], credit=2)

        def halves(*steps):
            return [f"{step}.{h}" for step in steps for h in range(2)]

        pe_steps = ["K.AR.0"] + halves("B.AR") + ["K.AR.1"] + halves("X0") + ["B_rows"]
        for j in range(1, LEVELS):
            pe_steps += halves(f"X{j}") + [f"XT{j}.0", f"P{j}.0", f"XT{j}.1", f"P{j}.1"] + (["K_rows"] if j == 1 else [])
        pe_steps += halves(f"X{LEVELS}") + ["W.0"] + halves(f"P{LEVELS}") + ["W.1"] + halves("U", "Y", "S")
        pe = s.progress("pe", pe_steps, credit=2)
        dve = s.progress("dve", halves("XT0") + ["rb", "P0"] +
                         sum([[f"XT{j}.0", f"P{j}.0", f"XT{j}.1", f"P{j}.1"] for j in range(1, LEVELS)], []) +
                         halves(f"P{LEVELS}") +
                         halves("U") + ["grown.0", "S.0", "grown.1", "S.1"], credit=2)
        act = s.progress("act", halves("X0") + ["B_rows"] + halves("X1") + ["K_rows"] +
                         halves(*[f"X{j}" for j in range(2, LEVELS + 1)], "W", "Y"), credit=2)
        mask = s.progress("mask", ["ak", "rk"], credit=2)
        half = [slice(0, PAIRS // 2), slice(PAIRS // 2, PAIRS)]
        block = s.block()

        def all_trips(engine, body):
            with engine.Fori(0, CHUNKS // 2 - 1) as trip:
                body(trip, False)
            body(CHUNKS // 2 - 1, True)

        @block.sync
        def _(sp):
            def load_fresh(trip):
                for n in names:
                    sp.dma_start(fresh[n][:], d.cm[n].rearrange("(m p) t -> p m t", p=P)
                                 [:, :, ds(trip * 2 * CHUNK, 2 * CHUNK)]).then_inc(arrived, 16)

            def load_v(chunk, b):
                for h in range(2):
                    sp.dma_start(v_bd[b][h * CHUNK:(h + 1) * CHUNK, :, h * HEAD:(h + 1) * HEAD],
                                 d.v_rows.rearrange("t (m e) -> t m e", e=P)
                                 [ds(chunk * CHUNK, CHUNK), :, h * HEAD:(h + 1) * HEAD]).then_inc(v_in[b], 16)

            load_fresh(0)
            sp.wait_ge(ready, 1)
            for b in range(2):
                load_v(b, b)
            with sp.Fori(0, CHUNKS // 2 - 1) as trip:
                sp.wait_ge(g_trip.sem, g_trip.after("shift", trip))
                sp.wait_ge(prep.sem, prep.after("K", trip * 2 + 1))
                sp.wait_ge(pool.sem, pool.after("R", trip * 2 + 1))
                sp.wait_ge(ready, 1)
                load_fresh(trip + 1)
                for b in range(2):
                    sp.wait_ge(pe.sem, pe.after("S.1", trip * 2 + b))
                    sp.wait_ge(ready, 1)
                    load_v(trip * 2 + 2 + b, b)

        @block.gpsimd
        def _(g):
            for z in (*a_bd, *b_bd, *k_bd, *v_bd, state):
                g.memset(z[:], 0.0).then_inc(ready_parts, 1)
            g.wait_ge(ready_parts, 9)
            g.sem_inc(ready, 1)
            g_trip.open(g)
            pool.open(g)

            def shift(trip):
                g.wait_ge(v_trip.sem, v_trip.after("total", trip))
                g.wait_ge(a_trip.sem, a_trip.after("fall1", trip - 1))
                g.tensor_sub(shifted[:], total[:], fresh["decay"][:]).then_inc(g_trip.sem, 1)

            def decayed(trip, b):
                chunk = trip * 2 + b
                at = slice(b * CHUNK, (b + 1) * CHUNK)
                if b == 0:
                    g.wait_ge(a_trip.sem, a_trip.after("fall1", trip))
                g.wait_ge(pe.sem, pe.after("Y.1", chunk - 2))
                g.tensor_mul(ar[b][:, :, 0, :], fresh["kk"][:, :, at], fall1[:, :, at]).then_inc(pool.sem, 1)
                if b == 0:
                    g.wait_ge(a_trip.sem, a_trip.after("fall", trip))
                g.tensor_mul(ar[b][:, :, 1, :], fresh["r"][:, :, at], fall[:, :, at]).then_inc(pool.sem, 1)

            def body(trip, last):
                decayed(trip, 1)
                if not last:
                    shift(trip + 1)
                    decayed(trip + 1, 0)

            shift(0)
            decayed(0, 0)
            all_trips(g, body)

        @block.vector
        def _(v):
            v.wait_ge(ready, 1)
            v_trip.open(v)
            v_ends.open(v)
            prep.open(v)
            dve.open(v)
            mask.open(v)

            def add_up(trip):
                v.wait_ge(arrived, 80 * trip + 80)
                v.wait_ge(g_trip.sem, g_trip.after("shift", trip - 1))
                v.wait_ge(a_trip.sem, a_trip.after("fall", trip - 1))
                v.tensor_tensor_scan(total[:].rearrange("p m t -> p (m t)"), c.chunk_start[:],
                                     fresh["decay"][:].rearrange("p m t -> p (m t)"), 0.0,
                                     ALU.mult, ALU.add).then_inc(v_trip.sem, 1)

            def diagonal(trip, b, step):
                chunk = trip * 2 + b
                at = slice(b * CHUNK, (b + 1) * CHUNK)
                dst, src, scale = {"A": (a_bd, "kk", fall1), "B": (b_bd, "kka", rise), "K": (k_bd, "k", rise)}[step]
                if b == 0 and step != "K":
                    v.wait_ge(a_trip.sem, a_trip.after("fall1" if step == "A" else "rise", trip))
                if step == "A":
                    v.wait_ge(pe.sem, pe.after("W.1", chunk - 2))
                for h in range(2):
                    rows = slice(h * HEAD, (h + 1) * HEAD)
                    mul = v.tensor_mul(dst[b][rows, :, rows], fresh[src][rows, :, at], scale[rows, :, at])
                mul.then_inc(prep.sem, 1)

            def first_powers(chunk):
                for h in range(2):
                    v.wait_ge(pe.sem, pe.after(f"B.AR.{h}", chunk))
                    v.tensor_tensor(xt[0][:, half[h], :].rearrange("p m (h t) -> p m h t", h=2),
                                    spread(bank(1, h)[:, :, 0:CHUNK], 2, 2),
                                    spread(c.up_neg[:].rearrange("p (h t) -> p h t", h=2), 1, PAIRS // 2),
                                    ALU.mult).then_inc(dve.sem, 1)
                v.tensor_tensor(rb_t[:], banks(1)[:, :, CHUNK:P], spread(c.up_incl[:], 1, PAIRS),
                                ALU.mult).then_inc(dve.sem, 1)
                v.wait_ge(dve.sem, dve.after("XT0.1", chunk))
                v.tensor_tensor(pt[0][:], xt[0][:], spread(c.ident[:], 1, PAIRS), ALU.add).then_inc(dve.sem, 1)
                v.wait_ge(pe.sem, pe.after("K.AR.1", chunk))
                v.tensor_tensor(ak_t[:].rearrange("p m (h t) -> p m h t", h=2),
                                spread(banks(3)[:, :, 0:CHUNK], 2, 2),
                                spread(c.up_pos[:].rearrange("p (h t) -> p h t", h=2), 1, PAIRS),
                                ALU.mult).then_inc(mask.sem, 1)
                v.tensor_tensor(rk_t[:], banks(3)[:, :, CHUNK:P], spread(c.up_incl[:], 1, PAIRS),
                                ALU.mult).then_inc(mask.sem, 1)

            def body(trip, last):
                v.wait_ge(dve.sem, dve.after("S.1", trip * 2 - 1))
                v.wait_ge(a_trip.sem, a_trip.after("fall", trip))
                v.tensor_copy(ends[:], fall[:].rearrange("p m (b t) -> p m b t", b=2)
                              [:, :, :, CHUNK - 1]).then_inc(v_ends.sem, 1)
                for b in range(2):
                    chunk = trip * 2 + b
                    first_powers(chunk)
                    for j in range(1, LEVELS + 1):
                        for h in range(2):
                            if j < LEVELS:
                                v.wait_ge(pe.sem, pe.after(f"XT{j}.{h}", chunk))
                                v.tensor_copy(xt[j % 2][:, half[h], :], bank(1, h)).then_inc(dve.sem, 1)
                            v.wait_ge(pe.sem, pe.after(f"P{j}.{h}", chunk))
                            v.tensor_add(pt[j % 2][:, half[h], :], pt[(j - 1) % 2][:, half[h], :],
                                         bank(2, h)).then_inc(dve.sem, 1)
                        if b == 0 or not last:
                            next_trip, next_b = (trip, 1) if b == 0 else (trip + 1, 0)
                            if j == 1 and b == 1:
                                add_up(next_trip)
                            if j == 3:
                                diagonal(next_trip, next_b, "A")
                            if j == 4:
                                diagonal(next_trip, next_b, "B")
                                diagonal(next_trip, next_b, "K")
                    for h in range(2):
                        v.wait_ge(pe.sem, pe.after(f"U.{h}", chunk))
                        v.tensor_copy(u_bd[:, half[h], :], bank(2, h)).then_inc(dve.sem, 1)
                    for h in range(2):
                        v.wait_ge(pe.sem, pe.after(f"S.{h}", chunk))
                        v.tensor_add(grown[:, half[h], :], state[:, half[h], :], bank(1, h)).then_inc(dve.sem, 1)
                        v.wait_ge(dve.sem, dve.after(f"grown.{h}", chunk))
                        if h == 0:
                            v.wait_ge(v_ends.sem, v_ends.after("ends", trip))
                        v.tensor_tensor(state[:, half[h], :], grown[:, half[h], :],
                                        spread(ends[:, half[h], b], 2, P), ALU.mult).then_inc(dve.sem, 1)

            add_up(0)
            for step in ("A", "B", "K"):
                diagonal(0, 0, step)
            all_trips(v, body)

        @block.scalar
        def _(a):
            a_trip.open(a)
            act.open(a)

            def decays(trip, step):
                if step == "fall1":
                    a.wait_ge(g_trip.sem, g_trip.after("shift", trip))
                    a.activation(fall1[:], shifted[:], ACT.Exp, scale=-DECAY).then_inc(a_trip.sem, 1)
                elif step == "rise":
                    a.activation(rise[:], total[:], ACT.Exp, scale=DECAY).then_inc(a_trip.sem, 1)
                else:
                    a.wait_ge(v_ends.sem, v_ends.after("ends", trip - 1))
                    a.wait_ge(pool.sem, pool.after("R", trip * 2 - 1))
                    a.activation(fall[:], total[:], ACT.Exp, scale=-DECAY).then_inc(a_trip.sem, 1)

            def body(trip, last):
                for b in range(2):
                    chunk = trip * 2 + b
                    for j in range(LEVELS + 1):
                        for h in range(2):
                            a.wait_ge(pe.sem, pe.after(f"X{j}.{h}", chunk))
                            a.activation(x[j % 2][:, half[h], :], bank(0, h), ACT.Copy).then_inc(act.sem, 1)
                        if j == 0:
                            a.wait_ge(pe.sem, pe.after("B_rows", chunk))
                            a.activation(b_rows[:], banks(2), ACT.Copy).then_inc(act.sem, 1)
                        if j == 1:
                            a.wait_ge(pe.sem, pe.after("K_rows", chunk))
                            a.activation(k_rows[:], banks(3), ACT.Copy).then_inc(act.sem, 1)
                        if b == 1 and not last and j in (2, 3, 4):
                            decays(trip + 1, ("fall1", "rise", "fall")[j - 2])
                    for h in range(2):
                        a.wait_ge(pe.sem, pe.after(f"W.{h}", chunk))
                        a.activation(w_bd[:, half[h], :], bank(3, h), ACT.Copy, scale=-1.0).then_inc(act.sem, 1)
                    for h in range(2):
                        a.wait_ge(pe.sem, pe.after(f"Y.{h}", chunk))
                        a.activation(y[:, half[h], ds(chunk * CHUNK, CHUNK)],
                                     psum[:, h, 0:PAIRS // 2 * CHUNK].rearrange("p (m t) -> p m t", t=CHUNK),
                                     ACT.Copy).then_inc(act.sem, 1)

            for step in ("fall1", "rise", "fall"):
                decays(0, step)
            all_trips(a, body)

        @block.tensor
        def _(t):
            def each_pair(slot, h, *products):
                for m in range(half[h].start, half[h].stop):
                    for n, (lhs, rhs) in enumerate(products):
                        mm = t.matmul(banks(slot)[:, m, :], lhs[:, m, :], rhs[:, m, :],
                                      start=(n == 0), stop=(n == len(products) - 1))
                mm.then_inc(pe.sem, 1)

            def turned(slot, pairs, src):
                for m in range(pairs.start, pairs.stop):
                    mm = t.transpose(banks(slot)[:, m, :], src[:, m, :], c.ident[:])
                mm.then_inc(pe.sem, 1)

            pe.open(t)

            def body(trip, last):
                for b in range(2):
                    chunk = trip * 2 + b
                    ar_b = ar[b][:].rearrange("p m a t -> p m (a t)")
                    t.wait_ge(prep.sem, prep.after("K", chunk))
                    t.wait_ge(pool.sem, pool.after("R", chunk))
                    t.wait_ge(act.sem, act.after("Y.1", chunk - 1))
                    each_pair(3, 0, (k_bd[b], ar_b))
                    for h in range(2):
                        t.wait_ge(dve.sem, dve.after(f"grown.{h}", chunk - 1))
                        each_pair(1, h, (b_bd[b], ar_b))
                    each_pair(3, 1, (k_bd[b], ar_b))
                    for h in range(2):
                        t.wait_ge(dve.sem, dve.after(f"XT0.{h}", chunk))
                        turned(0, half[h], xt[0])
                    turned(2, slice(0, PAIRS), b_bd[b])
                    for j in range(1, LEVELS + 1):
                        old, new = (j - 1) % 2, j % 2
                        for h in range(2):
                            t.wait_ge(dve.sem, dve.after("rb" if j == 1 else f"XT{j - 1}.{h}", chunk))
                            if j == 1:
                                t.wait_ge(act.sem, act.after(f"X0.{h}", chunk))
                            each_pair(0, h, (xt[old], x[old]))
                        if j == LEVELS:
                            t.wait_ge(dve.sem, dve.after("S.1", chunk - 1))
                            t.wait_ge(act.sem, act.after("K_rows", chunk))
                            t.wait_ge(v_in[b], 32 * trip + 32)
                            each_pair(3, 0, (a_bd[b], state), (ak_t, v_bd[b]))
                        for h in range(2):
                            t.wait_ge(act.sem, act.after(f"X{j}.{h}", chunk))
                            if j < LEVELS:
                                turned(1, half[h], x[new])
                            t.wait_ge(dve.sem, dve.after("P0" if j == 1 else f"P{j - 1}.{h}", chunk))
                            each_pair(2, h, (x[new], pt[old]))
                        if j == 1:
                            t.wait_ge(mask.sem, mask.after("rk", chunk))
                            turned(3, slice(0, PAIRS), k_bd[b])
                    each_pair(3, 1, (a_bd[b], state), (ak_t, v_bd[b]))
                    for h in range(2):
                        t.wait_ge(act.sem, act.after(f"W.{h}", chunk))
                        t.wait_ge(dve.sem, dve.after(f"P{LEVELS}.{h}", chunk))
                        each_pair(2, h, (pt[LEVELS % 2], w_bd))
                    for h in range(2):
                        t.wait_ge(dve.sem, dve.after(f"U.{h}", chunk))
                        for m in range(half[h].start, half[h].stop):
                            at = (m - half[h].start) * CHUNK
                            for n, (lhs, rhs) in enumerate(((state, ar_b[:, m, CHUNK:P]), (v_bd[b], rk_t[:, m, :]),
                                                            (u_bd, rb_t[:, m, :]))):
                                mm = t.matmul(psum[:, h, at:at + CHUNK], lhs[:, m, :], rhs,
                                              start=(n == 0), stop=(n == 2))
                        mm.then_inc(pe.sem, 1)
                    for h in range(2):
                        each_pair(1, h, (k_rows, v_bd[b]), (b_rows, u_bd))

            all_trips(t, body)


class OutWeights:

    def __init__(self, s, w_out):
        self.w = s.sb("w", [P, KT, D])
        self.arrived = [s.sem(f"w_in{a}") for a in range(NH)]
        self.source = w_out.rearrange("(k p) e -> p k e", p=P)

    def load(self, engine):
        for a in range(NH):
            engine.dma_start(self.w[:, :, a * HALF:(a + 1) * HALF],
                             self.source[:, :, a * HALF:(a + 1) * HALF]).then_inc(self.arrived[a], 16)


def staggered(engine, ahead, early=None, late=None):
    def turn(tile, b, last=False):
        if early is not None:
            early(tile, b)
        if not last:
            ahead(tile + 1, 1 - b)
        if late is not None:
            late(tile, b)

    ahead(0, 0)
    with engine.Fori(0, KT // 2 - 1) as trip:
        for b in range(2):
            turn(trip * 2 + b, b)
    turn(KT - 2, 0)
    turn(KT - 1, 1, last=True)


def rwkv_output(nc, io, c, d, y, weights):
    with Stage(nc, "gn") as s:
        r, k, v_, gate = ([s.sb(f"{n}{b}", [P, T]) for b in range(2)] for n in ("r", "k", "v", "gate"))
        squares = [s.sb(f"squares{b}", [P, T]) for b in range(2)]
        inv = [s.sb(f"inv{b}", [P, T]) for b in range(2)]
        psum = s.psum()
        rk_in = [s.sem(f"rk_in{b}") for b in range(2)]
        v_gate_in = [s.sem(f"v_gate_in{b}") for b in range(2)]
        opened, between = s.sem("opened"), s.sem("between")
        pe1 = s.progress("pe1", ["sum", "bonus"], credit=2)
        dve1 = s.progress("dve1", ["rk", "centered"], credit=2)
        act1 = s.progress("act1", ["square"], credit=2)
        pe2 = s.progress("pe2", ["squares"], credit=2)
        dve2 = s.progress("dve2", ["variance", "bonus", "unit"], credit=2)
        act2 = s.progress("act2", ["ln", "inverse", "affine"], credit=2)
        pool = s.progress("pool", ["add", "gate"], credit=2)
        block = s.block()

        def flat(bank):
            return psum[:, bank:bank + 2, :].rearrange("p a t -> p (a t)")

        @block.sync
        def _(sp):
            def load_rk(tile, b):
                sp.wait_ge(pe1.sem, pe1.after("bonus", tile - 2))
                sp.wait_ge(opened, 1)
                for buf, name in ((r, "r"), (k, "k")):
                    sp.dma_start(buf[b][:], d.cm[name][ds(tile * P, P), :]).then_inc(rk_in[b], 16)

            def load_v_gate(tile, b):
                sp.wait_ge(pool.sem, pool.after("gate", tile - 2))
                sp.wait_ge(opened, 1)
                for buf, name in ((v_, "v"), (gate, "gate")):
                    sp.dma_start(buf[b][:], d.cm[name][ds(tile * P, P), :]).then_inc(v_gate_in[b], 16)

            staggered(sp, load_rk, late=load_v_gate)

        @block.tensor
        def _(t):
            pe1.open(t)
            pe2.open(t)

            def head_sum(bank, src):
                for half in range(NH):
                    mm = t.matmul(psum[:, bank + half, :], c.head_ones[:], src(half * HALF), start=True, stop=True)
                return mm

            def sums(tile, b):
                t.wait_ge(dve1.sem, dve1.after("centered", tile - 1))
                head_sum(0, lambda at: y[:, tile, at:at + HALF]).then_inc(pe1.sem, 1)
                t.wait_ge(dve1.sem, dve1.after("rk", tile))
                t.wait_ge(dve2.sem, dve2.after("bonus", tile - 2))
                head_sum(4 + 2 * b, lambda at: r[b][:, at:at + HALF]).then_inc(pe1.sem, 1)

            def square_sums(tile, b):
                t.wait_ge(act1.sem, act1.after("square", tile))
                t.wait_ge(dve2.sem, dve2.after("variance", tile - 1))
                head_sum(2, lambda at: squares[b][:, at:at + HALF]).then_inc(pe2.sem, 1)

            staggered(t, sums, early=square_sums)

        @block.vector
        def _(v):
            v.sem_inc(opened, 1)
            dve1.open(v)
            dve2.open(v)

            def center(tile, b):
                v.wait_ge(rk_in[b], tile * 16 + (32 - 16 * b))
                v.scalar_tensor_tensor(out=r[b][:], in0=r[b][:], scalar=c.col("rk")[:, ds(tile, 1)], in1=k[b][:],
                                       op0=ALU.mult, op1=ALU.mult).then_inc(dve1.sem, 1)
                v.wait_ge(pe1.sem, pe1.after("sum", tile))
                v.scalar_tensor_tensor(out=y[:, tile, :], in0=flat(0), scalar=-1.0 / HEAD, in1=y[:, tile, :],
                                       op0=ALU.mult, op1=ALU.add).then_inc(dve1.sem, 1)

            def variance(tile, b):
                v.wait_ge(pe2.sem, pe2.after("squares", tile))
                v.wait_ge(act2.sem, act2.after("affine", tile - 2))
                v.tensor_scalar(inv[b][:], flat(2), 1.0 / HEAD, GN_EPS, ALU.mult, ALU.add).then_inc(dve2.sem, 1)

            def scale(tile, b):
                v.wait_ge(pe1.sem, pe1.after("bonus", tile))
                v.wait_ge(v_gate_in[b], tile * 16 + (32 - 16 * b))
                v.tensor_mul(v_[b][:], v_[b][:], flat(4 + 2 * b)).then_inc(dve2.sem, 1)
                v.wait_ge(act2.sem, act2.after("inverse", tile))
                v.tensor_mul(inv[b][:], inv[b][:], y[:, tile, :]).then_inc(dve2.sem, 1)

            staggered(v, center, variance, scale)

        @block.scalar
        def _(a):
            a.preload_act_table_set("natural_log_exp_and_others")
            weights.load(a)
            act1.open(a)
            act2.open(a)

            def square(tile, b):
                a.wait_ge(dve1.sem, dve1.after("centered", tile))
                a.wait_ge(pe2.sem, pe2.after("squares", tile - 2))
                a.wait_ge(act2.sem, act2.after("affine", tile - 2))
                a.activation(squares[b][:], y[:, tile, :], ACT.Square).then_inc(act1.sem, 1)

            def invert(tile, b):
                a.wait_ge(dve2.sem, dve2.after("variance", tile))
                a.activation(inv[b][:], inv[b][:], ACT.Ln).then_inc(act2.sem, 1)
                a.wait_ge(act2.sem, act2.after("ln", tile))
                a.activation(inv[b][:], inv[b][:], ACT.Exp, scale=-0.5).then_inc(act2.sem, 1)

            def affine(tile, b):
                a.wait_ge(dve2.sem, dve2.after("unit", tile))
                a.activation(y[:, tile, :], inv[b][:], ACT.Identity, bias=c.col("ln_b")[:, ds(tile, 1)],
                             scale=c.col("ln_w")[:, ds(tile, 1)]).then_inc(act2.sem, 1)

            staggered(a, square, invert, affine)

        @block.gpsimd
        def _(g):
            pool.open(g)
            with g.Fori(0, PAIRS // 2) as trip:
                for b in range(2):
                    tile = trip * 2 + b
                    g.wait_ge(act2.sem, act2.after("affine", tile))
                    g.wait_ge(dve2.sem, dve2.after("bonus", tile))
                    g.wait_ge(opened, 1)
                    g.tensor_add(y[:, tile, :], y[:, tile, :], v_[b][:]).then_inc(pool.sem, 1)
                    g.wait_ge(pool.sem, pool.after("add", tile))
                    g.sem_inc(between, 1)
                    g.tensor_mul(y[:, tile, :], y[:, tile, :], gate[b][:]).then_inc(pool.sem, 1)


def project_out(nc, name, weights, mixed, h, source=None):
    with Stage(nc, name) as s:
        psum = s.psum()
        w, w_in = weights.w, weights.arrived
        h_in, product, added = s.sem("h_in"), s.sem("product"), s.sem("added")
        block = s.block()

        if source is not None:
            @block.sync
            def _(sp):
                sp.dma_start(h[:], source.rearrange("(i p) e -> p i e", p=P)).then_inc(h_in, 16)

        @block.tensor
        def _(t):
            for i in range(TT):
                if i >= 4:
                    t.wait_ge(added, i - 3)
                for a in range(NH):
                    if i == 0:
                        t.wait_ge(w_in[a], 16)
                    for k in range(KT):
                        mm = t.matmul(psum[:, 2 * (i % 4) + a, :], mixed[:, k, i * P:(i + 1) * P],
                                      w[:, k, a * HALF:(a + 1) * HALF], start=(k == 0), stop=(k == KT - 1))
                mm.then_inc(product, 1)

        @block.vector
        def _(v):
            if source is not None:
                v.wait_ge(h_in, 16)
            for i in range(TT):
                v.wait_ge(product, i + 1)
                v.tensor_add(h[:, i, :], h[:, i, :], psum[:, 2 * (i % 4):2 * (i % 4) + 2, :].rearrange("p a t -> p (a t)")
                             ).then_inc(added, 1)


def route(nc, io, c, d, r, weights, layer, name, u):
    with Stage(nc, name) as s:
        n_out = GROUPS + EXPERTS
        w = s.sb("w", [P, KT, n_out])
        bias = s.sb("bias", [P, n_out])
        logits_t = s.sb("logits_t", [n_out, T])
        logits = s.sb("logits", [P, TT, n_out])
        lg = logits[:, :, 0:GROUPS]
        le = logits[:, :, GROUPS:n_out]
        iota = s.sb("iota", [P, EXPERTS])
        expert_base = s.sb("expert_base", [P, EXPERTS])
        limits = s.sb("limits", [P, TT - 1])
        blocks = s.sb("blocks", [1, EXTRA])
        assignment = s.sb("assignment", [P, TT, 2], I32)
        top = s.sb("top", [P, TT])
        masked = s.sb("masked", [P, TT, EXPERTS])
        group_hot = s.sb("group_hot", [P, TT, GROUPS])
        group_exp = s.sb("group_exp", [P, TT, GROUPS])
        first = s.sb("first", [P, TT, EXPERTS])
        second = s.sb("second", [P, TT, EXPERTS])
        cand = s.sb("cand", [P, TT, EXPERTS])
        least = s.sb("least", [P, TT])
        top1 = s.sb("top1", [P, TT])
        top2 = s.sb("top2", [P, TT])
        p_group = s.sb("p_group", [P, TT])
        ratio = s.sb("ratio", [P, TT])
        share = s.sb("share", [P, TT])
        chosen = s.sb("chosen", [P, TT, EXPERTS], BF16)
        count = s.sb("count", [P, EXPERTS])
        over = s.sb("over", [P, EXPERTS, TT - 1])
        extra = s.sb("extra", [P, EXPERTS])
        extra_end = s.sb("extra_end", [P, EXPERTS])
        extra_base = s.sb("extra_base", [P, EXPERTS])
        slot = s.sb("slot", [P, TT, EXPERTS])
        picked = s.sb("picked", [P, TT, 2])
        slot_of = s.sb("slot_of", [P, TT, 2], I32)
        passed = s.sb("passed", [1, EXTRA, EXPERTS])
        block_expert = s.sb("block_expert", [1, EXTRA + 1])
        empty = s.sb("empty", [REGIONS, P], I32)
        table = s.sb("table", [REGIONS, P], I32)
        table_f = s.sb("table_f", [REGIONS, P])
        psum = s.psum()
        loaded, made, product, step, soft = (s.sem(x) for x in ("loaded", "made", "product", "step", "soft"))
        emptied, written, table_in = d.pool_dma[layer]["emptied"], d.pool_dma[layer]["written"], d.pool_dma[layer]["table_in"]
        step_act, chosen_ready, slots_ready, table_ready = (
            s.sem(x) for x in ("step_act", "chosen_ready", "slots_ready", "table_ready"))
        logits_made, logits_copied = s.sem("logits_made"), s.sem("logits_copied")
        block = s.block()

        @block.sync
        def _(sp):
            sp.dma_start(w[:, :, 0:GROUPS], io["moe_rg"][layer].rearrange("(k p) e -> p k e", p=P)).then_inc(loaded, 16)
            sp.dma_start(w[:, :, GROUPS:n_out], io["moe_re"][layer].rearrange("(k p) e -> p k e", p=P)).then_inc(loaded, 16)
            sp.dma_start(bias[:, 0:GROUPS], io["moe_rg_b"][layer:layer + 1, :].partition_broadcast(P)
                         .rearrange("p a e -> p (a e)")).then_inc(loaded, 16)
            sp.dma_start(bias[:, GROUPS:n_out], io["moe_re_b"][layer].rearrange("(a g) e -> a (g e)", a=1)
                         .partition_broadcast(P).rearrange("p a e -> p (a e)")).then_inc(loaded, 16)
            weights.load_first(sp)

        @block.gpsimd
        def _(g):
            g.memset(empty[:], NO_TOKEN).then_inc(made, 1)
            g.iota(iota[:], [[1, EXPERTS]], base=0, channel_multiplier=0,
                   allow_small_or_imprecise_dtypes=True).then_inc(made, 1)
            g.iota(expert_base[:], [[SLOTS, EXPERTS]], base=0, channel_multiplier=0,
                   allow_small_or_imprecise_dtypes=True).then_inc(made, 1)
            g.iota(limits[:], [[SLOTS, TT - 1]], base=SLOTS, channel_multiplier=0,
                   allow_small_or_imprecise_dtypes=True).then_inc(made, 1)
            g.iota(blocks[:], [[1, EXTRA]], base=0, channel_multiplier=0,
                   allow_small_or_imprecise_dtypes=True).then_inc(made, 1)
            g.iota(assignment[:], [[2 * P, TT], [1, 2]], base=0, channel_multiplier=2).then_inc(made, 1)
            g.wait_ge(made, 6)
            g.dma_start(d.slot_table.rearrange("(r p) o -> r (p o)", p=P), empty[:]).then_inc(emptied, 16)
            g.wait_ge(emptied, 16)
            g.wait_ge(slots_ready, 1)
            for i in range(TT):
                for choice in range(2):
                    g.indirect_dma_start(
                        out=d.slot_table, out_offset=bass.IndirectOffsetOnAxis(ap=slot_of[:, i, choice:choice + 1], axis=0),
                        in_=assignment[:, i, choice:choice + 1], in_offset=None).then_inc(written, 16)
            g.wait_ge(written, 16 * 2 * TT)
            g.dma_start(table[:], d.slot_table.rearrange("(r p) o -> r (p o)", p=P)).then_inc(table_in, 16)

        @block.tensor
        def _(t):
            t.wait_ge(loaded, 64)
            for half in range(NH):
                for k in range(KT):
                    mm = t.matmul(psum[0:n_out, 4 + half, :], w[:, k, :], u[:, k, half * HALF:(half + 1) * HALF],
                                  start=(k == 0), stop=(k == KT - 1))
                mm.then_inc(logits_made, 1)
            for half in range(NH):
                t.wait_ge(logits_copied, half + 1)
                for i in range(half * TT // 2, (half + 1) * TT // 2):
                    mm = t.transpose(psum[:, 0, i * 64:i * 64 + n_out], logits_t[:, i * P:(i + 1) * P],
                                     c.ident[0:n_out, 0:n_out])
            mm.then_inc(product, 1)
            t.wait_ge(chosen_ready, 1)
            for i in range(TT):
                for j in range(i):
                    t.matmul(psum[:, 1, i * EXPERTS:(i + 1) * EXPERTS], c.ones_bf[:], chosen[:, j, :],
                             start=(j == 0), stop=False)
                t.matmul(psum[:, 1, i * EXPERTS:(i + 1) * EXPERTS], c.before[:], chosen[:, i, :],
                         start=(i == 0), stop=True)
            for j in range(TT):
                mm = t.matmul(psum[:, 2, 0:EXPERTS], c.ones_bf[:], chosen[:, j, :], start=(j == 0), stop=(j == TT - 1))
            mm.then_inc(product, 1)
            t.wait_ge(table_ready, 1)
            t.transpose(psum[:, 3, 0:REGIONS], table_f[:], c.ident[0:REGIONS, 0:REGIONS]).then_inc(product, 1)

        @block.scalar
        def _(a):
            for half in range(NH):
                a.wait_ge(logits_made, half + 1)
                a.activation(logits_t[:, half * HALF:(half + 1) * HALF], psum[0:n_out, 4 + half, :],
                             ACT.Copy).then_inc(logits_copied, 1)
            a.wait_ge(soft, 1)
            a.activation(group_exp[:], group_exp[:], ACT.Exp).then_inc(step_act, 1)
            a.wait_ge(soft, 2)
            a.activation(ratio[:], ratio[:], ACT.Exp).then_inc(step_act, 1)

        @block.vector
        def _(v):
            done = [0]

            def after(ins):
                done[0] += 1
                ins.then_inc(step, 1)
                v.wait_ge(step, done[0])

            def one_hot(out, values, best, n):
                after(v.tensor_reduce(best[:], values, AX_X, ALU.max))
                after(v.tensor_tensor(cand[:, :, 0:n], values, spread(best[:], 2, n), ALU.is_ge))
                after(v.scalar_tensor_tensor(out=cand[:, :, 0:n], in0=cand[:, :, 0:n], scalar=-64.0,
                                             in1=spread(iota[:, 0:n], 1, TT), op0=ALU.mult, op1=ALU.add))
                after(v.tensor_reduce(least[:], cand[:, :, 0:n], AX_X, ALU.min))
                after(v.tensor_tensor(out, cand[:, :, 0:n], spread(least[:], 2, n), ALU.is_equal))

            v.wait_ge(product, 1)
            v.wait_ge(made, 6)
            after(v.tensor_tensor(logits[:], psum[:, 0, :].rearrange("p (i e) -> p i e", e=64)[:, :, 0:n_out],
                                  spread(bias[:], 1, TT), ALU.add))
            one_hot(group_hot[:], lg, top, GROUPS)
            v.tensor_tensor(group_exp[:], lg, spread(top[:], 2, GROUPS), ALU.subtract).then_inc(soft, 1)
            after(v.tensor_scalar(masked[:].rearrange("p i (g e) -> p i g e", e=PER_GROUP),
                                  spread(group_hot[:], 3, PER_GROUP), 3e38, -3e38, ALU.mult, ALU.add))
            after(v.tensor_tensor(second[:].rearrange("p i (g e) -> p i g e", e=PER_GROUP),
                                  le.rearrange("p i (g e) -> p i g e", e=PER_GROUP),
                                  spread(group_hot[:], 3, PER_GROUP), ALU.mult))
            after(v.tensor_tensor(masked[:], masked[:], second[:], ALU.add))
            one_hot(first[:], masked[:], top1, EXPERTS)
            after(v.scalar_tensor_tensor(out=masked[:], in0=first[:], scalar=-3e38, in1=masked[:],
                                         op0=ALU.mult, op1=ALU.add))
            one_hot(second[:], masked[:], top2, EXPERTS)
            v.tensor_sub(ratio[:], top2[:], top1[:]).then_inc(soft, 1)
            after(v.tensor_add(cand[:], first[:], second[:]))
            after(v.tensor_copy(chosen[:], cand[:]))
            v.sem_inc(chosen_ready, 1)
            v.wait_ge(product, 2)
            after(v.tensor_copy(count[:], psum[:, 2, 0:EXPERTS]))
            after(v.tensor_tensor(over[:], spread(count[:], 2, TT - 1), spread(limits[:], 1, EXPERTS), ALU.is_gt))
            after(v.tensor_reduce(extra[:], over[:], AX_X, ALU.add))
            after(v.tensor_tensor_scan(extra_end[:], c.ones[:, 0:EXPERTS], extra[:], 0.0, ALU.mult, ALU.add))
            after(v.tensor_sub(extra_base[:], extra_end[:], extra[:]))
            after(v.tensor_scalar(extra_base[:], extra_base[:], float(SLOTS), float(SLOTS * (EXPERTS - 1)), ALU.mult, ALU.add))
            after(v.tensor_sub(extra_base[:], extra_base[:], expert_base[:]))
            rank = psum[:, 1, 0:TT * EXPERTS].rearrange("p (i e) -> p i e", e=EXPERTS)
            after(v.tensor_scalar(slot[:], rank, float(SLOTS), None, ALU.is_ge))
            after(v.tensor_tensor(slot[:], slot[:], spread(extra_base[:], 1, TT), ALU.mult))
            after(v.tensor_tensor(slot[:], slot[:], rank, ALU.add))
            after(v.tensor_tensor(slot[:], slot[:], spread(expert_base[:], 1, TT), ALU.add))
            for choice, hot in enumerate((first, second)):
                after(v.tensor_mul(cand[:], slot[:], hot[:]))
                after(v.tensor_reduce(picked[:, :, choice], cand[:], AX_X, ALU.add))
            after(v.tensor_copy(slot_of[:], picked[:]))
            v.sem_inc(slots_ready, 1)
            v.wait_ge(step_act, 2)
            after(v.tensor_reduce(p_group[:], group_exp[:], AX_X, ALU.add))
            after(v.tensor_scalar(share[:], ratio[:], 1.0, None, ALU.add))
            after(v.tensor_mul(share[:], share[:], p_group[:]))
            after(v.reciprocal(r.gates[:, :, 0], share[:]))
            after(v.tensor_mul(r.gates[:, :, 1], r.gates[:, :, 0], ratio[:]))
            after(v.tensor_tensor(passed[:], spread(extra_end[0:1, :], 1, EXTRA), spread(blocks[:], 2, EXPERTS), ALU.is_le))
            after(v.tensor_reduce(block_expert[:, 0:EXTRA], passed[:], AX_X, ALU.add))
            after(v.tensor_scalar(block_expert[:, 0:EXTRA], block_expert[:, 0:EXTRA], float(EXPERTS - 1), None, ALU.min))
            after(v.tensor_copy(block_expert[:, EXTRA:EXTRA + 1], extra_end[0:1, EXPERTS - 1:EXPERTS]))
            after(v.tensor_copy(r.extra_blocks[:], block_expert[:]))
            v.wait_ge(table_in, 16)
            after(v.tensor_copy(table_f[:], table[:]))
            v.sem_inc(table_ready, 1)
            v.wait_ge(product, 3)
            after(v.tensor_copy(r.scatter_row[:], psum[:, 3, 0:REGIONS]))
            after(v.tensor_scalar(r.gather_row[:], r.scatter_row[:], 1, None, ALU.arith_shift_right))


class Routing:

    def __init__(self, s):
        self.gates = s.sb("gates", [P, TT, 2])
        self.scatter_row = s.sb("scatter_row", [P, REGIONS], I32)
        self.gather_row = s.sb("gather_row", [P, REGIONS], I32)
        self.extra_blocks = s.sb("extra_blocks", [1, EXTRA + 1], I32)


class Weights:

    def __init__(self, s, io, layer):
        self.w_in = [s.sb(f"w_in{b}", [P, KT, 2 * FF]) for b in range(2)]
        self.w_out = [s.sb(f"w_out{b}", [P, FF // P, D]) for b in range(2)]
        self.w_in_in = [s.sem(f"w_in_in{b}") for b in range(2)]
        self.w_out_in = [s.sem(f"w_out_in{b}") for b in range(2)]
        self.all_in = io["moe_w_in"][layer].rearrange("e (k p) f -> p e k f", p=P)
        self.all_out = io["moe_w_out"][layer].rearrange("e (k p) f -> p e k f", p=P)

    def load_in(self, engine, n, b):
        engine.dma_start(self.w_in[b][:], self.all_in[:, ds(n, 1), :, :].rearrange("p e k f -> p (e k) f")
                         ).then_inc(self.w_in_in[b], 16)

    def load_out(self, engine, n, b):
        engine.dma_start(self.w_out[b][:], self.all_out[:, ds(n, 1), :, :].rearrange("p e k f -> p (e k) f")
                         ).then_inc(self.w_out_in[b], 16)

    def load_first(self, engine):
        self.load_in(engine, 0, 0)
        self.load_out(engine, 0, 0)
        self.load_in(engine, 1, 1)


class ExpertBuffers:
    def __init__(self, s, weights):
        self.w_in, self.w_out = weights.w_in, weights.w_out
        self.x = [s.sb(f"x{b}", [P, D]) for b in range(2)]
        self.x_t = s.sb("x_t", [P, KT, P])
        self.silu = s.sb("silu", [P, FF])
        self.act = s.sb("act", [P, FF])
        self.act_t = s.sb("act_t", [P, FF // P, P])
        self.out = [s.sb(f"out{b}", [P, D]) for b in range(2)]
        self.gather_row = [s.sb(f"gather_row{b}", [P, 1], I32) for b in range(2)]
        self.scatter_row = [s.sb(f"scatter_row{b}", [P, 1], I32) for b in range(2)]
        self.psum = s.psum()
        self.gate_p = self.psum[:, 0, :]
        self.value_p = self.psum[:, 1, :]
        self.x_p = self.psum[:, 2:4, :].rearrange("p a (k t) -> p (a k) t", t=P)
        self.act_p = self.psum[:, 4, :].rearrange("p (k t) -> p k t", t=P)
        self.out_p = self.psum[:, 6:8, :].rearrange("p a e -> p (a e)")

    def turn_x(self, t, c, b):
        for k in range(KT):
            mm = t.transpose(self.x_p[:, k, :], self.x[b][:, k * P:(k + 1) * P], c.ident[:])
        return mm

    def up(self, t, b):
        for a in range(2):
            for k in range(KT):
                mm = t.matmul(self.psum[:, a, :], self.x_t[:, k, :], self.w_in[b][:, k, a * FF:(a + 1) * FF],
                              start=(k == 0), stop=(k == KT - 1))
        return mm

    def turn_act(self, t, c):
        for k in range(FF // P):
            mm = t.transpose(self.act_p[:, k, :], self.act[:, k * P:(k + 1) * P], c.ident[:])
        return mm

    def down(self, t, b):
        for a in range(2):
            for k in range(FF // P):
                mm = t.matmul(self.psum[:, 6 + a, :], self.act_t[:, k, :], self.w_out[b][:, k, a * HALF:(a + 1) * HALF],
                              start=(k == 0), stop=(k == FF // P - 1))
        return mm


def gather(g, d, e, b, bound):
    return g.indirect_dma_start(out=e.x[b][:], out_offset=None, in_=d.rows,
                                in_offset=bass.IndirectOffsetOnAxis(ap=e.gather_row[b][:], axis=0),
                                bounds_check=bound, oob_is_err=False)


def scatter(g, d, e, b, bound):
    return g.indirect_dma_start(out=d.expert_rows, in_=e.out[b][:], in_offset=None,
                                out_offset=bass.IndirectOffsetOnAxis(ap=e.scatter_row[b][:], axis=0),
                                bounds_check=bound, oob_is_err=False)


class Turn:

    def __init__(self, at, trip=None):
        self.trip, self.at, self.b = trip, at, at % 2
        self.n = at if trip is None else trip * 2 + at

    def has(self, first, last):
        return self.trip is not None or first <= self.at <= last

    def uses(self, ahead):
        k = (self.at + ahead) // 2 + 1
        return 16 * k if self.trip is None else self.trip * 16 + 16 * k


HEAD_TURNS = 3
TAIL_TURNS = 4


def all_turns(engine, turn):
    for n in range(HEAD_TURNS):
        turn(Turn(n))
    steady = EXPERTS + 1 - HEAD_TURNS - TAIL_TURNS
    with engine.Fori(0, steady // 2) as trip:
        for j in range(2):
            turn(Turn(HEAD_TURNS + j, trip))
    for n in range(HEAD_TURNS + steady, EXPERTS + 1):
        turn(Turn(n))


def experts(nc, c, d, r, weights, layer, name):
    with Stage(nc, name) as s:
        e = ExpertBuffers(s, weights)
        w_in_in, w_out_in = weights.w_in_in, weights.w_out_in
        gathered = [d.pool_dma[layer][f"gathered{b}"] for b in range(2)]
        scattered = [d.pool_dma[layer][f"scattered{b}"] for b in range(2)]
        cleared, first_x, first_x_t, rows_set = (s.sem(x) for x in ("cleared", "first_x", "first_x_t", "rows_set"))
        pe = s.progress("pe", ["up", "turn_x", "down", "turn_act"], credit=2)
        dve = s.progress("dve", ["act", "x_t", "out"], credit=2)
        act = s.progress("act", ["silu", "out", "act_t"], credit=2)
        pool = s.progress("pool", ["gather_row", "scatter_row"], credit=2)
        block = s.block()
        last = EXPERTS - 1

        @block.sync
        def _(sp):
            def turn(t):
                if t.has(0, last - 2):
                    sp.wait_ge(pe.sem, pe.after("up", t.n))
                    sp.wait_ge(cleared, 2)
                    weights.load_in(sp, t.n + 2, t.b)
                if t.has(0, last - 1):
                    sp.wait_ge(pe.sem, pe.after("down", t.n))
                    sp.wait_ge(cleared, 2)
                    weights.load_out(sp, t.n + 1, 1 - t.b)

            all_turns(sp, turn)

        @block.gpsimd
        def _(g):
            last_token, last_assignment = g.to_reg(T - 1), g.to_reg(2 * T - 1)
            for b in range(2):
                g.memset(e.x[b][:], 0.0).then_inc(cleared, 1)
            g.wait_ge(cleared, 2)
            pool.open(g)
            for b in range(2):
                g.tensor_copy(e.gather_row[b][:], r.gather_row[:, b:b + 1]).then_inc(cleared, 1)
                g.wait_ge(cleared, 3 + b)
                gather(g, d, e, b, last_token).then_inc(gathered[b], 16)

            def turn(t):
                b = t.b
                if t.has(0, last - 2):
                    if t.trip is None and t.n == 0:
                        g.wait_ge(first_x, 1)
                    else:
                        g.wait_ge(pe.sem, pe.after("turn_x", t.n - 1))
                    g.wait_ge(gathered[b], t.uses(0))
                    g.wait_ge(cleared, 2)
                    g.tensor_copy(e.gather_row[b][:], r.gather_row[:, ds(t.n + 2, 1)]).then_inc(pool.sem, pool.count())
                    g.wait_ge(pool.sem, pool.after("gather_row", t.n))
                    g.sem_inc(rows_set, 1)
                    gather(g, d, e, b, last_token).then_inc(gathered[b], 16)
                else:
                    pool.skip()
                if t.has(1, last + 1):
                    g.wait_ge(dve.sem, dve.after("out", t.n))
                    g.wait_ge(act.sem, act.after("out", t.n))
                    if t.has(3, last + 1):
                        g.wait_ge(scattered[1 - b], t.uses(-3))
                    g.wait_ge(cleared, 2)
                    g.tensor_copy(e.scatter_row[1 - b][:], r.scatter_row[:, ds(t.n - 1, 1)]).then_inc(pool.sem, pool.count())
                    g.wait_ge(pool.sem, pool.after("scatter_row", t.n))
                    g.sem_inc(rows_set, 1)
                    scatter(g, d, e, 1 - b, last_assignment).then_inc(scattered[1 - b], 16)
                else:
                    pool.skip()

            all_turns(g, turn)
            for b in range(2):
                g.wait_ge(scattered[b], 16 * (EXPERTS // 2))

        @block.tensor
        def _(t_):
            pe.open(t_)
            t_.wait_ge(gathered[0], 16)
            e.turn_x(t_, c, 0).then_inc(first_x, 1)
            t_.wait_ge(first_x_t, 1)

            def turn(t):
                b = t.b
                if t.has(0, last):
                    t_.wait_ge(w_in_in[b], t.uses(0))
                    t_.wait_ge(dve.sem, dve.after("x_t", t.n - 1))
                    e.up(t_, b).then_inc(pe.sem, pe.count())
                else:
                    pe.skip()
                if t.has(0, last - 1):
                    t_.wait_ge(gathered[1 - b], t.uses(1))
                    e.turn_x(t_, c, 1 - b).then_inc(pe.sem, pe.count())
                else:
                    pe.skip()
                if t.has(1, last + 1):
                    t_.wait_ge(w_out_in[1 - b], t.uses(-1))
                    t_.wait_ge(act.sem, act.after("act_t", t.n - 1))
                    if t.has(2, last + 1):
                        t_.wait_ge(dve.sem, dve.after("out", t.n - 1))
                        t_.wait_ge(act.sem, act.after("out", t.n - 1))
                    e.down(t_, 1 - b).then_inc(pe.sem, pe.count())
                else:
                    pe.skip()
                if t.has(0, last):
                    t_.wait_ge(dve.sem, dve.after("act", t.n))
                    e.turn_act(t_, c).then_inc(pe.sem, pe.count())
                else:
                    pe.skip()

            all_turns(t_, turn)

        @block.vector
        def _(v):
            dve.open(v)
            gain = spread(c.gain(1, layer), 2, P)
            v.wait_ge(first_x, 1)
            v.tensor_tensor(e.x_t[:], e.x_p, gain, ALU.mult).then_inc(first_x_t, 1)

            def turn(t):
                if t.has(0, last):
                    v.wait_ge(act.sem, act.after("silu", t.n))
                    v.wait_ge(pe.sem, pe.after("turn_act", t.n - 1))
                    v.tensor_mul(e.act[:], e.silu[:], e.value_p).then_inc(dve.sem, dve.count())
                else:
                    dve.skip()
                if t.has(0, last - 1):
                    v.wait_ge(pe.sem, pe.after("turn_x", t.n))
                    v.tensor_tensor(e.x_t[:], e.x_p, gain, ALU.mult).then_inc(dve.sem, dve.count())
                else:
                    dve.skip()
                if t.has(1, last + 1):
                    v.wait_ge(pe.sem, pe.after("down", t.n))
                    if t.has(3, last + 1):
                        v.wait_ge(scattered[1 - t.b], t.uses(-3))
                    v.tensor_copy(e.out[1 - t.b][:, HALF:D], e.out_p[:, HALF:D]).then_inc(dve.sem, dve.count())
                else:
                    dve.skip()

            all_turns(v, turn)

        @block.scalar
        def _(a):
            act.open(a)

            def turn(t):
                if t.has(0, last):
                    a.wait_ge(pe.sem, pe.after("up", t.n))
                    a.wait_ge(dve.sem, dve.after("act", t.n - 1))
                    a.activation(e.silu[:], e.gate_p, ACT.Silu).then_inc(act.sem, act.count())
                else:
                    act.skip()
                if t.has(1, last + 1):
                    a.wait_ge(pe.sem, pe.after("down", t.n))
                    if t.has(3, last + 1):
                        a.wait_ge(scattered[1 - t.b], t.uses(-3))
                    a.activation(e.out[1 - t.b][:, 0:HALF], e.out_p[:, 0:HALF], ACT.Copy).then_inc(act.sem, act.count())
                else:
                    act.skip()
                if t.has(0, last):
                    a.wait_ge(pe.sem, pe.after("turn_act", t.n))
                    a.activation(e.act_t[:], e.act_p, ACT.Copy).then_inc(act.sem, act.count())
                else:
                    act.skip()

            all_turns(a, turn)


def extra_experts(nc, io, c, d, r, weights, layer, name):
    with Stage(nc, name) as s:
        e = ExpertBuffers(s, weights)
        w_in_in, w_out_in = s.sem("w_in_in"), s.sem("w_out_in")
        x_in, scattered = d.pool_dma[layer]["extra_gathered"], d.pool_dma[layer]["extra_scattered"]
        cleared, rows_set = s.sem("cleared"), s.sem("rows_set")
        pe = s.progress("pe", ["turn_x", "up", "turn_act", "down"])
        dve = s.progress("dve", ["x_t", "act"])
        act = s.progress("act", ["silu", "act_t", "out"])
        pool = s.progress("pool", ["gather_row", "scatter_row"])
        block = s.block()

        def for_each(engine, body):
            n_blocks = engine.value_load(r.extra_blocks[0:1, EXTRA:EXTRA + 1], min_val=0, max_val=EXTRA)
            with engine.If(n_blocks > 0):
                with engine.Fori(0, EXTRA) as i:
                    with engine.If(i < n_blocks):
                        body(i)
                    with engine.Else():
                        engine.nop()
            with engine.Else():
                engine.nop()

        @block.scalar
        def _(a):
            act.open(a)

            def body(i):
                expert = a.value_load(r.extra_blocks[0:1, ds(i, 1)], min_val=0, max_val=EXPERTS - 1)
                a.wait_ge(pe.sem, pe.after("down", i - 1))
                a.wait_ge(cleared, 1)
                a.dma_start(e.w_in[0][:], io["moe_w_in"][layer].rearrange("e (k p) f -> p e k f", p=P)
                            [:, ds(expert, 1), :, :].rearrange("p e k f -> p (e k) f")).then_inc(w_in_in, 16)
                a.dma_start(e.w_out[0][:], io["moe_w_out"][layer].rearrange("e (k p) f -> p e k f", p=P)
                            [:, ds(expert, 1), :, :].rearrange("p e k f -> p (e k) f")).then_inc(w_out_in, 16)
                a.wait_ge(pe.sem, pe.after("up", i))
                a.activation(e.silu[:], e.gate_p, ACT.Silu).then_inc(act.sem, 1)
                a.wait_ge(pe.sem, pe.after("turn_act", i))
                a.activation(e.act_t[:], e.act_p, ACT.Copy).then_inc(act.sem, 1)
                a.wait_ge(pe.sem, pe.after("down", i))
                a.wait_ge(pool.sem, pool.after("scatter_row", i - 1))
                a.activation(e.out[0][:], e.out_p, ACT.Copy).then_inc(act.sem, 1)

            for_each(a, body)

        @block.gpsimd
        def _(g):
            last_token, last_assignment = g.to_reg(T - 1), g.to_reg(2 * T - 1)
            g.memset(e.x[0][:], 0.0).then_inc(cleared, 1)
            g.wait_ge(cleared, 1)
            pool.open(g)

            def body(i):
                g.wait_ge(pe.sem, pe.after("turn_x", i - 1))
                g.wait_ge(cleared, 1)
                g.tensor_copy(e.gather_row[0][:], r.gather_row[:, ds(i + EXPERTS, 1)]).then_inc(pool.sem, 1)
                g.wait_ge(pool.sem, pool.after("gather_row", i))
                g.sem_inc(rows_set, 1)
                gather(g, d, e, 0, last_token).then_inc(x_in, 16)
                g.wait_ge(act.sem, act.after("out", i))
                g.wait_ge(cleared, 1)
                g.tensor_copy(e.scatter_row[0][:], r.scatter_row[:, ds(i + EXPERTS, 1)]).then_inc(cleared, 1)
                g.wait_ge(cleared, i + 2)
                g.sem_inc(rows_set, 1)
                scatter(g, d, e, 0, last_assignment).then_inc(scattered, 16)
                g.wait_ge(scattered, i * 16 + 16)
                g.sem_inc(pool.sem, 1)

            for_each(g, body)

        @block.tensor
        def _(t):
            pe.open(t)

            def body(i):
                t.wait_ge(x_in, i * 16 + 16)
                e.turn_x(t, c, 0).then_inc(pe.sem, 1)
                t.wait_ge(dve.sem, dve.after("x_t", i))
                t.wait_ge(w_in_in, i * 16 + 16)
                e.up(t, 0).then_inc(pe.sem, 1)
                t.wait_ge(dve.sem, dve.after("act", i))
                e.turn_act(t, c).then_inc(pe.sem, 1)
                t.wait_ge(act.sem, act.after("act_t", i))
                t.wait_ge(w_out_in, i * 16 + 16)
                t.wait_ge(act.sem, act.after("out", i - 1))
                e.down(t, 0).then_inc(pe.sem, 1)

            for_each(t, body)

        @block.vector
        def _(v):
            dve.open(v)

            def body(i):
                v.wait_ge(pe.sem, pe.after("turn_x", i))
                v.tensor_tensor(e.x_t[:], e.x_p, spread(c.gain(1, layer), 2, P), ALU.mult).then_inc(dve.sem, 1)
                v.wait_ge(act.sem, act.after("silu", i))
                v.tensor_mul(e.act[:], e.silu[:], e.value_p).then_inc(dve.sem, 1)

            for_each(v, body)


def combine(nc, c, d, r, name, h, out=None):
    with Stage(nc, name) as s:
        rows = [s.sb(f"rows{b}", [P, 2, D]) for b in range(4)]
        rows_in = [s.sem(f"rows_in{b}") for b in range(4)]
        stored = s.sem("stored")
        dve = s.progress("dve", ["first", "second"])
        block = s.block()
        by_token = d.expert_rows.rearrange("(t a) e -> t a e", a=2)

        @block.sync
        def _(sp):
            for tile in range(TT):
                if tile >= 4:
                    sp.wait_ge(dve.sem, dve.after("second", tile - 4))
                sp.dma_start(rows[tile % 4][:], by_token[tile * P:(tile + 1) * P, :, :]).then_inc(rows_in[tile % 4], 16)

        @block.vector
        def _(v):
            dve.open(v)
            for tile in range(TT):
                v.wait_ge(rows_in[tile % 4], tile // 4 * 16 + 16)
                for choice, step in enumerate(("first", "second")):
                    v.scalar_tensor_tensor(out=h[:, tile, :], in0=rows[tile % 4][:, choice, :], in1=h[:, tile, :],
                                           scalar=r.gates[:, tile, choice:choice + 1],
                                           op0=ALU.mult, op1=ALU.add).then_inc(dve.sem, 1)
                    if choice == 0:
                        v.wait_ge(dve.sem, dve.after("first", tile))

        if out is not None:
            @block.scalar
            def _(a):
                for tile in range(TT):
                    a.wait_ge(dve.sem, dve.after("second", tile))
                    a.dma_start(out[tile * P:(tile + 1) * P, :], h[:, tile, :]).then_inc(stored, 16)
                a.wait_ge(stored, 16 * TT)


def mixture(nc, io, c, d, layer, h, u, out=None):
    name = f"moe{layer}"
    with Stage(nc, name) as s:
        r = Routing(s)
        weights = Weights(s, io, layer)
        norm(nc, c, f"{name}_norm", h, c.gain(1, layer), u, 0, rows_out=d.rows)
        route(nc, io, c, d, r, weights, layer, f"{name}_route", u)
        experts(nc, c, d, r, weights, layer, f"{name}_first")
        extra_experts(nc, io, c, d, r, weights, layer, f"{name}_extra")
        combine(nc, c, d, r, f"{name}_sum", h, out)


def hgrn_project(nc, io, c, d, u):
    with Stage(nc, "hproj") as s:
        ring = [s.sb(f"ring{b}", [P, KT, 2 * P]) for b in range(2)]
        wide = [s.sb(f"wide{b}", [P, KT, HALF]) for b in range(NH)]
        out = [s.sb(f"out{b}", [P, T]) for b in range(2)]
        key = [s.sb(f"key{b}", [P, T]) for b in range(2)]
        psum = s.psum()
        ring_in = [s.sem(f"ring_in{b}") for b in range(2)]
        wide_in = [s.sem(f"wide_in{b}") for b in range(NH)]
        stored = [s.sem(f"stored{b}") for b in range(2)]
        keys_out = [s.sem(f"keys_out{b}") for b in range(2)]
        rows_out = [s.sem(f"rows_out{b}") for b in range(2)]
        n_tiles = (2 * HG_FD + D) // P
        first_gate = 2 * HG_FD // P
        tiles_pe = s.progress("tiles_pe", ["tile"], credit=2)
        tiles_act = s.progress("tiles_act", ["out"], credit=2)
        sig_act, key_act, key_dve = s.sem("sig_act"), s.sem("key_act"), s.sem("key_dve")
        rows_pe, rows_dve = s.sem("rows_pe"), s.sem("rows_dve")
        block = s.block()
        w = io["hg_in"][0].rearrange("(k p) e -> p k e", p=P)
        columns = [HG_FD, HG_FD + 2 * P, 0, 2 * P] + [2 * HG_FD + D + i * 2 * P for i in range(D // (2 * P))]

        @block.sync
        def _(sp):
            for n, at in enumerate(columns):
                if n >= 2:
                    sp.wait_ge(tiles_pe.sem, tiles_pe.after("tile", 2 * (n - 2) + 1))
                sp.dma_start(ring[n % 2][:], w[:, :, at:at + 2 * P]).then_inc(ring_in[n % 2], 16)
                if n == 1:
                    for a in range(NH):
                        at = 2 * HG_FD + a * HALF
                        sp.dma_start(wide[a][:], w[:, :, at:at + HALF]).then_inc(wide_in[a], 16)

        def rows_buf(i):
            return key[i % 2][:]

        def pair(b):
            return psum[:, 2 * b:2 * b + 2, :].rearrange("p a t -> p (a t)")

        @block.tensor
        def _(t):
            tiles_pe.open(t)

            def four(first, trip):
                for n in range(4):
                    tile = first + n if trip is None else trip * 4 + first + n
                    if n % 2 == 0:
                        uses = first // 4 if trip is None else trip + first // 4
                        t.wait_ge(ring_in[n // 2], uses * 16 + 16)
                    t.wait_ge(tiles_act.sem, tiles_act.after("out", tile - 2))
                    for half in range(NH):
                        for k in range(KT):
                            mm = t.matmul(psum[:, 2 * (n % 2) + half, :], ring[n // 2][:, k, (n % 2) * P:(n % 2 + 1) * P],
                                          u[:, k, half * HALF:(half + 1) * HALF], start=(k == 0), stop=(k == KT - 1))
                    mm.then_inc(tiles_pe.sem, 1)

            four(0, None)
            four(4, None)
            with t.Fori(0, (n_tiles - first_gate) // 4) as trip:
                four(first_gate, trip)
            for i in range(TT):
                if i >= 2:
                    t.wait_ge(rows_dve, i - 1)
                for a in range(NH):
                    if i == 0:
                        t.wait_ge(wide_in[a], 16)
                    for k in range(KT):
                        mm = t.matmul(psum[:, 4 + 2 * (i % 2) + a, :], u[:, k, i * P:(i + 1) * P], wide[a][:, k, :],
                                      start=(k == 0), stop=(k == KT - 1))
                mm.then_inc(rows_pe, 1)

        @block.scalar
        def _(a):
            tiles_act.open(a)
            for tile in range(HG_PAIRS):
                b = tile % 2
                a.wait_ge(tiles_pe.sem, tiles_pe.after("tile", tile))
                if tile >= 2:
                    a.wait_ge(keys_out[b], 16 * (tile // 2))
                    a.wait_ge(stored[b], 16 * (tile // 2))
                a.activation(key[b][:], pair(b), ACT.Sigmoid, scale=-1.0).then_inc(key_act, 1)
                a.activation(out[b][:], pair(b), ACT.Sigmoid).then_inc(sig_act, 1)
                a.wait_ge(sig_act, tile + 1)
                a.activation(out[b][:], out[b][:], ACT.Ln, scale=c.one_less_lb[:, tile:tile + 1],
                             bias=c.lb[:, tile:tile + 1]).then_inc(tiles_act.sem, 1)
                a.wait_ge(tiles_act.sem, tiles_act.after("out", tile))
                a.dma_start(d.cm["decay"][tile * P:(tile + 1) * P, :], out[b][:]).then_inc(stored[b], 16)
                a.wait_ge(key_dve, tile + 1)
                a.dma_start(d.cm["k"][tile * P:(tile + 1) * P, :], key[b][:]).then_inc(keys_out[b], 16)
            for tile in range(HG_PAIRS):
                b = tile % 2
                a.wait_ge(tiles_pe.sem, tiles_pe.after("tile", tile + HG_PAIRS))
                a.wait_ge(stored[b], 16 * (tile // 2 + 2))
                a.activation(out[b][:], pair(b), ACT.Silu).then_inc(tiles_act.sem, 1)
                a.wait_ge(tiles_act.sem, tiles_act.after("out", tile + HG_PAIRS))
                a.dma_start(d.cm["r"][tile * P:(tile + 1) * P, :], out[b][:]).then_inc(stored[b], 16)
            with a.Fori(0, KT // 2) as trip:
                for b in range(2):
                    tile = trip * 2 + b
                    a.wait_ge(tiles_pe.sem, tiles_pe.after("tile", tile + first_gate))
                    a.wait_ge(stored[b], trip * 16 + 16 * HG_PAIRS)
                    a.activation(out[b][:], pair(b), ACT.Silu).then_inc(tiles_act.sem, 1)
                    a.wait_ge(tiles_act.sem, tiles_act.after("out", tile + first_gate))
                    a.dma_start(d.cm["gate"][ds(tile * P, P), :], out[b][:]).then_inc(stored[b], 16)
            for i in range(TT):
                a.wait_ge(rows_dve, i + 1)
                a.dma_start(d.v_rows[i * P:(i + 1) * P, :], rows_buf(i)).then_inc(rows_out[i % 2], 16)
            for b in range(2):
                a.wait_ge(stored[b], 16 * (HG_PAIRS + KT // 2))
                a.wait_ge(keys_out[b], 16 * (HG_PAIRS // 2))
                a.wait_ge(rows_out[b], 16 * (TT // 2))

        @block.vector
        def _(v):
            for tile in range(HG_PAIRS):
                v.wait_ge(key_act, tile + 1)
                v.tensor_scalar(key[tile % 2][:], key[tile % 2][:], c.one_less_lb[:, tile:tile + 1], None,
                                ALU.mult).then_inc(key_dve, 1)
            for b in range(2):
                v.wait_ge(keys_out[b], 16 * (HG_PAIRS // 2))
            for i in range(TT):
                v.wait_ge(rows_pe, i + 1)
                if i >= 2:
                    v.wait_ge(rows_out[i % 2], 16 * (i // 2))
                v.tensor_copy(rows_buf(i), pair(2 + i % 2)).then_inc(rows_dve, 1)


def hgrn_scan(nc, c, d, o):
    with Stage(nc, "hscan") as s:
        SPAN = 2 * CHUNK
        SPANS = T // SPAN
        fresh = {n: s.sb(n, [P, SPANS, HG_PAIRS, SPAN]) for n in ("decay", "r", "k")}
        up = fresh["decay"]
        down = s.sb("down", [P, SPANS, HG_PAIRS, SPAN])
        total = s.sb("total", [P, SPANS, HG_PAIRS, SPAN])
        late = s.sb("late", [P, CHUNKS, HG_PAIRS])
        e_mid = s.sb("e_mid", [P, CHUNKS, HG_PAIRS])
        e_end = s.sb("e_end", [P, CHUNKS, HG_PAIRS])
        e_late = s.sb("e_late", [P, CHUNKS, HG_PAIRS])
        q_bd = [s.sb(f"q_bd{b}", [P, HG_PAIRS, P]) for b in range(4)]
        k_bd = [s.sb(f"k_bd{b}", [P, HG_PAIRS, P]) for b in range(2)]
        k_rows = [s.sb(f"k_rows{b}", [P, HG_PAIRS, P]) for b in range(2)]
        values = [s.sb(f"values{b}", [P, HG_PAIRS, P]) for b in range(2)]
        att_t = [s.sb(f"att_t{b}", [P, HG_PAIRS, P]) for b in range(2)]
        state = s.sb("state", [P, HG_PAIRS, P])
        state_mid = [s.sb(f"state_mid{b}", [P, HG_PAIRS, P]) for b in range(2)]
        kept = s.sb("kept", [P, HG_PAIRS, P])
        grown = s.sb("grown", [P, HG_PAIRS, P])
        psum = s.psum()

        def bank(n):
            return psum[:, n, :].rearrange("p (m e) -> p m e", e=P)

        def of_span(buf, span):
            return buf[:, ds(span, 1), :, :].rearrange("p g m t -> p (g m) t")

        def of_chunk(factors, chunk):
            return spread(factors[:, ds(chunk, 1), :].rearrange("p n m -> p (n m)"), 2, P)

        arrived = [s.sem(f"arrived{n}") for n in range(3)]
        ready, zeroed, between = s.sem("ready"), s.sem("zeroed"), s.sem("between")
        v_in = [s.sem(f"v_in{b}") for b in range(2)]
        v_span = s.progress("v_span", ["total", "offset", "clamp", "late"])
        a_span = s.progress("a_span", ["down", "up", "mid", "end", "late"])
        prep = s.progress("prep", ["q_bd", "k_bd"], credit=2)
        ahead_pe = s.progress("ahead_pe", ["att", "k_rows"], credit=2)
        ahead_dve = s.progress("ahead_dve", ["att"], credit=2)
        ahead_act = s.progress("ahead_act", ["k_rows"], credit=2)
        pe = s.progress("pe", ["S", "o"], credit=4)
        act = s.progress("act", ["o"], credit=2)
        dve = s.progress("dve", ["grown", "S", "mid"], credit=2)
        pool = s.progress("pool", ["kept"], credit=2)
        block = s.block()
        last_quad = CHUNKS // 4 - 1

        def all_quads(engine, chunk_part):
            with engine.Fori(0, last_quad) as quad:
                for i in range(4):
                    chunk_part(quad * 4 + i, i, quad)
            for i in range(4):
                chunk_part(last_quad * 4 + i, i, None)

        def has(ahead, i, quad):
            return quad is not None or i + ahead < 4

        @block.sync
        def _(sp):
            def load_span(span, sem):
                for n in fresh:
                    sp.dma_start(of_span(fresh[n], span), d.cm[n].rearrange("(m p) t -> p m t", p=P)
                                 [:, 0:HG_PAIRS, span * SPAN:(span + 1) * SPAN]).then_inc(sem, 16)

            def load_values(chunk, b):
                for h in range(2):
                    sp.dma_start(values[b][h * CHUNK:(h + 1) * CHUNK, :, :],
                                 d.v_rows.rearrange("t (m h e) -> t m h e", h=2, e=P)
                                 [ds(chunk * CHUNK, CHUNK), :, h, :]).then_inc(v_in[b], 16)

            load_span(0, arrived[0])
            for b in range(2):
                load_values(b, b)
            for span in range(1, SPANS):
                load_span(span, arrived[min(span, 2)])
            with sp.Fori(0, CHUNKS // 2 - 1) as trip:
                for b in range(2):
                    sp.wait_ge(pe.sem, pe.after("o", trip * 2 + b))
                    sp.wait_ge(ready, 1)
                    load_values(trip * 2 + 2 + b, b)

        @block.gpsimd
        def _(g):
            for z in (*q_bd, *k_bd, state, state_mid[0]):
                g.memset(z[:], 0.0).then_inc(zeroed, 1)
            g.wait_ge(zeroed, 8)
            g.sem_inc(ready, 1)
            pool.open(g)

            def chunk_part(chunk, i, quad):
                g.wait_ge(dve.sem, dve.after("S", chunk - 1))
                g.sem_inc(between, 1)
                if i % 2 == 0:
                    g.wait_ge(a_span.sem, a_span.after("end", (quad * 2 if quad is not None else last_quad * 2) + i // 2))
                    g.sem_inc(between, 1)
                g.tensor_tensor(kept[:], state[:], of_chunk(e_end, chunk), ALU.mult).then_inc(pool.sem, 1)

            all_quads(g, chunk_part)

        @block.vector
        def _(v):
            v.wait_ge(ready, 1)
            v_span.open(v)
            prep.open(v)
            ahead_dve.open(v)
            dve.open(v)

            def decays(span, sem, count):
                v.wait_ge(arrived[sem], count)
                sum_ = of_span(total, span)
                offset = of_span(up, span)
                v.tensor_tensor_scan(sum_.rearrange("p m t -> p (m t)"), c.chunk_start[:, 0:HG_PAIRS * SPAN],
                                     of_span(fresh["decay"], span).rearrange("p m t -> p (m t)"), 0.0,
                                     ALU.mult, ALU.add).then_inc(v_span.sem, 1)
                v.wait_ge(v_span.sem, v_span.after("total", span))
                parts = sum_.rearrange("p m (c t) -> p (m c) t", c=2)
                v.tensor_tensor(offset.rearrange("p m (c t) -> p (m c) t", c=2), parts,
                                spread(parts[:, :, CHUNK // 2 - 1], 2, CHUNK), ALU.subtract).then_inc(v_span.sem, 1)
                v.wait_ge(v_span.sem, v_span.after("offset", span))
                v.tensor_scalar(offset, offset, -MAX_EXP, MAX_EXP, ALU.max, ALU.min).then_inc(v_span.sem, 1)
                ends = sum_.rearrange("p m (c t) -> p c m t", c=2)
                v.tensor_sub(late[:, ds(span * 2, 2), :], ends[:, :, :, CHUNK - 1],
                             ends[:, :, :, CHUNK // 2 - 1]).then_inc(v_span.sem, 1)

            def diagonals(chunk, i, span):
                at = slice(i % 2 * CHUNK, (i % 2 + 1) * CHUNK)
                if i % 2 == 0:
                    v.wait_ge(a_span.sem, a_span.after("up", span))
                v.wait_ge(pe.sem, pe.after("o", chunk - 4))
                for h in range(2):
                    rows = slice(h * HEAD, (h + 1) * HEAD)
                    mul = v.tensor_mul(q_bd[i][rows, :, rows], of_span(fresh["r"], span)[rows, :, at],
                                       of_span(down, span)[rows, :, at])
                mul.then_inc(prep.sem, 1)
                v.wait_ge(ahead_pe.sem, ahead_pe.after("k_rows", chunk - 2))
                for h in range(2):
                    rows = slice(h * HEAD, (h + 1) * HEAD)
                    mul = v.tensor_mul(k_bd[i % 2][rows, :, rows], of_span(fresh["k"], span)[rows, :, at],
                                       of_span(up, span)[rows, :, at])
                mul.then_inc(prep.sem, 1)

            def causal(chunk, b):
                v.wait_ge(ahead_pe.sem, ahead_pe.after("att", chunk))
                v.wait_ge(pe.sem, pe.after("o", chunk - 2))
                v.tensor_tensor(att_t[b][:], bank(b), spread(c.up_incl_bd[:], 1, HG_PAIRS),
                                ALU.mult).then_inc(ahead_dve.sem, 1)

            def chunk_part(chunk, i, quad):
                b = i % 2
                q2 = last_quad * 2 if quad is None else quad * 2
                if has(1, i, quad):
                    causal(chunk + 1, 1 - b)
                v.wait_ge(pe.sem, pe.after("S", chunk))
                v.tensor_tensor(grown[:], bank(6 + b), of_chunk(e_late, chunk), ALU.mult).then_inc(dve.sem, 1)
                v.wait_ge(dve.sem, dve.after("grown", chunk))
                v.wait_ge(pool.sem, pool.after("kept", chunk))
                v.tensor_add(state[:], kept[:], grown[:]).then_inc(dve.sem, 1)
                if has(1, i, quad):
                    v.wait_ge(dve.sem, dve.after("S", chunk))
                    v.wait_ge(pe.sem, pe.after("o", chunk - 1))
                    v.tensor_tensor(state_mid[1 - b][:], state[:], of_chunk(e_mid, chunk + 1), ALU.mult).then_inc(dve.sem, 1)
                if has(2, i, quad):
                    diagonals(chunk + 2, (i + 2) % 4, q2 + (i + 2) // 2)
                if quad is not None and b == 0:
                    decays(q2 + i // 2 + 2, 2, 48 * (SPANS - 2))

            decays(0, 0, 48)
            diagonals(0, 0, 0)
            diagonals(1, 1, 0)
            decays(1, 1, 48)
            causal(0, 0)
            v.wait_ge(a_span.sem, a_span.after("late", 1))
            all_quads(v, chunk_part)

        @block.scalar
        def _(a):
            a_span.open(a)
            ahead_act.open(a)
            act.open(a)

            def decays(span):
                a.wait_ge(v_span.sem, v_span.after("late", span))
                a.activation(of_span(down, span), of_span(up, span), ACT.Exp).then_inc(a_span.sem, 1)
                a.activation(of_span(up, span), of_span(up, span), ACT.Exp, scale=-1.0).then_inc(a_span.sem, 1)
                ends = of_span(total, span).rearrange("p m (c t) -> p c m t", c=2)
                pair = ds(span * 2, 2)
                a.activation(e_mid[:, pair, :], ends[:, :, :, CHUNK // 2 - 1], ACT.Exp).then_inc(a_span.sem, 1)
                a.activation(e_end[:, pair, :], ends[:, :, :, CHUNK - 1], ACT.Exp).then_inc(a_span.sem, 1)
                a.activation(e_late[:, pair, :], late[:, pair, :], ACT.Exp).then_inc(a_span.sem, 1)

            def rows(chunk, b):
                a.wait_ge(ahead_pe.sem, ahead_pe.after("k_rows", chunk))
                a.wait_ge(pe.sem, pe.after("S", chunk - 2))
                a.activation(k_rows[b][:], bank(2 + b), ACT.Copy).then_inc(ahead_act.sem, 1)

            def chunk_part(chunk, i, quad):
                if has(1, i, quad):
                    rows(chunk + 1, 1 - i % 2)
                a.wait_ge(pe.sem, pe.after("o", chunk))
                a.activation(o[:, :, ds(chunk * CHUNK, CHUNK)],
                             psum[:, 4 + i % 2, :].rearrange("p (h t) -> p h t", t=CHUNK), ACT.Copy).then_inc(act.sem, 1)
                if quad is not None and i % 2 == 0:
                    decays(quad * 2 + i // 2 + 2)

            decays(0)
            rows(0, 0)
            decays(1)
            all_quads(a, chunk_part)

        @block.tensor
        def _(t):
            t.wait_ge(ready, 1)
            ahead_pe.open(t)
            pe.open(t)

            def ahead(chunk, i):
                b = i % 2
                t.wait_ge(prep.sem, prep.after("k_bd", chunk))
                t.wait_ge(ahead_dve.sem, ahead_dve.after("att", chunk - 2))
                for m in range(HG_PAIRS):
                    mm = t.matmul(bank(b)[:, m, :], k_bd[b][:, m, :], q_bd[i][:, m, :], start=True, stop=True)
                mm.then_inc(ahead_pe.sem, 1)
                t.wait_ge(ahead_act.sem, ahead_act.after("k_rows", chunk - 2))
                for m in range(HG_PAIRS):
                    mm = t.transpose(bank(2 + b)[:, m, :], k_bd[b][:, m, :], c.ident[:])
                mm.then_inc(ahead_pe.sem, 1)

            def chunk_part(chunk, i, quad):
                b = i % 2
                if has(1, i, quad):
                    ahead(chunk + 1, (i + 1) % 4)
                uses = (last_quad * 2 if quad is None else quad * 2) + i // 2 + 1
                t.wait_ge(v_in[b], uses * 32)
                t.wait_ge(ahead_act.sem, ahead_act.after("k_rows", chunk))
                t.wait_ge(dve.sem, dve.after("grown", chunk - 2))
                for m in range(HG_PAIRS):
                    mm = t.matmul(bank(6 + b)[:, m, :], k_rows[b][:, m, :], values[b][:, m, :], start=True, stop=True)
                mm.then_inc(pe.sem, 1)
                t.wait_ge(ahead_dve.sem, ahead_dve.after("att", chunk))
                t.wait_ge(act.sem, act.after("o", chunk - 2))
                t.wait_ge(dve.sem, dve.after("mid", chunk - 1))
                for m in range(HG_PAIRS):
                    t.matmul(bank(4 + b)[:, m, :], values[b][:, m, :], att_t[b][:, m, :], start=True, stop=False)
                    mm = t.matmul(bank(4 + b)[:, m, :], state_mid[b][:, m, :], q_bd[i][:, m, :], start=False, stop=True)
                mm.then_inc(pe.sem, 1)

            ahead(0, 0)
            all_quads(t, chunk_part)


def hgrn_output(nc, io, c, d, o, weights):
    with Stage(nc, "hnorm") as s:
        gate = [s.sb(f"gate{b}", [P, T]) for b in range(2)]
        squares = [s.sb(f"squares{b}", [P, T]) for b in range(2)]
        inv = [s.sb(f"inv{b}", [P, T]) for b in range(2)]
        psum = s.psum()
        loaded = [s.sem(f"loaded{b}") for b in range(2)]
        opened = s.sem("opened")
        pe = s.progress("pe", ["squares"], credit=2)
        dve = s.progress("dve", ["mean", "unit"], credit=2)
        act1 = s.progress("act1", ["square"], credit=2)
        act2 = s.progress("act2", ["ln", "inverse"], credit=2)
        pool = s.progress("pool", ["gate"], credit=2)
        block = s.block()

        @block.sync
        def _(sp):
            with sp.Fori(0, HG_HEADS // 2) as trip:
                for b in range(2):
                    tile = trip * 2 + b
                    sp.wait_ge(pool.sem, pool.after("gate", tile - 2))
                    sp.wait_ge(opened, 1)
                    sp.dma_start(gate[b][:], d.cm["gate"][ds(tile * P, P), :]).then_inc(loaded[b], 16)

        @block.tensor
        def _(t):
            pe.open(t)
            with t.Fori(0, HG_HEADS // 2) as trip:
                for b in range(2):
                    tile = trip * 2 + b
                    t.wait_ge(act1.sem, act1.after("square", tile))
                    t.wait_ge(dve.sem, dve.after("mean", tile - 2))
                    for half in range(NH):
                        mm = t.matmul(psum[:, 2 * b + half, :], c.ones[:], squares[b][:, half * HALF:(half + 1) * HALF],
                                      start=True, stop=True)
                    mm.then_inc(pe.sem, 1)

        @block.scalar
        def _(a):
            a.preload_act_table_set("natural_log_exp_and_others")
            weights.load(a)
            act1.open(a)
            act2.open(a)

            def square(tile, b):
                a.wait_ge(pe.sem, pe.after("squares", tile - 2))
                a.activation(squares[b][:], o[:, tile, :], ACT.Square).then_inc(act1.sem, 1)

            def invert(tile, b):
                a.wait_ge(dve.sem, dve.after("mean", tile))
                a.activation(inv[b][:], inv[b][:], ACT.Ln).then_inc(act2.sem, 1)
                a.wait_ge(act2.sem, act2.after("ln", tile))
                a.activation(inv[b][:], inv[b][:], ACT.Exp, scale=-0.5).then_inc(act2.sem, 1)

            staggered(a, square, late=invert)

        @block.vector
        def _(v):
            v.sem_inc(opened, 1)
            dve.open(v)
            with v.Fori(0, HG_HEADS // 2) as trip:
                for b in range(2):
                    tile = trip * 2 + b
                    v.wait_ge(pe.sem, pe.after("squares", tile))
                    v.tensor_scalar(inv[b][:], psum[:, 2 * b:2 * b + 2, :].rearrange("p a t -> p (a t)"),
                                    1.0 / P, RMS_EPS, ALU.mult, ALU.add).then_inc(dve.sem, 1)
                    v.wait_ge(act2.sem, act2.after("inverse", tile))
                    v.scalar_tensor_tensor(out=o[:, tile, :], in0=o[:, tile, :], scalar=c.hg_norm(), in1=inv[b][:],
                                           op0=ALU.mult, op1=ALU.mult).then_inc(dve.sem, 1)

        @block.gpsimd
        def _(g):
            pool.open(g)
            with g.Fori(0, HG_HEADS // 2) as trip:
                for b in range(2):
                    tile = trip * 2 + b
                    g.wait_ge(loaded[b], trip * 16 + 16)
                    g.wait_ge(dve.sem, dve.after("unit", tile))
                    g.wait_ge(opened, 1)
                    g.tensor_mul(o[:, tile, :], o[:, tile, :], gate[b][:]).then_inc(pool.sem, 1)


def build(nc, io, out):
    Stage.used.clear()
    c = Constants(nc)
    d = Scratch(nc)
    x = io["x"].rearrange("b t d -> (b t) d")
    setup(nc, io, c)
    with Stage(nc, "rwkv_in") as s:
        u = s.sb("u", [P, KT, 1 + T])
        with Stage(nc, "first") as s2:
            norm(nc, c, "rwkv_norm", s2.sb("h", [P, TT, D]), c.gain(0, 0), u, 1, source=x)
        rwkv_project(nc, io, c, u, d)
    with Stage(nc, "trunk") as s:
        mixed = s.sb("mixed", [P, KT, T])
        rwkv_scan(nc, c, d, mixed)
        h = s.sb("h", [P, TT, D])
        with Stage(nc, "rwkv_end") as s2:
            weights = OutWeights(s2, io["rw_out"][0])
            rwkv_output(nc, io, c, d, mixed, weights)
            project_out(nc, "rwkv_out", weights, mixed, h, source=x)
        mixture(nc, io, c, d, 0, h, mixed)
        clear_semaphores(nc)
        norm(nc, c, "hgrn_norm", h, c.gain(0, 1), mixed, 0)
        hgrn_project(nc, io, c, d, mixed)
        hgrn_scan(nc, c, d, mixed)
        with Stage(nc, "hgrn_end") as s2:
            weights = OutWeights(s2, io["hg_out"][0])
            hgrn_output(nc, io, c, d, mixed, weights)
            project_out(nc, "hgrn_out", weights, mixed, h)
        clear_semaphores(nc)
        mixture(nc, io, c, d, 1, h, mixed, out.rearrange("b t d -> (b t) d"))


_NAMES = ["x", "norm1_g", "norm2_g", "rw_mu", "rw_in", "rw_w0", "rw_w1", "rw_w2", "rw_a0", "rw_a1", "rw_a2",
          "rw_g1", "rw_g2", "rw_kk", "rw_ka", "rw_rk", "rw_ln_w", "rw_ln_b", "rw_out", "hg_lower", "hg_in",
          "hg_norm", "hg_out", "moe_rg", "moe_rg_b", "moe_re", "moe_re_b", "moe_w_in", "moe_w_out"]


def kernel(**inputs):
    import numpy as np
    import concourse.bacc as bacc
    from concourse.bass_utils import run_bass_kernel_spmd

    nc = bacc.Bacc("TRN2", target_bir_lowering=False, num_devices=1)
    arrays, io = {}, {}
    for name in _NAMES:
        a = np.ascontiguousarray(inputs[name])
        arrays[f"in_{name}"] = a
        io[name] = nc.dram_tensor(f"in_{name}", a.shape, mybir.dt.from_np(a.dtype), kind="ExternalInput").ap()
    out = nc.dram_tensor("out", (1, T, D), F32, kind="ExternalOutput").ap()
    build(nc, io, out)
    r = run_bass_kernel_spmd(nc, [arrays], core_ids=[0])
    return r.results[0]["out"]
```
